# Optimizing a Trainium2 kernel written in Bass

```python
import math
import jax, jax.numpy as jnp
from jax import lax
import numpy as np

D_MODEL = 1024
BATCH = 1
SEQ = 256
DEPTH = 1
DEC_BATCH = 8
DEC_SEQ = 1
PAST_LEN = 2048
PAGE_SIZE = 128

D_CONV = D_MODEL
CONV_W = 3
N_RET_HEADS = 4
RET_DK = D_MODEL // N_RET_HEADS
RET_DV = 2 * RET_DK
RET_QK = N_RET_HEADS * RET_DK
RET_VDIM = N_RET_HEADS * RET_DV
RET_CHUNK = 128
ROPE_BASE = 10000.0
N_EXPERTS = 32
TOP_K = 4
D_FF = D_MODEL
SWIGLU_ALPHA = 1.702
SWIGLU_LIMIT = 7.0
EXPERT_BLOCK = 128
NORM_EPS = 1e-5
SPLIT_WIDTHS = (D_CONV, D_CONV, D_CONV, RET_QK, RET_QK, RET_VDIM, RET_VDIM, D_MODEL, D_MODEL)
N_IN_COLS = sum(SPLIT_WIDTHS)

kernel_name = "hybrid_conv_retention_moe_step"

def rmsnorm(x, g):
    x32 = x.astype(jnp.float32)
    y = x32 * lax.rsqrt(jnp.mean(x32 * x32, axis=-1, keepdims=True) + NORM_EPS)
    return (y * g.astype(jnp.float32)).astype(x.dtype)

def rotary(x, pos):
    half = x.shape[-1] // 2
    inv = ROPE_BASE ** (-jnp.linspace(0.0, 1.0, half, dtype=jnp.float32))
    ang = pos.astype(jnp.float32)[:, None] * inv[None, :]
    cos = jnp.cos(ang)[None, :, None, :]
    sin = jnp.sin(ang)[None, :, None, :]
    x32 = x.astype(jnp.float32)
    x1, x2 = x32[..., :half], x32[..., half:]
    return jnp.concatenate([x1 * cos - x2 * sin, x1 * sin + x2 * cos], axis=-1)

def retention_chunkwise(q, k, v, s0):
    B, L, H, DK = q.shape
    DV = v.shape[-1]
    C = math.gcd(L, RET_CHUNK)
    n = L // C
    log_g = jnp.log1p(-jnp.exp2(-5.0 - jnp.arange(H, dtype=jnp.float32)))
    pos = jnp.arange(C, dtype=jnp.float32)
    diff = pos[:, None] - pos[None, :]
    decay_mask = jnp.where(diff >= 0, jnp.exp(jnp.maximum(diff, 0.0)[None] * log_g[:, None, None]), 0.0)
    q_decay = jnp.exp((pos + 1.0)[None, :] * log_g[:, None])[..., None]
    k_decay = jnp.exp((C - 1.0 - pos)[None, :] * log_g[:, None])[..., None]
    chunk_decay = jnp.exp(C * log_g)[:, None, None]

    def to_chunks(t):
        return t.reshape(B, n, C, H, t.shape[-1]).transpose(1, 0, 3, 2, 4)

    qc, kc, vc = to_chunks(q), to_chunks(k), to_chunks(v.astype(jnp.float32))

    def step(S, inp):
        qb, kb, vb = inp
        scores = jnp.einsum('bhqd,bhkd->bhqk', qb, kb) * decay_mask
        intra = jnp.einsum('bhqk,bhkv->bhqv', scores, vb)
        cross = jnp.einsum('bhqd,bhdv->bhqv', qb * q_decay, S)
        S_new = chunk_decay * S + jnp.einsum('bhkd,bhkv->bhdv', kb * k_decay, vb)
        return S_new, intra + cross

    s_final, out = lax.scan(step, s0.astype(jnp.float32), (qc, kc, vc))
    out = out.transpose(1, 0, 3, 2, 4).reshape(B, L, H, DV)
    return out, s_final.astype(s0.dtype)

def short_conv(u, buf, w):
    L = u.shape[1]
    full = jnp.concatenate([buf.astype(u.dtype), u], axis=1)
    y = w[0] * full[:, 0:L]
    for i in range(1, CONV_W):
        y = y + w[i] * full[:, i:i + L]
    return y, full[:, -(CONV_W - 1):]

def mixer(xn, pos, conv_buf, ret_state, w_in, conv_w, w_a, w_b, w_o):
    B, L, _ = xn.shape
    proj = jnp.einsum('bld,dc->blc', xn, w_in)
    idx = [int(i) for i in np.cumsum(SPLIT_WIDTHS)[:-1]]
    cb, cc, ch, q, k, v, g, ga, gb = jnp.split(proj, idx, axis=-1)
    conv_out, conv_new = short_conv(cc * ch, conv_buf, conv_w)
    o_a = jnp.einsum('blc,cd->bld', cb * conv_out, w_a)
    qh = rotary(q.reshape(B, L, N_RET_HEADS, RET_DK), pos)
    kh = rotary(k.reshape(B, L, N_RET_HEADS, RET_DK), pos) * (RET_DK ** -0.5)
    vh = v.reshape(B, L, N_RET_HEADS, RET_DV)
    r, ret_new = retention_chunkwise(qh, kh, vh, ret_state)
    r = r * lax.rsqrt(jnp.mean(r * r, axis=-1, keepdims=True) + NORM_EPS)
    r = (jax.nn.silu(g.astype(jnp.float32)) * r.reshape(B, L, RET_VDIM)).astype(xn.dtype)
    o_b = jnp.einsum('blv,vd->bld', r, w_b)
    merged = jax.nn.sigmoid(ga) * o_a + jax.nn.sigmoid(gb) * o_b
    return jnp.einsum('bld,de->ble', merged, w_o), conv_new, ret_new

def expert_ffn(xb, w1, b1, w2, b2):
    h = xb @ w1 + b1
    gate, up = h[:, :D_FF], h[:, D_FF:]
    gate = jnp.minimum(gate, SWIGLU_LIMIT)
    up = jnp.clip(up, -SWIGLU_LIMIT, SWIGLU_LIMIT)
    glu = gate * jax.nn.sigmoid(SWIGLU_ALPHA * gate)
    return ((up + 1.0) * glu) @ w2 + b2

def moe_ffn(x, w_router, b_router, w_e1, b_e1, w_e2, b_e2):
    shp = x.shape
    xt = x.reshape(-1, D_MODEL)
    T = xt.shape[0]
    logits = xt.astype(jnp.float32) @ w_router.astype(jnp.float32) + b_router.astype(jnp.float32)
    top_vals, top_idx = lax.top_k(logits, TOP_K)
    gates = jax.nn.softmax(top_vals, axis=-1)
    TK = T * TOP_K
    flat_e = top_idx.reshape(TK)
    order = jnp.argsort(flat_e, stable=True)
    sorted_e = flat_e[order]
    counts = jnp.zeros((N_EXPERTS,), jnp.int32).at[flat_e].add(1)
    padded = (counts + EXPERT_BLOCK - 1) // EXPERT_BLOCK * EXPERT_BLOCK
    pad_end = jnp.cumsum(padded)
    pad_start = pad_end - padded
    start = jnp.cumsum(counts) - counts
    dest = pad_start[sorted_e] + jnp.arange(TK, dtype=jnp.int32) - start[sorted_e]
    n_blocks = -(-TK // EXPERT_BLOCK) + N_EXPERTS
    rows = n_blocks * EXPERT_BLOCK
    token_of = (order // TOP_K).astype(jnp.int32)
    row_token = jnp.zeros((rows,), jnp.int32).at[dest].set(token_of)
    block_expert = jnp.minimum(
        jnp.searchsorted(pad_end, jnp.arange(n_blocks, dtype=jnp.int32) * EXPERT_BLOCK, side='right'),
        N_EXPERTS - 1).astype(jnp.int32)
    xb = xt[row_token].reshape(n_blocks, EXPERT_BLOCK, D_MODEL)

    def run_block(args):
        blk, e = args
        return expert_ffn(blk, w_e1[e], b_e1[e], w_e2[e], b_e2[e])

    yb = lax.map(run_block, (xb, block_expert)).reshape(rows, D_MODEL)
    y_assign = yb[dest] * gates.reshape(TK)[order][:, None].astype(x.dtype)
    y = jnp.zeros((T, D_MODEL), x.dtype).at[token_of].add(y_assign.astype(x.dtype))
    return y.reshape(shp)

def layer(x, pos, conv_buf, ret_state, norm1, w_in, conv_w, w_a, w_b, w_o,
          norm2, w_router, b_router, w_e1, b_e1, w_e2, b_e2):
    m, conv_new, ret_new = mixer(rmsnorm(x, norm1), pos, conv_buf, ret_state, w_in, conv_w, w_a, w_b, w_o)
    h = x + m
    h = h + moe_ffn(rmsnorm(h, norm2), w_router, b_router, w_e1, b_e1, w_e2, b_e2)
    return h, conv_new, ret_new

def setup_inputs(seed: int = 0) -> dict:
    key = jax.random.key(seed)
    ks = jax.random.split(key, 20)
    f32 = jnp.float32
    nrm = lambda k, s, sc: jax.random.normal(k, s, f32) * sc
    return {
        "x_prompt": nrm(ks[0], (BATCH, SEQ, D_MODEL), 1.0),
        "x_sample": nrm(ks[1], (DEC_BATCH, DEC_SEQ, D_MODEL), 1.0),
        "state_conv": nrm(ks[2], (DEPTH, DEC_BATCH, CONV_W - 1, D_CONV), 0.5),
        "state_ret": nrm(ks[3], (DEPTH, DEC_BATCH, N_RET_HEADS, RET_DK, RET_DV), 0.1),
        "norm1": 1.0 + nrm(ks[4], (DEPTH, D_MODEL), 0.02),
        "w_in": nrm(ks[5], (DEPTH, D_MODEL, N_IN_COLS), D_MODEL ** -0.5),
        "conv_w": nrm(ks[6], (DEPTH, CONV_W, D_CONV), CONV_W ** -0.5),
        "w_a": nrm(ks[7], (DEPTH, D_CONV, D_MODEL), D_CONV ** -0.5),
        "w_b": nrm(ks[8], (DEPTH, RET_VDIM, D_MODEL), RET_VDIM ** -0.5),
        "w_o": nrm(ks[9], (DEPTH, D_MODEL, D_MODEL), D_MODEL ** -0.5),
        "norm2": 1.0 + nrm(ks[10], (DEPTH, D_MODEL), 0.02),
        "w_router": nrm(ks[11], (DEPTH, D_MODEL, N_EXPERTS), D_MODEL ** -0.5),
        "b_router": nrm(ks[12], (DEPTH, N_EXPERTS), 0.01),
        "w_e1": nrm(ks[13], (DEPTH, N_EXPERTS, D_MODEL, 2 * D_FF), D_MODEL ** -0.5),
        "b_e1": nrm(ks[14], (DEPTH, N_EXPERTS, 2 * D_FF), 0.02),
        "w_e2": nrm(ks[15], (DEPTH, N_EXPERTS, D_FF, D_MODEL), D_FF ** -0.5),
        "b_e2": nrm(ks[16], (DEPTH, N_EXPERTS, D_MODEL), 0.02),
        "norm_f": 1.0 + nrm(ks[17], (D_MODEL,), 0.02),
    }

def reference(x_prompt, x_sample, state_conv, state_ret, norm1, w_in, conv_w, w_a, w_b, w_o,
              norm2, w_router, b_router, w_e1, b_e1, w_e2, b_e2, norm_f):
    B, L = x_prompt.shape[0], x_prompt.shape[1]
    pos_p = jnp.arange(L, dtype=jnp.int32)
    pos_s = PAST_LEN + jnp.arange(x_sample.shape[1], dtype=jnp.int32)
    h_p, h_s = x_prompt, x_sample
    conv_p_l, ret_p_l, conv_s_l, ret_s_l = [], [], [], []
    for l in range(DEPTH):
        conv0 = jnp.zeros((B, CONV_W - 1, D_CONV), x_prompt.dtype)
        ret0 = jnp.zeros((B, N_RET_HEADS, RET_DK, RET_DV), state_ret.dtype)
        h_p, cp, rp = layer(h_p, pos_p, conv0, ret0, norm1[l], w_in[l], conv_w[l], w_a[l], w_b[l], w_o[l],
                            norm2[l], w_router[l], b_router[l], w_e1[l], b_e1[l], w_e2[l], b_e2[l])
        h_s, cs, rs = layer(h_s, pos_s, state_conv[l], state_ret[l], norm1[l], w_in[l], conv_w[l], w_a[l],
                            w_b[l], w_o[l], norm2[l], w_router[l], b_router[l], w_e1[l], b_e1[l], w_e2[l], b_e2[l])
        conv_p_l.append(cp); ret_p_l.append(rp); conv_s_l.append(cs); ret_s_l.append(rs)
    y_prompt = rmsnorm(h_p, norm_f)
    y_sample = rmsnorm(h_s, norm_f)
    conv_prompt = jnp.stack(conv_p_l)
    ret_prompt = jnp.stack(ret_p_l)
    conv_sample = jnp.stack(conv_s_l)
    ret_sample = jnp.stack(ret_s_l)
    return (y_prompt, y_sample, conv_prompt, ret_prompt, conv_sample, ret_sample)


_drawn_inputs = setup_inputs


def setup_inputs(seed=0):
    import zlib

    import numpy as np

    out = dict(_drawn_inputs(seed))
    spreads = {}
    factors = {'b_router': 2.813, 'b_e1': 5.501, 'b_e2': 6.277, 'norm_f': 2.87}
    for name, (base, spread) in spreads.items():
        noise = np.random.default_rng([zlib.crc32(name.encode()), seed]).standard_normal(out[name].shape)
        drawn = base * np.exp(spread * noise) if base else spread * noise
        out[name] = __import__('jax').numpy.asarray(drawn.astype(out[name].dtype))
    for name, factor in factors.items():
        out[name] = (out[name] * factor).astype(out[name].dtype)
    return out
```

```python
import concourse.bass as bass
from concourse import mybir
from contextlib import ExitStack
import numpy as np

F32 = mybir.dt.float32
I32 = mybir.dt.int32
ALU = mybir.AluOpType
ACT = mybir.ActivationFunctionType
AX = mybir.AxisListType

D = 1024
LP = 256
NS = 8
T = LP + NS
TT = 3
ROWS = (128, 128, NS)
KD = D // 128
H = 4
DK = D // H
DV = 2 * DK
NV = DV // 128
PAST = 2048
E = 32
TOP = 4
SLOTS = 64
PAIRS = E // 2
MAX_ROUNDS = -(-T // SLOTS)
ALPHA = 1.702
LIMIT = 7.0
EPS = 1e-5
PRIMED = 1
NOT_ROUTED = 4096.0

RING = 12
CH = 2048
MIXER_CHUNKS = 5 * RING
PAIR_CHUNKS = 2 * RING
COUNTED = PAIR_CHUNKS - 4

C_COS, C_SIN, C_COSK, C_SINK = 0, T, 2 * T, 3 * T
C_MASK = 4 * T
C_ID = C_MASK + H * LP
C_TRI = C_ID + 128
C_KDEC = C_TRI + 128
C_SLOT = C_KDEC + 2 * H
C_THR = C_SLOT + SLOTS
N_CONST = C_THR + MAX_ROUNDS

W_CB, W_CC, W_CH, W_Q, W_K, W_V, W_G, W_GA, W_GB = (0, 1024, 2048, 3072, 4096, 5120, 7168, 9216, 10240)

R_STATE, R_CONV, R_NORM, N_PAR = 0, 2 * NS, 2 * NS + 3, 2 * NS + 4


def gamma(h):
    return 1.0 - 2.0 ** (-5 - h)


def shape_constants():
    f = np.float32
    c = np.zeros((128, N_CONST), f)
    pos = np.concatenate([np.arange(LP), np.full(NS, PAST)]).astype(f)
    inv = f(10000.0) ** (-np.linspace(0.0, 1.0, 128, dtype=f))
    ang = (pos[None, :] * inv[:, None]).astype(f)
    c[:, C_COS:C_COS + T] = np.cos(ang)
    c[:, C_SIN:C_SIN + T] = np.sin(ang)
    c[:, C_COSK:C_COSK + T] = c[:, C_COS:C_COS + T] * f(DK ** -0.5)
    c[:, C_SINK:C_SINK + T] = c[:, C_SIN:C_SIN + T] * f(DK ** -0.5)
    p = np.arange(128)
    q = np.arange(LP)
    for h in range(H):
        d = q[None, :] - p[:, None]
        c[:, C_MASK + h * LP:C_MASK + (h + 1) * LP] = np.where(d >= 0, gamma(h) ** np.maximum(d, 0), 0.0)
        for t in range(2):
            c[:, C_KDEC + 2 * h + t] = gamma(h) ** (LP - 1 - (t * 128 + p)).astype(np.float64)
    c[:, C_ID:C_ID + 128] = np.eye(128)
    c[:, C_TRI:C_TRI + 128] = p[:, None] < p[None, :]
    c[:, C_SLOT:C_SLOT + SLOTS] = np.arange(SLOTS)
    c[:, C_THR:C_THR + MAX_ROUNDS] = np.arange(MAX_ROUNDS) * SLOTS
    return c


def bank_plan():
    count, plan = [0] * 8, {}

    def use(name, bank):
        count[bank] += 1
        plan[name] = (bank, count[bank])

    def proj(name, n=4):
        for j in range(n):
            use((name, j), j)

    use("par", 4)
    proj("xT0")
    proj("xT1")
    for h in range(H):
        if h % 2 == 0:
            proj(("q", h // 2))
            proj(("k", h // 2))
        proj(("v", h), 3)
        proj(("g", h))
        if h >= 1:
            use(("rs", h - 1), 5)
            use(("rsT", h - 1), 4)
        use(("kt", h), 4)
        use(("sc", h), 5)
        use(("out", h, 0), 6)
        use(("out", h, 1), 7)
        use(("st", h, 0), 6)
        use(("st", h, 1), 7)
        if h >= 1:
            use(("ss", h - 1), 5)
    proj(("cc", 0))
    use(("rs", H - 1), 5)
    use(("rsT", H - 1), 4)
    proj(("ch", 0))
    proj(("cb", 0))
    use(("ss", H - 1), 5)
    for n in ("cc", "ch", "cb"):
        proj((n, 1))
    use("ct0", 4)
    use("ct1", 5)
    for n in ("ga", "wa", "gb", "wb"):
        proj((n, 0))
        proj((n, 1))
    for t in range(TT):
        for n in range(2):
            use(("wo", t, n), 2 * t + n)
    for n in ("x2T0", "x2T1"):
        proj(n)
    use("logits", 4)
    use("rank", 5)
    use("count", 6)
    use("gT", 7)
    for t in range(TT):
        for n in range(2):
            use(("b2", t, n), 2 * (t % 2) + n)
    return plan, count


def build(nc, a, o):
    plan, uses = bank_plan()
    ctx = ExitStack()
    with ctx:
        def sb(name, shape, dt=F32):
            return ctx.enter_context(nc.sbuf_tensor(name, shape, dt))

        def sem(name):
            return ctx.enter_context(nc.semaphore(name))

        ring = sb("ring", [128, RING, CH])
        hx = sb("hx", [128, TT, D])
        cst = sb("cst", [128, N_CONST])
        par = sb("par", [128, KD, N_PAR])
        ones = sb("ones", [128, 128])
        stat = sb("stat", [128, 16])
        router = sb("router", [128, KD, E])
        router_b = sb("router_b", [128, E])
        rg = sb("rg", [128, 2, TT, E])
        rgc = sb("rgc", [128, 2, TT, 2])
        small = sb("small", [128, 12, E])
        rounds_i = sb("rounds_i", [128, 1], I32)
        arena = sb("arena", [128, 21700])

        def view(at, *dims):
            n = int(np.prod(dims))
            assert at + n <= 21700
            v = arena[:, at:at + n]
            if len(dims) == 2:
                v = v.rearrange("p (a b) -> p a b", a=dims[0])
            if len(dims) == 3:
                v = v.rearrange("p (a b c) -> p a b c", a=dims[0], b=dims[1])
            return v

        squares_out = view(8704, TT, D)
        xnT = view(0, KD, T)
        xsT = view(2112, KD, 32)
        rT = view(2368, H * NV, T)
        xn = view(2368, TT, D)
        prow = view(15100, 1024)
        sg = view(6592, 2, 4, T)
        qT = view(8704, 4, T)
        kT = view(9760, 4, T)
        rot = view(10816, 4, T)
        v_sb = view(11872, 2, DV)
        vs_sb = view(12896, 128)
        ktok = view(13024, 2, DK)
        sc = view(13536, 384)
        st = view(14000, 2, DV)
        sq = view(15100, NV, T)
        rinv = view(16160, T)
        qsm = view(16424, 2, 2, NS * 32)
        ks = view(17448, 2, 2 * NS)
        S = [view(17480 + 1024 * n, 2, DV) for n in range(3)]
        vb = [view(20552 + 512 * n, DV) for n in range(2)]
        cc = view(8704, 4, T)
        U = view(9760, 4, T + 2)
        cv = view(10824, 4, T)
        aT = view(11880, KD, T)
        ctok = view(17480, D)
        merged = view(6592, KD, T)
        gbs = view(8704, KD, T)
        xn2 = view(0, TT, D)
        xn2T = view(3072, KD, T)
        xgT = view(5184, KD, 128)
        P = view(6208, TT * 2, SLOTS)
        Pg = view(6592, TT * 2, SLOTS)
        pick = view(6976, 2, SLOTS)
        pgT = view(7104, T)
        gcl = view(7368, 2, 512)
        ucl = view(8392, 2, 512)
        sig = view(9416, 2, 512)
        acts = view(10440, 2, 512)
        actT = view(11464, 2, 512)
        ysb = view(12488, D)
        gT = view(13512, T)
        n2b = view(15100, D)
        nfb = view(16124, D)
        b2 = view(17148, D)
        b1 = view(18172, 2 * D)
        rs_t = sb("rs_t", [128, 128])

        psum = [ctx.enter_context(nc.psum_tensor(f"bank{n}", [128, 512], F32)) for n in range(8)]

        cos, sin = cst[:, C_COS:C_COS + T], cst[:, C_SIN:C_SIN + T]
        cosk, sink = cst[:, C_COSK:C_COSK + T], cst[:, C_SINK:C_SINK + T]
        ident = cst[:, C_ID:C_ID + 128]
        tri = cst[:, C_TRI:C_TRI + 128]
        slot_no = cst[:, C_SLOT:C_SLOT + SLOTS]

        def mask(h, n):
            return cst[:, C_MASK + h * LP:C_MASK + h * LP + n]

        v_dram = nc.dram_tensor("v_decode", (H, NS, DV), F32, kind="Internal").ap()

        chunk = [sem(f"chunk{n}") for n in range(RING)]
        chunk_used = sem("chunk_used")
        filled = [sem(f"filled{n}") for n in range(8)]
        emptied = [sem(f"emptied{n}") for n in range(8)]
        x_in, cst_in, prow_in, row0_out = sem("x_in"), sem("cst_in"), sem("prow_in"), sem("row0_out")
        const_set = sem("const_set")
        sumsq, mean1, root1, xn_ready = sem("sumsq"), sem("mean1"), sem("root1"), sem("xn_ready")
        xsT_ready = sem("xsT_ready")
        dve, act = sem("dve"), sem("act")
        qk_ready = sem("qk_ready")
        vs_out = [sem("vs_out0"), sem("vs_out1")]
        gate_sig, st_out = sem("gate_sig"), sem("st_out")
        qs_ready = sem("qs_ready")
        S_in = [sem(f"S_in{n}") for n in range(3)]
        S_out = [sem(f"S_out{n}") for n in range(3)]
        vb_in = [sem(f"vb_in{n}") for n in range(2)]
        S_scaled, S_new, S_read = sem("S_scaled"), sem("S_new"), sem("S_read")
        sq_ready = sem("sq_ready")
        rT_ready, ctok_out, merged_ready = sem("rT_ready"), sem("ctok_out"), sem("merged_ready")
        late_in = sem("late_in")
        b1_zero = sem("b1_zero")
        sumsq2, mean2, root2 = sem("sumsq2"), sem("mean2"), sem("root2")
        xn2_ready, neg_max, gate_exp = sem("xn2_ready"), sem("neg_max"), sem("gate_exp")
        selected, routed, rounds_ready, gT_ready = sem("selected"), sem("routed"), sem("rounds_ready"), sem("gT_ready")
        cols_ready, pick_ready, P_ready = sem("cols_ready"), sem("pick_ready"), sem("P_ready")
        gathered, xg_lo, xg_hi = sem("gathered"), sem("xg_lo"), sem("xg_hi")
        pg_turned, pgT_ready = sem("pg_turned"), sem("pgT_ready")
        up_done, g_clip, u_clip, sig_ready, ug_ready, act_ready = (sem("up_done"), sem("g_clip"), sem("u_clip"),
                                                                   sem("sig_ready"), sem("ug_ready"), sem("act_ready"))
        act_turned, actT_ready, down_done, y_ready = sem("act_turned"), sem("actT_ready"), sem("down_done"), sem("y_ready")
        combined, added, round_done = sem("combined"), sem("added"), sem("round_done")
        sumsq3, mean3, root3, y_scaled, y_out = sem("sumsq3"), sem("mean3"), sem("root3"), sem("y_scaled"), sem("y_out")

        block = ctx.enter_context(nc.Block())

        def fill(pe, name):
            bank, n = plan[name]
            if n > 1:
                pe.wait_ge(emptied[bank], n - 1)
            return psum[bank]

        def fills(ins, name):
            ins.then_inc(filled[plan[name][0]], 1)

        def read(eng, name):
            bank, n = plan[name]
            eng.wait_ge(filled[bank], n)
            return psum[bank]

        def empties(ins, name):
            ins.then_inc(emptied[plan[name][0]], 1)

        w_in = a["w_in"][0]

        def cols(w, c):
            return [w[512 * n:512 * (n + 1), c:c + 512].rearrange("(k p) n -> p k n", p=128) for n in range(2)]

        def mixer_chunks():
            def group(w, c, last):
                return [(x, last) for x in cols(w, c)]

            for g in range(2):
                yield from group(w_in, W_Q + 512 * g, (("q", g), 3))
                yield from group(w_in, W_K + 512 * g, (("k", g), 3))
                for h in (2 * g, 2 * g + 1):
                    yield from group(w_in, W_V + DV * h, (("v", h), 2))
                    yield from group(w_in, W_G + DV * h, (("g", h), 3))
            for g in range(2):
                for n, w in (("cc", W_CC), ("ch", W_CH), ("cb", W_CB)):
                    yield from group(w_in, w + 512 * g, ((n, g), 3))
            for n, w, c in (("ga", w_in, W_GA), ("wa", a["w_a"][0], 0), ("gb", w_in, W_GB)):
                for g in range(2):
                    yield from group(w, c + 512 * g, ((n, g), 3))
            for g in range(2):
                for half in range(2):
                    yield from group(a["w_b"][0][D * half:D * (half + 1), :], 512 * g, (("wb", g), 3))
            for g in range(2):
                yield from group(a["w_o"][0], 512 * g, ("wo", 2, g))

        w1_rows = a["w_e1"].rearrange("l e (k p) n -> (l e) k p n", p=128)
        w2_rows = a["w_e2"].rearrange("l e (k two p) n -> (l e) k p two n", p=128, two=2)

        @block.sync
        def _(sp):
            sp.dma_start(hx[:, 0:2, :], a["x_prompt"][0].rearrange("(t p) d -> p t d", p=128)).then_inc(x_in, 16)
            sp.dma_start(hx[0:NS, 2, :], a["x_sample"][:, 0, :]).then_inc(x_in, 16)
            sp.dma_start(cst[:, :], a["tables"]).then_inc(cst_in, 16)
            mixer = list(mixer_chunks())
            assert len(mixer) == MIXER_CHUNKS

            def slot_free(n):
                bank, use = plan[mixer[n][1]]
                sp.wait_ge(filled[bank], use)

            for n, (src, _) in enumerate(mixer):
                if n >= RING:
                    slot_free(n - RING)
                sp.dma_start(ring[:, n % RING, :].rearrange("p (k n) -> p k n", k=4), src).then_inc(chunk[n % RING], 16)

            def pair_order():
                return [(True, e, k) for e in range(2) for k in range(8)] + [(False, e, k) for e in range(2) for k in range(4)]

            def used(it, n):
                w1, e, k = pair_order()[n]
                if k == (7 if w1 else 3):
                    sp.wait_ge(up_done if w1 else down_done, 2 * it + (e + 1 + (PRIMED if w1 else 0)))
                else:
                    before = 7 * e + k if w1 else 14 + 3 * e + k
                    sp.wait_ge(chunk_used, COUNTED * it + (before + 1))

            def load_pair(it, pair, first=False):
                for n, (w1, e, k) in enumerate(pair_order()):
                    dst = ring[:, n % RING, :]
                    if w1:
                        src = w1_rows[bass.ds(2 * pair + e, 1), k].rearrange("e p n -> p (e n)")
                    else:
                        src = w2_rows[bass.ds(2 * pair + e, 1), k].rearrange("e p two n -> p (e two) n")
                        dst = dst.rearrange("p (two n) -> p two n", two=2)
                    if n >= RING:
                        used(it, n - RING)
                    elif first:
                        slot_free(MIXER_CHUNKS - RING + n)
                    else:
                        used(it - 1, n + RING)
                    sp.dma_start(dst, src).then_inc(chunk[n % RING], 16)

            load_pair(0, 0, first=True)
            with sp.Fori(1, PAIRS) as pair:
                load_pair(pair, pair)
            sp.wait_ge(rounds_ready, 1)
            rounds = sp.value_load(rounds_i[0:1, 0:1], min_val=1, max_val=MAX_ROUNDS)
            with sp.If(rounds > 1):
                with sp.Fori(1, rounds) as r:
                    with sp.Fori(0, PAIRS) as pair:
                        load_pair(r * PAIRS + pair, pair)
            for t in range(TT):
                sp.wait_ge(y_scaled, t + 1)
                dst = o["y_prompt"][0, 128 * t:128 * (t + 1), :] if t < 2 else o["y_sample"][:, 0, :]
                sp.dma_start(dst, hx[0:ROWS[t], t, :]).then_inc(y_out, 16)
            sp.wait_ge(y_out, 16 * TT)

        @block.gpsimd
        def _(pool):
            pool.memset(ones[:, :], 1.0).then_inc(const_set, 1)
            pool.memset(rg[:, 0, :, :], -NOT_ROUTED).then_inc(const_set, 1)
            pool.memset(rg[:, 1, :, :], 0.0).then_inc(const_set, 1)
            pool.memset(qsm[:, :, :, :], 0.0).then_inc(const_set, 1)
            pool.memset(xsT[:, :, :], 0.0).then_inc(const_set, 1)
            pool.memset(stat[:, :], 1.0).then_inc(const_set, 1)
            src = a["state_ret"][0]
            total = H * NS

            def load(n):
                h, b = divmod(n, NS)
                if n >= 3:
                    pool.wait_ge(S_out[n % 3], 16 * (n // 3))
                    was_h, was_b = divmod(n - 3, NS)
                    if was_b == NS - 1:
                        pool.wait_ge(filled[5], plan[("rs", was_h)][1])
                    else:
                        pool.wait_ge(S_read, (NS - 1) * was_h + was_b + 1)
                pool.dma_start(S[n % 3], src[b, h].rearrange("(k p) v -> p k v", p=128)).then_inc(S_in[n % 3], 16)

            def load_v(n):
                h, b = divmod(n, NS)
                if b == 0:
                    pool.wait_ge(vs_out[h % 2], 64 * (h // 2 + 1))
                if n >= 2:
                    pool.wait_ge(S_new, n - 1)
                pool.dma_start(vb[n % 2], v_dram[h, b:b + 1, :].to_broadcast([128, DV])).then_inc(vb_in[n % 2], 16)

            for n in range(3):
                load(n)
            for n in range(2):
                load_v(n)
            for n in range(total):
                h, b = divmod(n, NS)
                pool.wait_ge(S_new, n + 1)
                pool.dma_start(o["ret_sample"][0, b, h].rearrange("(k p) v -> p k v", p=128), S[n % 3])\
                    .then_inc(S_out[n % 3], 16)
                if n + 2 < total:
                    load_v(n + 2)
                if n + 3 < total:
                    load(n + 3)
            for n in range(3):
                pool.wait_ge(S_out[n], 16 * len(range(n, total, 3)))
            pool.wait_ge(rT_ready, H)
            pool.wait_ge(filled[5], plan[("ss", H - 1)][1])
            pool.wait_ge(ctok_out, 32)
            pool.memset(b1[:, :], 0.0).then_inc(b1_zero, 1)
            pool.wait_ge(b1_zero, 1)
            pool.dma_start(b1[0:E, :], a["b_e1"][0]).then_inc(late_in, 16)
            pool.dma_start(b2[0:E, :], a["b_e2"][0]).then_inc(late_in, 16)
            pool.dma_start(n2b[:, :], a["norm2"][0:1, :].to_broadcast([128, D])).then_inc(late_in, 16)
            pool.dma_start(nfb[:, :], a["norm_f"].rearrange("(o n) -> o n", o=1).to_broadcast([128, D])).then_inc(late_in, 16)

            pool.wait_ge(routed, 1)
            pool.wait_ge(rounds_ready, 1)
            rounds = pool.value_load(rounds_i[0:1, 0:1], min_val=1, max_val=MAX_ROUNDS)
            with pool.Fori(0, rounds) as r:
                with pool.Fori(0, PAIRS) as pair:
                    it = r * PAIRS + pair
                    e = 2 * pair
                    pool.wait_ge(P_ready, 2 * it + PRIMED)
                    pool.tensor_copy(rgc[:, :, :, :], rg[:, :, :, bass.ds(e, 2)]).then_inc(cols_ready, 1)
                    pool.wait_ge(up_done, 2 * it + PRIMED)
                    pool.tensor_copy(pick[:, :, :],
                                     cst[:, bass.ds(e + C_ID, 2)].rearrange("p (e o) -> p e o", o=1)
                                     .to_broadcast([128, 2, SLOTS])).then_inc(pick_ready, 1)
                pool.wait_ge(cols_ready, PAIRS * (r + 1))
                pool.tensor_tensor(rg[:, 0, :, :], rg[:, 0, :, :],
                                   cst[:, C_THR + 1:C_THR + 2].rearrange("p (a o) -> p a o", a=1).to_broadcast([128, TT, E]),
                                   ALU.subtract).then_inc(round_done, 1)
                pool.wait_ge(round_done, r + 1)

        @block.scalar
        def _(ac):
            ac.sem_inc(actT_ready, PRIMED)
            ac.dma_start(prow[R_STATE:R_STATE + 2 * NS, :], a["state_conv"][0].rearrange("b w d -> (b w) d")).then_inc(prow_in, 16)
            ac.dma_start(prow[R_CONV:R_CONV + 3, :], a["conv_w"][0]).then_inc(prow_in, 16)
            ac.dma_start(prow[R_NORM:R_NORM + 1, :], a["norm1"]).then_inc(prow_in, 16)
            ac.dma_start(router[:, :, :], a["w_router"][0].rearrange("(k p) e -> p k e", p=128)).then_inc(prow_in, 16)
            ac.dma_start(router_b[:, :], a["b_router"].to_broadcast([128, E])).then_inc(prow_in, 16)
            ac.dma_start(o["conv_sample"][0, :, 0, :], a["state_conv"][0, :, 1, :]).then_inc(row0_out, 16)
            ac.wait_ge(x_in, 32)
            ac.wait_ge(const_set, 6)
            for t, n in enumerate(ROWS):
                ac.activation(squares_out[0:n, t, :], hx[0:n, t, :], ACT.Square, accum_out=stat[0:n, t:t + 1]).then_inc(sumsq, 1)
            ac.wait_ge(mean1, 1)
            ac.activation(stat[:, 6:9], stat[:, 3:6], ACT.Sqrt).then_inc(root1, 1)

            ac.wait_ge(emptied[4], plan["par"][1])
            for k in range(1, KD, 2):
                name = (f"xT{k // 4}", k % 4)
                ins = ac.activation(xnT[:, k, :], read(ac, name)[:, 0:T], ACT.Copy, scale=par[:, k, R_NORM:R_NORM + 1])
                empties(ins, name)

            def norm_head(h):
                ac.wait_ge(emptied[4], plan[("rsT", h)][1])
                for g in range(2):
                    ac.wait_ge(emptied[6 + g], plan[("out", h, g)][1])
                if h >= 1:
                    ac.wait_ge(filled[5], plan[("ss", h - 1)][1])
                ac.activation(sq[:, :, :], rT[:, NV * h:NV * (h + 1), :], ACT.Square).then_inc(sq_ready, 1)
                bank = read(ac, ("ss", h))
                if h >= 1:
                    ac.wait_ge(rT_ready, h)
                ins = ac.activation(rinv[:, :], bank[:, 0:T], ACT.Sqrt, scale=1.0 / DV, bias=stat[:, 15:16])
                empties(ins, ("ss", h))

            def decode_scale(h):
                for b in range(NS):
                    n = NS * h + b
                    ac.wait_ge(S_in[n % 3], 16 * (n // 3 + 1))
                    ac.activation(S[n % 3], S[n % 3], ACT.Copy, scale=gamma(h)).then_inc(S_scaled, 1)

            for h in range(H):
                for t in range(2):
                    name = (("v", h), t)
                    bank = read(ac, name)
                    if t == 0 and h >= 1:
                        ac.wait_ge(filled[7], plan[("st", h - 1, 1)][1])
                    ins = ac.activation(v_sb[:, t, :], bank[:, :], ACT.Copy)
                    empties(ins, name)
                name = (("v", h), 2)
                bank = read(ac, name)
                if h >= 1:
                    ac.wait_ge(vs_out[(h - 1) % 2], 64 * ((h - 1) // 2 + 1))
                ins = ac.activation(vs_sb[:, :], bank[:, 0:128], ACT.Copy)
                empties(ins, name)
                ac.wait_ge(emptied[2], plan[name][1])
                for j in range(NV):
                    ac.dma_start(v_dram[h, :, 128 * j:128 * (j + 1)], vs_sb[32 * j:32 * j + NS, :]).then_inc(vs_out[h % 2], 16)
                for j in range(4):
                    bank = read(ac, (("g", h), j))
                    if j == 0 and h >= 2:
                        ac.wait_ge(rT_ready, h - 1)
                    ac.activation(sg[:, h % 2, j, :], bank[:, 0:T], ACT.Sigmoid).then_inc(gate_sig, 1)
                if h >= 1:
                    decode_scale(h - 1)
                bank = read(ac, ("kt", h))
                for t in range(2):
                    ins = ac.activation(ktok[:, t, :], bank[:, DK * t:DK * (t + 1)], ACT.Copy,
                                        scale=cst[:, C_KDEC + 2 * h + t:C_KDEC + 2 * h + t + 1])
                    if t == 1:
                        empties(ins, ("kt", h))
                for g in range(2):
                    bank = read(ac, ("out", h, g))
                    ins = ac.activation(rT[:, NV * h + 2 * g:NV * h + 2 * g + 2, 0:LP],
                                        bank[:, :].rearrange("p (a q) -> p a q", a=2), ACT.Copy)
                    empties(ins, ("out", h, g))
                for g in range(2):
                    bank = read(ac, ("st", h, g))
                    if g == 0 and h >= 1:
                        ac.wait_ge(st_out, 16 * h)
                    ins = ac.activation(st[:, g, :], bank[:, :], ACT.Copy)
                    empties(ins, ("st", h, g))
                ac.wait_ge(emptied[6], plan[("st", h, 0)][1])
                ac.wait_ge(emptied[7], plan[("st", h, 1)][1])
                ac.dma_start(o["ret_prompt"][0, 0, h].rearrange("(k p) v -> p k v", p=128), st[:, :, :]).then_inc(st_out, 16)
                if h >= 1:
                    norm_head(h - 1)
            for g in range(2):
                for j in range(4):
                    name = (("cc", g), j)
                    bank = read(ac, name)
                    if g == 1:
                        ac.wait_ge(emptied[j], plan[(("ch", 0), j)][1])
                    ins = ac.activation(cc[:, j, :], bank[:, 0:T], ACT.Copy)
                    empties(ins, name)
                if g == 0:
                    decode_scale(H - 1)
                    norm_head(H - 1)
            for g in range(2):
                bank = read(ac, f"ct{g}")
                if g == 0:
                    for n in range(3):
                        ac.wait_ge(S_out[n], 16 * len(range(n, H * NS, 3)))
                ins = ac.activation(ctok[0:NS + 2, 512 * g:512 * (g + 1)], bank[0:NS + 2, :], ACT.Copy)
                empties(ins, f"ct{g}")
            ac.wait_ge(emptied[4], plan["ct0"][1])
            ac.wait_ge(emptied[5], plan["ct1"][1])
            ac.dma_start(o["conv_prompt"][0, 0], ctok[0:2, :]).then_inc(ctok_out, 16)
            ac.dma_start(o["conv_sample"][0, :, 1, :], ctok[2:2 + NS, :]).then_inc(ctok_out, 16)
            for name, dst in (("ga", merged), ("gb", gbs)):
                for g in range(2):
                    for j in range(4):
                        use = ((name, g), j)
                        bank = read(ac, use)
                        if name == "ga" and g == 0 and j == 0:
                            ac.wait_ge(rT_ready, H)
                        if name == "gb" and g == 0 and j == 0:
                            ac.wait_ge(filled[3], plan[(("wa", 1), 3)][1])
                        ins = ac.activation(dst[:, 4 * g + j, :], bank[:, 0:T], ACT.Sigmoid)
                        empties(ins, use)
            for t, n in enumerate(ROWS):
                for c in range(2):
                    ac.wait_ge(emptied[2 * t + c], plan[("wo", t, c)][1])
                ac.activation(squares_out[0:n, t, :], hx[0:n, t, :], ACT.Square,
                              accum_out=stat[0:n, t:t + 1]).then_inc(sumsq2, 1)
            ac.wait_ge(mean2, 1)
            ac.activation(stat[:, 6:9], stat[:, 3:6], ACT.Sqrt).then_inc(root2, 1)
            for t, n in enumerate(ROWS):
                ac.wait_ge(neg_max, t + 1)
                ac.activation(small[0:n, 8 + t, :], small[0:n, t, :], ACT.Exp, bias=stat[0:n, 9 + t:10 + t]).then_inc(gate_exp, 1)

            ac.wait_ge(rounds_ready, 1)
            rounds = ac.value_load(rounds_i[0:1, 0:1], min_val=1, max_val=MAX_ROUNDS)
            with ac.Fori(0, rounds) as r:
                with ac.Fori(0, PAIRS) as pair:
                    it = r * PAIRS + pair
                    ac.wait_ge(gathered, 2 * it + 1)
                    ac.activation(xgT[:, 0:4, :], psum[6][:, :].rearrange("p (k s) -> p k s", k=4), ACT.Copy).then_inc(xg_lo, 1)
                    ac.wait_ge(pg_turned, it + (1 + PRIMED))
                    ac.activation(pgT[:, :], psum[5][:, 0:T], ACT.Copy).then_inc(pgT_ready, 1)
                    for e in range(2):
                        ac.wait_ge(g_clip, 2 * it + e + 1)
                        ac.activation(sig[:, e, :], gcl[:, e, :], ACT.Sigmoid, scale=ALPHA).then_inc(sig_ready, 1)
                    for e in range(2):
                        ac.wait_ge(act_turned, 2 * it + e + 1)
                        ac.activation(actT[:, e, :], psum[5][:, :], ACT.Copy).then_inc(actT_ready, 1)
            for t, n in enumerate(ROWS):
                if t == 0:
                    ac.wait_ge(added, 6 * PAIRS * rounds + PRIMED)
                ac.activation(squares_out[0:n, t, :], hx[0:n, t, :], ACT.Square,
                              accum_out=stat[0:n, t:t + 1]).then_inc(sumsq3, 1)
            ac.wait_ge(mean3, 1)
            ac.activation(stat[:, 6:9], stat[:, 3:6], ACT.Sqrt).then_inc(root3, 1)
            ac.wait_ge(row0_out, 16)
            ac.wait_ge(st_out, 16 * H)

        @block.vector
        def _(v):
            steps = [0]
            for primed in (P_ready, added, y_ready):
                v.sem_inc(primed, PRIMED)

            def own(ins):
                steps[0] += 1
                ins.then_inc(dve, 1)

            def settle():
                v.wait_ge(dve, steps[0])

            def mean_to(src, dst, out_sem):
                v.tensor_scalar(dst, src, 1.0 / D, EPS, ALU.mult, ALU.add).then_inc(out_sem, 1)

            empties(v.tensor_copy(par[:, :, :], read(v, "par")[:, 0:KD * N_PAR].rearrange("p (k n) -> p k n", k=KD)), "par")
            v.wait_ge(const_set, 6)
            own(v.memset(stat[:, 15:16], EPS))
            v.wait_ge(sumsq, 3)
            mean_to(stat[:, 0:3], stat[:, 3:6], mean1)
            v.wait_ge(root1, 1)
            own(v.reciprocal(stat[:, 9:12], stat[:, 6:9]))
            settle()
            for t, n in enumerate(ROWS):
                v.tensor_scalar(xn[0:n, t, :], hx[0:n, t, :], stat[0:n, 9 + t:10 + t], None, ALU.mult).then_inc(xn_ready, 1)
            v.wait_ge(emptied[4], plan["par"][1])
            for k in range(0, KD, 2):
                name = (f"xT{k // 4}", k % 4)
                ins = v.tensor_scalar(xnT[:, k, :], read(v, name)[:, 0:T], par[:, k, R_NORM:R_NORM + 1], None, ALU.mult)
                empties(ins, name)
            for j in range(4):
                v.wait_ge(emptied[j], plan[("xT1", j)][1])
            v.tensor_copy(xsT[:, :, 0:NS], xnT[:, :, LP:T]).then_inc(xsT_ready, 1)

            def rotate(name, dst, cs, sn):
                for n in range(2):
                    a0, a1 = ((name, 2 * n), (name, 2 * n + 1))
                    x1, x2 = read(v, a0)[:, 0:T], read(v, a1)[:, 0:T]
                    own(v.tensor_tensor(rot[:, 0, :], x1, cs, ALU.mult))
                    own(v.tensor_tensor(rot[:, 1, :], x2, sn, ALU.mult))
                    ins = v.tensor_tensor(rot[:, 2, :], x1, sn, ALU.mult)
                    empties(ins, a0)
                    ins = v.tensor_tensor(rot[:, 3, :], x2, cs, ALU.mult)
                    empties(ins, a1)
                    settle()
                    v.wait_ge(emptied[2 * n], plan[a0][1])
                    v.wait_ge(emptied[2 * n + 1], plan[a1][1])
                    v.tensor_tensor(dst[:, 2 * n, :], rot[:, 0, :], rot[:, 1, :], ALU.subtract).then_inc(qk_ready, 1)
                    v.tensor_tensor(dst[:, 2 * n + 1, :], rot[:, 2, :], rot[:, 3, :], ALU.add).then_inc(qk_ready, 1)
                    v.wait_ge(qk_ready, qk[0] + 2)
                    qk[0] += 2

            qk = [0]

            def decode(h):
                for b in range(NS):
                    n = NS * h + b
                    v.wait_ge(S_scaled, n + 1)
                    v.wait_ge(vb_in[n % 2], 16 * (n // 2 + 1))
                    own(v.scalar_tensor_tensor(S[n % 3][:, 0, :], vb[n % 2], ks[:, h % 2, b:b + 1],
                                               S[n % 3][:, 0, :], ALU.mult, ALU.add))
                    v.scalar_tensor_tensor(S[n % 3][:, 1, :], vb[n % 2], ks[:, h % 2, NS + b:NS + b + 1],
                                           S[n % 3][:, 1, :], ALU.mult, ALU.add).then_inc(S_new, 1)
                ins = v.tensor_copy(rs_t[:, :], read(v, ("rs", h))[:, 0:128])
                empties(ins, ("rs", h))
                bank = read(v, ("rsT", h))
                ins = v.tensor_copy(rT[:, NV * h:NV * (h + 1), LP:T],
                                    bank[:, 0:128].rearrange("p (j s) -> p j s", j=NV)[:, :, 0:NS])
                empties(ins, ("rsT", h))

            def finish_head(h):
                v.wait_ge(emptied[5], plan[("ss", h)][1])
                own(v.reciprocal(rinv[:, :], rinv[:, :]))
                settle()
                for j in range(NV):
                    own(v.tensor_tensor(sg[:, h % 2, j, :], sg[:, h % 2, j, :], rinv[:, :], ALU.mult))
                settle()
                for j in range(NV):
                    ins = v.tensor_tensor(rT[:, NV * h + j, :], rT[:, NV * h + j, :], sg[:, h % 2, j, :], ALU.mult)
                ins.then_inc(rT_ready, 1)

            for h in range(H):
                if h % 2 == 0:
                    if h:
                        v.wait_ge(filled[5], plan[("sc", h - 1)][1])
                        v.wait_ge(filled[4], plan[("kt", h - 1)][1])
                    rotate(("q", h // 2), qT, cos, sin)
                    rotate(("k", h // 2), kT, cosk, sink)
                if h >= 2:
                    v.wait_ge(filled[5], plan[("rs", h - 2)][1])
                hh = 2 * (h % 2)
                for half in range(2):
                    own(v.tensor_copy(qsm[:, h % 2, half, 0:33 * (NS - 1) + 1:33], qT[:, hh + half, LP:T]))
                    v.tensor_copy(ks[:, h % 2, NS * half:NS * (half + 1)], kT[:, hh + half, LP:T]).then_inc(qs_ready, 1)
                v.wait_ge(qs_ready, 2 * (h + 1))
                settle()
                for j in range(4):
                    name = (("g", h), j)
                    v.wait_ge(gate_sig, 4 * h + j + 1)
                    bank = psum[plan[name][0]]
                    ins = v.tensor_tensor(sg[:, h % 2, j, :], sg[:, h % 2, j, :], bank[:, 0:T], ALU.mult)
                    empties(ins, name)
                for j in range(4):
                    v.wait_ge(emptied[j], plan[(("g", h), j)][1])
                if h >= 1:
                    decode(h - 1)
                bank = read(v, ("sc", h))
                own(v.tensor_tensor(sc[:, 0:LP], bank[:, 0:LP], mask(h, LP), ALU.mult))
                ins = v.tensor_tensor(sc[:, LP:384], bank[:, LP:384], mask(h, 128), ALU.mult)
                empties(ins, ("sc", h))
                if h >= 1:
                    finish_head(h - 1)
            for g in range(2):
                if g == 0:
                    decode(H - 1)
                    v.wait_ge(filled[7], plan[("st", H - 1, 1)][1])
                    own(v.memset(U[:, :, 0:2], 0.0))
                for j in range(4):
                    name = (("ch", g), j)
                    bank = read(v, name)
                    v.wait_ge(emptied[j], plan[(("cc", g), j)][1])
                    if g == 1 and j == 0:
                        v.wait_ge(filled[4], plan["ct0"][1])
                    empties(v.tensor_tensor(U[:, j, 2:T + 2], bank[:, 0:T], cc[:, j, :], ALU.mult), name)
                for j in range(4):
                    v.wait_ge(emptied[j], plan[(("ch", g), j)][1])
                settle()

                def tap(j, i):
                    return par[:, 4 * g + j, R_CONV + i:R_CONV + i + 1]

                old = par[:, 4 * g:4 * g + 4, R_STATE:R_STATE + 2 * NS].rearrange("p k (b w) -> p k w b", w=2)
                for j in range(4):
                    own(v.tensor_scalar(cv[:, j, 0:LP], U[:, j, 0:LP], tap(j, 0), None, ALU.mult))
                    own(v.tensor_scalar(cv[:, j, LP:T], old[:, j, 0, :], tap(j, 0), None, ALU.mult))
                settle()
                for j in range(4):
                    own(v.scalar_tensor_tensor(cv[:, j, 0:LP], U[:, j, 1:LP + 1], tap(j, 1), cv[:, j, 0:LP], ALU.mult, ALU.add))
                    own(v.scalar_tensor_tensor(cv[:, j, LP:T], old[:, j, 1, :], tap(j, 1), cv[:, j, LP:T], ALU.mult, ALU.add))
                settle()
                for j in range(4):
                    own(v.scalar_tensor_tensor(cv[:, j, :], U[:, j, 2:T + 2], tap(j, 2), cv[:, j, :], ALU.mult, ALU.add))
                settle()
                for j in range(4):
                    name = (("cb", g), j)
                    bank = read(v, name)
                    ins = v.tensor_tensor(aT[:, 4 * g + j, :], bank[:, 0:T], cv[:, j, :], ALU.mult)
                    empties(ins, name)
                for j in range(4):
                    v.wait_ge(emptied[j], plan[(("cb", g), j)][1])
                if g == 0:
                    finish_head(H - 1)
            for g in range(2):
                for j in range(4):
                    name = (("wa", g), j)
                    bank = read(v, name)
                    v.wait_ge(emptied[j], plan[(("ga", g), j)][1])
                    ins = v.tensor_tensor(merged[:, 4 * g + j, :], merged[:, 4 * g + j, :], bank[:, 0:T], ALU.mult)
                    empties(ins, name)
            for g in range(2):
                for j in range(4):
                    name = (("wb", g), j)
                    bank = read(v, name)
                    v.wait_ge(emptied[j], plan[(("gb", g), j)][1])
                    ins = v.tensor_tensor(gbs[:, 4 * g + j, :], gbs[:, 4 * g + j, :], bank[:, 0:T], ALU.mult)
                    empties(ins, name)
                for j in range(4):
                    v.wait_ge(emptied[j], plan[(("wb", g), j)][1])
                for j in range(4):
                    v.tensor_tensor(merged[:, 4 * g + j, :], merged[:, 4 * g + j, :], gbs[:, 4 * g + j, :], ALU.add)\
                        .then_inc(merged_ready, 1)
            for t, n in enumerate(ROWS):
                for c in range(2):
                    bank = read(v, ("wo", t, c))
                    ins = v.tensor_tensor(hx[0:n, t, 512 * c:512 * (c + 1)], hx[0:n, t, 512 * c:512 * (c + 1)],
                                          bank[0:n, :], ALU.add)
                    empties(ins, ("wo", t, c))
            v.wait_ge(sumsq2, 3)
            mean_to(stat[:, 0:3], stat[:, 3:6], mean2)
            v.wait_ge(root2, 1)
            own(v.reciprocal(stat[:, 9:12], stat[:, 6:9]))
            settle()
            v.wait_ge(late_in, 64)
            for t, n in enumerate(ROWS):
                v.scalar_tensor_tensor(xn2[0:n, t, :], hx[0:n, t, :], stat[0:n, 9 + t:10 + t], n2b[0:n, :],
                                       ALU.mult, ALU.mult).then_inc(xn2_ready, 1)
            for k in range(KD):
                name = (f"x2T{k // 4}", k % 4)
                ins = v.tensor_copy(xn2T[:, k, :], read(v, name)[:, 0:T])
                empties(ins, name)
            bank = read(v, "logits")
            for t, n in enumerate(ROWS):
                ins = v.tensor_tensor(small[0:n, t, :], bank[0:n, E * t:E * (t + 1)], router_b[0:n, :], ALU.add)
                if t == 2:
                    empties(ins, "logits")
                else:
                    own(ins)
            v.wait_ge(emptied[4], plan["logits"][1])
            settle()
            for t, n in enumerate(ROWS):
                own(v.max(small[0:n, 3, 8 * t:8 * t + 8], small[0:n, t, :]))
            settle()

            def top(t, i):
                return small[0:ROWS[t], 3, 8 * t + i:8 * t + i + 1]

            for t, n in enumerate(ROWS):
                v.tensor_scalar(stat[0:n, 9 + t:10 + t], top(t, 0), -1.0, None, ALU.mult).then_inc(neg_max, 1)
            for t, n in enumerate(ROWS):
                gt, eq, ceq = small[0:n, 4, :], small[0:n, 5, :], small[0:n, 6, :]
                need = small[0:n, 7, 0:1]
                count = small[0:n, 7, 1:2]
                own(v.tensor_scalar(gt, small[0:n, t, :], top(t, TOP - 1), None, ALU.is_gt))
                own(v.tensor_scalar(eq, small[0:n, t, :], top(t, TOP - 1), None, ALU.is_equal))
                settle()
                own(v.reduce_sum(count, gt, AX.X))
                own(v.tensor_tensor_scan(ceq, ones[0:n, 0:E], eq, 0.0, ALU.mult, ALU.add))
                settle()
                own(v.tensor_scalar(need, count, -1.0, float(TOP), ALU.mult, ALU.add))
                settle()
                own(v.scalar_tensor_tensor(ceq, ceq, need, eq, ALU.is_le, ALU.mult))
                settle()
                v.tensor_tensor(rg[0:n, 1, t, :], gt, ceq, ALU.add).then_inc(selected, 1)
                v.wait_ge(selected, t + 1)
            bank = read(v, "rank")
            for t, n in enumerate(ROWS):
                own(v.scalar_tensor_tensor(rg[0:n, 0, t, :], bank[0:n, E * t:E * (t + 1)], NOT_ROUTED, rg[0:n, 1, t, :],
                                           ALU.add, ALU.mult))
            settle()
            for t, n in enumerate(ROWS):
                own(v.tensor_scalar(rg[0:n, 0, t, :], rg[0:n, 0, t, :], -NOT_ROUTED, None, ALU.add))
            bank = read(v, "count")
            own(v.reduce_max(small[:, 7, 2:3], bank[:, 0:E], AX.X))
            settle()
            own(v.tensor_scalar(small[:, 4, 0:MAX_ROUNDS], cst[:, C_THR:C_THR + MAX_ROUNDS], small[:, 7, 2:3], None, ALU.is_lt))
            settle()
            own(v.reduce_sum(small[:, 7, 3:4], small[:, 4, 0:MAX_ROUNDS], AX.X))
            settle()
            v.tensor_copy(rounds_i[:, :], small[:, 7, 3:4]).then_inc(rounds_ready, 1)
            for t, n in enumerate(ROWS):
                ex = small[0:n, 8 + t, :]
                v.wait_ge(gate_exp, t + 1)
                own(v.tensor_tensor(ex, ex, rg[0:n, 1, t, :], ALU.mult))
                settle()
                own(v.reduce_sum(small[0:n, 7, 4:5], ex, AX.X))
                settle()
                own(v.reciprocal(small[0:n, 7, 5:6], small[0:n, 7, 4:5]))
                settle()
                ins = v.tensor_scalar(rg[0:n, 1, t, :], ex, small[0:n, 7, 5:6], None, ALU.mult)
                if t < 2:
                    own(ins)
            settle()
            ins.then_inc(routed, 1)
            v.wait_ge(routed, 1)
            ins = v.tensor_copy(gT[0:E, :], read(v, "gT")[0:E, 0:T])
            ins.then_inc(gT_ready, 1)
            for t, n in enumerate(ROWS):
                for c in range(2):
                    name = ("b2", t, c)
                    bank = read(v, name)
                    ins = v.tensor_tensor(hx[0:n, t, 512 * c:512 * (c + 1)], hx[0:n, t, 512 * c:512 * (c + 1)],
                                          bank[0:n, :], ALU.add)
                    empties(ins, name)
            for b in range(4):
                v.wait_ge(emptied[b], uses[b])

            v.wait_ge(rounds_ready, 1)
            rounds = v.value_load(rounds_i[0:1, 0:1], min_val=1, max_val=MAX_ROUNDS)
            slots = slot_no.rearrange("p (o s) -> p o s", o=1).to_broadcast([128, 2 * TT, SLOTS])

            def per_slot(n):
                return rgc[:, n, :, :].rearrange("p t (e o) -> p (t e) o", o=1).to_broadcast([128, 2 * TT, SLOTS])

            with v.Fori(0, rounds) as r:
                with v.Fori(0, PAIRS) as pair:
                    it = r * PAIRS + pair
                    v.wait_ge(cols_ready, it + 1)
                    v.wait_ge(pg_turned, it + PRIMED)
                    v.tensor_tensor(P, slots, per_slot(0), ALU.is_equal).then_inc(P_ready, 1)
                    v.wait_ge(P_ready, 2 * it + (1 + PRIMED))
                    v.tensor_tensor(Pg, P, per_slot(1), ALU.mult).then_inc(P_ready, 1)
                    v.wait_ge(gathered, 2 * it + 2)
                    v.tensor_copy(xgT[:, 4:8, :], psum[7][:, :].rearrange("p (k s) -> p k s", k=4)).then_inc(xg_hi, 1)
                    for e in range(2):
                        v.wait_ge(up_done, 2 * it + (e + 1 + PRIMED))
                        v.tensor_scalar(gcl[:, e, :], psum[2 * e][:, :], LIMIT, None, ALU.min).then_inc(g_clip, 1)
                        v.tensor_scalar(ucl[:, e, :], psum[2 * e + 1][:, :], LIMIT, -LIMIT, ALU.min, ALU.max).then_inc(u_clip, 1)
                        v.wait_ge(g_clip, 2 * it + e + 1)
                        v.wait_ge(u_clip, 2 * it + e + 1)
                        v.scalar_tensor_tensor(ucl[:, e, :], ucl[:, e, :], 1.0, gcl[:, e, :], ALU.add, ALU.mult)\
                            .then_inc(ug_ready, 1)
                        v.wait_ge(ug_ready, 2 * it + e + 1)
                        v.wait_ge(sig_ready, 2 * it + e + 1)
                        v.tensor_tensor(acts[:, e, :], ucl[:, e, :], sig[:, e, :], ALU.mult).then_inc(act_ready, 1)
                    for e in range(2):
                        v.wait_ge(down_done, 2 * it + e + 1)
                        v.tensor_copy(ysb[SLOTS * e:SLOTS * (e + 1), 0:512], psum[4][0:64, :]).then_inc(y_ready, 1)
                        v.tensor_copy(ysb[SLOTS * e:SLOTS * (e + 1), 512:1024], psum[4][64:128, :]).then_inc(y_ready, 1)
                    for t, n in enumerate(ROWS):
                        for c in range(2):
                            v.wait_ge(combined, 6 * it + 2 * t + c + 1)
                            v.tensor_tensor(hx[0:n, t, 512 * c:512 * (c + 1)], hx[0:n, t, 512 * c:512 * (c + 1)],
                                            psum[6 + c][0:n, :], ALU.add).then_inc(added, 1)
                    v.wait_ge(added, 6 * it + (6 + PRIMED))
            v.wait_ge(sumsq3, 3)
            mean_to(stat[:, 0:3], stat[:, 3:6], mean3)
            v.wait_ge(root3, 1)
            own(v.reciprocal(stat[:, 9:12], stat[:, 6:9]))
            settle()
            for t, n in enumerate(ROWS):
                v.scalar_tensor_tensor(hx[0:n, t, :], hx[0:n, t, :], stat[0:n, 9 + t:10 + t], nfb[0:n, :],
                                       ALU.mult, ALU.mult).then_inc(y_scaled, 1)

        @block.tensor
        def _(pe):
            at = [0]
            for primed in (pg_turned, up_done):
                pe.sem_inc(primed, PRIMED)

            def chunk_ready(n):
                pe.wait_ge(chunk[n % RING], 16 * (n // RING + 1))

            def weight(n, k):
                return ring[:, n % RING, 512 * k:512 * (k + 1)]

            def project(name, rhs, groups=1):
                first = at[0]
                at[0] += 2 * groups
                for j in range(4):
                    bank = fill(pe, (name, j))
                    for k in range(KD * groups):
                        n = first + k // 4
                        if j == 0 and k % 4 == 0:
                            chunk_ready(n)
                        ins = pe.matmul(bank[:, 0:T], weight(n, k % 4)[:, 128 * j:128 * (j + 1)], rhs[:, k, :],
                                        start=k == 0, stop=k == KD * groups - 1)
                    fills(ins, (name, j))

            pe.wait_ge(cst_in, 16)
            pe.wait_ge(prow_in, 80)
            bank = fill(pe, "par")
            for k in range(KD):
                ins = pe.transpose(bank[:, N_PAR * k:N_PAR * (k + 1)], prow[0:N_PAR, 128 * k:128 * (k + 1)],
                                   ident[0:N_PAR, 0:N_PAR])
            fills(ins, "par")
            pe.wait_ge(xn_ready, 3)
            for k in range(KD):
                name = (f"xT{k // 4}", k % 4)
                bank = fill(pe, name)
                for t, n in enumerate(ROWS):
                    ins = pe.transpose(bank[:, 128 * t:128 * t + n], xn[0:n, t, 128 * k:128 * (k + 1)], ident[0:n, 0:n])
                fills(ins, name)
            for j in range(4):
                pe.wait_ge(emptied[j], plan[("xT1", j)][1])

            def decode(h):
                bank = fill(pe, ("rs", h))
                for b in range(NS):
                    n = NS * h + b
                    pe.wait_ge(S_new, n + 1)
                    for half in range(2):
                        for j in range(NV):
                            ins = pe.matmul(bank[32 * j:32 * (j + 1), 0:128], qsm[:, h % 2, half, 32 * b:32 * (b + 1)],
                                            S[n % 3][:, half, 128 * j:128 * (j + 1)],
                                            start=b == 0 and half == 0, stop=b == NS - 1 and half == 1)
                    if b < NS - 1:
                        ins.then_inc(S_read, 1)
                fills(ins, ("rs", h))
                bank = fill(pe, ("rsT", h))
                pe.wait_ge(emptied[5], plan[("rs", h)][1])
                fills(pe.transpose(bank[:, 0:128], rs_t[:, :], ident), ("rsT", h))

            def squares(h):
                bank = fill(pe, ("ss", h))
                pe.wait_ge(sq_ready, h + 1)
                for j in range(NV):
                    ins = pe.matmul(bank[:, 0:T], ones[:, :], sq[:, j, :], start=j == 0, stop=j == NV - 1)
                fills(ins, ("ss", h))

            for h in range(H):
                if h % 2 == 0:
                    project(("q", h // 2), xnT)
                    project(("k", h // 2), xnT)
                if h == 0:
                    pe.wait_ge(xsT_ready, 1)
                first = at[0]
                at[0] += 2
                for t in range(3):
                    bank = fill(pe, (("v", h), t))
                    for k in range(KD):
                        w = weight(first + k // 4, k % 4)
                        if t == 0 and k % 4 == 0:
                            chunk_ready(first + k // 4)
                        if t < 2:
                            ins = pe.matmul(bank[:, :], xnT[:, k, 128 * t:128 * (t + 1)], w, start=k == 0, stop=k == KD - 1)
                        else:
                            for j in range(4):
                                ins = pe.matmul(bank[32 * j:32 * (j + 1), 0:128], xsT[:, k, :], w[:, 128 * j:128 * (j + 1)],
                                                start=k == 0, stop=k == KD - 1)
                    fills(ins, (("v", h), t))
                project(("g", h), xnT)
                if h >= 1:
                    decode(h - 1)
                hh = 2 * (h % 2)
                pe.wait_ge(qk_ready, 8 * (h // 2 + 1))
                bank = fill(pe, ("kt", h))
                for t in range(2):
                    for half in range(2):
                        ins = pe.transpose(bank[:, DK * t + 128 * half:DK * t + 128 * (half + 1)],
                                           kT[:, hh + half, 128 * t:128 * (t + 1)], ident)
                fills(ins, ("kt", h))
                bank = fill(pe, ("sc", h))
                for half in range(2):
                    pe.matmul(bank[:, 0:LP], kT[:, hh + half, 0:128], qT[:, hh + half, 0:LP], start=half == 0, stop=half == 1)
                for half in range(2):
                    ins = pe.matmul(bank[:, LP:384], kT[:, hh + half, 128:256], qT[:, hh + half, 128:256],
                                    start=half == 0, stop=half == 1)
                fills(ins, ("sc", h))
                pe.wait_ge(emptied[5], plan[("sc", h)][1])
                for t in range(2):
                    pe.wait_ge(emptied[t], plan[(("v", h), t)][1])
                for g in range(2):
                    bank = fill(pe, ("out", h, g))
                    for j in range(2):
                        dv = 128 * (2 * g + j)
                        pe.matmul(bank[:, LP * j:LP * (j + 1)], v_sb[:, 0, dv:dv + 128], sc[:, 0:LP], start=True, stop=False)
                        ins = pe.matmul(bank[:, LP * j + 128:LP * (j + 1)], v_sb[:, 1, dv:dv + 128], sc[:, LP:384],
                                        start=False, stop=True)
                    fills(ins, ("out", h, g))
                pe.wait_ge(emptied[4], plan[("kt", h)][1])
                for g in range(2):
                    bank = fill(pe, ("st", h, g))
                    for t in range(2):
                        ins = pe.matmul(bank[:, :], ktok[:, t, 128 * g:128 * (g + 1)], v_sb[:, t, :], start=t == 0, stop=t == 1)
                    fills(ins, ("st", h, g))
                if h >= 1:
                    squares(h - 1)
            project(("cc", 0), xnT)
            decode(H - 1)
            project(("ch", 0), xnT)
            project(("cb", 0), xnT)
            squares(H - 1)
            project(("cc", 1), xnT)
            bank = fill(pe, "ct0")
            for j in range(4):
                pe.wait_ge(emptied[j], plan[(("ch", 0), j)][1])
            for j in range(4):
                ins = pe.transpose(bank[0:NS + 2, 128 * j:128 * (j + 1)], U[:, j, LP:T + 2], ident)
            fills(ins, "ct0")
            project(("ch", 1), xnT)
            project(("cb", 1), xnT)
            bank = fill(pe, "ct1")
            for j in range(4):
                pe.wait_ge(emptied[j], plan[(("ch", 1), j)][1])
            for j in range(4):
                ins = pe.transpose(bank[0:NS + 2, 128 * j:128 * (j + 1)], U[:, j, LP:T + 2], ident)
            fills(ins, "ct1")
            for g in range(2):
                project(("ga", g), xnT)
            for j in range(4):
                pe.wait_ge(emptied[j], plan[(("cb", 1), j)][1])
            for g in range(2):
                project(("wa", g), aT)
            for g in range(2):
                project(("gb", g), xnT)
            pe.wait_ge(rT_ready, H)
            for g in range(2):
                project(("wb", g), rT, groups=2)
            pe.wait_ge(merged_ready, KD)
            first = at[0]
            assert first == MIXER_CHUNKS - 4
            for n in range(4):
                chunk_ready(first + n)
            for t, rows in enumerate(ROWS):
                for c in range(2):
                    bank = fill(pe, ("wo", t, c))
                    for k in range(KD):
                        ins = pe.matmul(bank[0:rows, :], merged[:, k, 128 * t:128 * t + rows], weight(first + 2 * c + k // 4, k % 4),
                                        start=k == 0, stop=k == KD - 1)
                    fills(ins, ("wo", t, c))
            pe.wait_ge(xn2_ready, 3)
            for k in range(KD):
                name = (f"x2T{k // 4}", k % 4)
                bank = fill(pe, name)
                for t, n in enumerate(ROWS):
                    ins = pe.transpose(bank[:, 128 * t:128 * t + n], xn2[0:n, t, 128 * k:128 * (k + 1)], ident[0:n, 0:n])
                fills(ins, name)
            for j in range(4):
                pe.wait_ge(emptied[j], plan[("x2T1", j)][1])
            bank = fill(pe, "logits")
            for t, n in enumerate(ROWS):
                for k in range(KD):
                    ins = pe.matmul(bank[0:n, E * t:E * (t + 1)], xn2T[:, k, 128 * t:128 * t + n], router[:, k, :],
                                    start=k == 0, stop=k == KD - 1)
            fills(ins, "logits")
            pe.wait_ge(selected, 3)
            bank = fill(pe, "rank")
            for t, n in enumerate(ROWS):
                for s in range(t + 1):
                    ins = pe.matmul(bank[0:n, E * t:E * (t + 1)], (tri if s == t else ones)[0:ROWS[s], 0:n],
                                    rg[0:ROWS[s], 1, s, :], start=s == 0, stop=s == t)
            fills(ins, "rank")
            bank = fill(pe, "count")
            for s in range(TT):
                ins = pe.matmul(bank[:, 0:E], ones[0:ROWS[s], :], rg[0:ROWS[s], 1, s, :], start=s == 0, stop=s == TT - 1)
            fills(ins, "count")
            pe.wait_ge(routed, 1)
            bank = fill(pe, "gT")
            for t, n in enumerate(ROWS):
                ins = pe.transpose(bank[0:E, 128 * t:128 * t + n], rg[0:n, 1, t, :], ident[0:n, 0:n])
            fills(ins, "gT")
            pe.wait_ge(gT_ready, 1)
            pe.wait_ge(late_in, 64)
            for t, n in enumerate(ROWS):
                for c in range(2):
                    bank = fill(pe, ("b2", t, c))
                    fills(pe.matmul(bank[0:n, :], gT[0:E, 128 * t:128 * t + n], b2[0:E, 512 * c:512 * (c + 1)],
                                    start=True, stop=True), ("b2", t, c))
            for b in range(4):
                pe.wait_ge(emptied[b], uses[b])

            rounds_at = rounds_i[0:1, 0:1]
            pe.wait_ge(rounds_ready, 1)
            rounds = pe.value_load(rounds_at, min_val=1, max_val=MAX_ROUNDS)
            uses_before = MIXER_CHUNKS // RING
            with pe.Fori(0, rounds) as r:
                with pe.Fori(0, PAIRS) as pair:
                    it = r * PAIRS + pair

                    def slot_ready(n):
                        pe.wait_ge(chunk[n % RING], 32 * it + 16 * (uses_before + n // RING + 1))

                    pe.wait_ge(P_ready, 2 * it + (2 + PRIMED))
                    pe.wait_ge(added, 6 * it + PRIMED)
                    for half in range(2):
                        for k in range(4 * half, 4 * half + 4):
                            for t, n in enumerate(ROWS):
                                ins = pe.matmul(psum[6 + half][:, 128 * (k % 4):128 * (k % 4 + 1)],
                                                xn2[0:n, t, 128 * k:128 * (k + 1)],
                                                P[0:n, 2 * t:2 * t + 2, :],
                                                start=t == 0, stop=t == TT - 1)
                        ins.then_inc(gathered, 1)
                    pe.wait_ge(actT_ready, 2 * it + PRIMED)
                    for t, n in enumerate(ROWS):
                        ins = pe.transpose(psum[5][:, 128 * t:128 * t + n],
                                           Pg[0:n, 2 * t:2 * t + 2, :].rearrange("p e s -> p (e s)"), ident[0:n, 0:n])
                    ins.then_inc(pg_turned, 1)
                    pe.wait_ge(pick_ready, it + 1)
                    for e in range(2):
                        if e == 0:
                            pe.wait_ge(xg_lo, it + 1)
                            pe.wait_ge(xg_hi, it + 1)
                        for k in range(-1, KD):
                            if k >= 0:
                                slot_ready(KD * e + k)
                            for q in range(2):
                                for half in range(2):
                                    out = psum[2 * e + q][64 * half:64 * (half + 1), :]
                                    c = D * q + 512 * half
                                    if k < 0:
                                        pe.matmul(out, pick[:, e, :], b1[:, c:c + 512], start=True, stop=False)
                                    else:
                                        ins = pe.matmul(out, xgT[:, k, 64 * e:64 * (e + 1)],
                                                        ring[:, (KD * e + k) % RING, c:c + 512], start=False, stop=k == KD - 1)
                            if k >= 0:
                                ins.then_inc(up_done if k == KD - 1 else chunk_used, 1)
                    for e in range(2):
                        pe.wait_ge(act_ready, 2 * it + e + 1)
                        if e == 0:
                            pe.wait_ge(pgT_ready, it + 1)
                        else:
                            pe.wait_ge(actT_ready, 2 * it + (e + PRIMED))
                        for k in range(4):
                            ins = pe.transpose(psum[5][:, 128 * k:128 * (k + 1)], acts[:, e, 128 * k:128 * (k + 1)], ident)
                        ins.then_inc(act_turned, 1)
                        pe.wait_ge(actT_ready, 2 * it + (e + 1 + PRIMED))
                        pe.wait_ge(y_ready, 4 * it + (2 * e + PRIMED))
                        for f in range(KD):
                            n = 2 * KD + 4 * e + f // 2
                            if f % 2 == 0:
                                slot_ready(n)
                            lhs = actT[:, e, 128 * (f % 4) + 64 * (f // 4):128 * (f % 4) + 64 * (f // 4) + 64]
                            for half in range(2):
                                c = D * (f % 2) + 512 * half
                                ins = pe.matmul(psum[4][64 * half:64 * (half + 1), :], lhs, ring[:, n % RING, c:c + 512],
                                                start=f == 0, stop=f == KD - 1)
                            if f % 2 == 1:
                                ins.then_inc(down_done if f == KD - 1 else chunk_used, 1)
                    pe.wait_ge(y_ready, 4 * it + (4 + PRIMED))
                    for t, n in enumerate(ROWS):
                        for c in range(2):
                            if t:
                                pe.wait_ge(added, 6 * it + (2 * t + c - 1 + PRIMED))
                            pe.matmul(psum[6 + c][0:n, :], pgT[:, 128 * t:128 * t + n], ysb[:, 512 * c:512 * (c + 1)],
                                      start=True, stop=True).then_inc(combined, 1)


INPUTS = ["x_prompt", "x_sample", "state_conv", "state_ret", "norm1", "w_in", "conv_w", "w_a", "w_b", "w_o", "norm2",
          "w_router", "b_router", "w_e1", "b_e1", "w_e2", "b_e2", "norm_f"]
OUTPUTS = [("y_prompt", (1, LP, D)), ("y_sample", (NS, 1, D)), ("conv_prompt", (1, 1, 2, D)),
           ("ret_prompt", (1, 1, H, DK, DV)), ("conv_sample", (1, NS, 2, D)), ("ret_sample", (1, NS, H, DK, DV))]


def kernel(**inputs):
    import concourse.bacc as bacc
    from concourse.bass_utils import run_bass_kernel_spmd

    nc = bacc.Bacc("TRN2", target_bir_lowering=False, num_devices=1)
    arrays = {name: np.ascontiguousarray(inputs[name]) for name in INPUTS}
    arrays["tables"] = shape_constants()
    a = {n: nc.dram_tensor(f"in_{n}", x.shape, F32, kind="ExternalInput").ap() for n, x in arrays.items()}
    o = {n: nc.dram_tensor(f"out_{n}", s, F32, kind="ExternalOutput").ap() for n, s in OUTPUTS}
    build(nc, a, o)
    r = run_bass_kernel_spmd(nc, [{f"in_{n}": x for n, x in arrays.items()}], core_ids=[0])
    return tuple(r.results[0][f"out_{n}"] for n, _ in OUTPUTS)
```

```python
import concourse.bass as bass
from concourse import mybir
from contextlib import ExitStack
import numpy as np

F32 = mybir.dt.float32
BF16 = mybir.dt.bfloat16
I32 = mybir.dt.int32
ALU = mybir.AluOpType
ACT = mybir.ActivationFunctionType
AX = mybir.AxisListType

D = 1024
LP = 256
NS = 8
T = LP + NS
TT = 3
ROWS = (128, 128, NS)
KD = D // 128
H = 4
DK = D // H
DV = 2 * DK
NV = DV // 128
PAST = 2048
E = 32
TOP = 4
SLOTS = 64
PAIRS = E // 2
MAX_ROUNDS = -(-T // SLOTS)
ALPHA = 1.702
LIMIT = 7.0
EPS = 1e-5
PRIMED = 1
NOT_ROUTED = 4096.0

RING = 12
CH = 2048
MIXER_CHUNKS = 5 * RING
PAIR_CHUNKS = 2 * RING
COUNTED = PAIR_CHUNKS - 4

C_COS, C_SIN, C_COSK, C_SINK = 0, T, 2 * T, 3 * T
C_MASK = 4 * T
C_ID = C_MASK + H * LP
C_TRI = C_ID + 128
C_KDEC = C_TRI + 128
C_SLOT = C_KDEC + 2 * H
C_THR = C_SLOT + SLOTS
C_PICK = C_THR + MAX_ROUNDS
N_CONST = C_PICK + E

W_CB, W_CC, W_CH, W_Q, W_K, W_V, W_G, W_GA, W_GB = (0, 1024, 2048, 3072, 4096, 5120, 7168, 9216, 10240)

R_STATE, R_CONV, R_NORM, N_PAR = 0, 2 * NS, 2 * NS + 3, 2 * NS + 4


def gamma(h):
    return 1.0 - 2.0 ** (-5 - h)


def shape_constants():
    f = np.float32
    c = np.zeros((128, N_CONST), f)
    pos = np.concatenate([np.arange(LP), np.full(NS, PAST)]).astype(f)
    inv = f(10000.0) ** (-np.linspace(0.0, 1.0, 128, dtype=f))
    ang = (pos[None, :] * inv[:, None]).astype(f)
    c[:, C_COS:C_COS + T] = np.cos(ang)
    c[:, C_SIN:C_SIN + T] = np.sin(ang)
    c[:, C_COSK:C_COSK + T] = c[:, C_COS:C_COS + T] * f(DK ** -0.5)
    c[:, C_SINK:C_SINK + T] = c[:, C_SIN:C_SIN + T] * f(DK ** -0.5)
    p = np.arange(128)
    q = np.arange(LP)
    for h in range(H):
        d = q[None, :] - p[:, None]
        c[:, C_MASK + h * LP:C_MASK + (h + 1) * LP] = np.where(d >= 0, gamma(h) ** np.maximum(d, 0), 0.0)
        for t in range(2):
            c[:, C_KDEC + 2 * h + t] = gamma(h) ** (LP - 1 - (t * 128 + p)).astype(np.float64)
    c[:, C_ID:C_ID + 128] = np.eye(128)
    c[:, C_TRI:C_TRI + 128] = p[:, None] < p[None, :]
    c[:, C_SLOT:C_SLOT + SLOTS] = np.arange(SLOTS)
    c[:, C_THR:C_THR + MAX_ROUNDS] = np.arange(MAX_ROUNDS) * SLOTS
    for part in range(3):
        c[32 * part:32 * part + E, C_PICK:C_PICK + E] = np.eye(E)
    return c


PROJ_BANKS = 3
RS_BANK, TURN_BANK, SUM_BANK = 3, 4, 5
STEP_EVERY_US = 6.8
VALUES_TO_STEP_US = 12.0


def mixer_order():
    main = []

    def proj(name, us=3.6):
        main.extend([(("proj", name, j), us) for j in range(4)])

    for h in range(H):
        if h % 2 == 0:
            proj(("q", h // 2))
            proj(("k", h // 2))
        main.extend([(("v", h, 2), 2.2), (("vs", h), 0.0), (("v", h, 0), 7.0), (("qs", h), 0.0), (("kt", h), 0.5),
                     (("sc", h), 1.4), (("v", h, 1), 7.0)])
        proj(("g", h))
        main.extend([(("out", h), 2.7), (("st", h), 3.6)])
    for g in range(2):
        for n in ("cc", "ch", "cb"):
            proj((n, g))
            if n == "ch":
                main.append((("taps", g), 0.0))
        main.append((("ct", g), 0.5))
    order, ends = [], []
    now, last, n = 0.0, 0.0, 0
    values_at = {}
    for event, us in main:
        order.append(event)
        now += us
        if event[0] == "vs":
            values_at[event[1]] = now
        if us < 2.0:
            continue
        if ends:
            order.append(ends.pop(0))
        if n < H * NS and n // NS in values_at and now - values_at[n // NS] > VALUES_TO_STEP_US \
                and now - last >= STEP_EVERY_US:
            order.append(("prep", n))
            if n:
                order.append(("step", n - 1))
            n += 1
            last = now
            now += 1.0
            if n % NS == 1 and n > 1:
                ends += [("rsT", n // NS - 1), ("sqr", n // NS - 1), ("ss", n // NS - 1)]
    assert n == H * NS
    order.append(("step", n - 1))
    order += ends + [("rsT", H - 1)]
    for g in range(2):
        order += [("proj", ("ga", g), j) for j in range(4)]
        if g == 0:
            order += [("sqr", H - 1), ("ss", H - 1)]
    for name in ("wa", "gb", "wb"):
        for g in range(2):
            order += [("proj", (name, g), j) for j in range(4)]
    at = {e: i for i, e in enumerate(order)}
    assert len(at) == len(order)
    for h in range(H - 2):
        assert at["ss", h] < at["proj", ("g", h + 2), 0] and at["rsT", h] < at["qs", h + 2]
    return order


def bank_plan(order):
    count, plan = [0] * 8, {}

    def use(name, bank):
        count[bank] += 1
        plan[name] = (bank, count[bank])

    use("par", TURN_BANK)
    for k in range(KD):
        use(("xT", k), k % PROJ_BANKS)
    n = KD
    for event in order:
        what, *which = event
        if what in ("proj", "v"):
            use(event, n % PROJ_BANKS)
            n += 1
        elif what == "step" and which[0] % NS == 0:
            use(("rs", which[0] // NS), RS_BANK)
        elif what in ("rsT", "kt"):
            use(event, TURN_BANK)
        elif what in ("sc", "ss"):
            use(event, SUM_BANK)
        elif what in ("out", "st"):
            use((what, which[0], 0), 6)
            use((what, which[0], 1), 7)
        elif what == "ct":
            use(event, TURN_BANK)
    for t in range(2):
        for c in range(2):
            use(("wo", t, c), 2 * t + c)
    use(("wo", 2, 0), 4)
    for t in range(2):
        for g in range(2):
            use(("x2T", t, g), 5 + (2 * t + g) % 3)
    use(("x2T", 2, 0), 0)
    use("logits", 1)
    use("rank", 2)
    use("count", 3)
    use("gT", 4)
    for t in range(TT):
        for c in range(2):
            use(("b2", t, c), 2 * (t % 2) + c)
    return plan, count


def build(nc, a, o):
    order = mixer_order()
    plan, uses = bank_plan(order)
    ctx = ExitStack()
    with ctx:
        def sb(name, shape, dt=F32):
            return ctx.enter_context(nc.sbuf_tensor(name, shape, dt))

        def sem(name):
            return ctx.enter_context(nc.semaphore(name))

        ring = sb("ring", [128, RING, CH])
        hx = sb("hx", [128, TT, D])
        cst = sb("cst", [128, N_CONST])
        par = sb("par", [128, KD, N_PAR])
        ones = sb("ones", [128, 128])
        stat = sb("stat", [128, 16])
        router = sb("router", [128, KD, E])
        router_b = sb("router_b", [128, E])
        rg = sb("rg", [128, 2, TT, E])
        rgc = sb("rgc", [128, 2, TT, 2])
        rounds_i = sb("rounds_i", [128, 1], I32)
        arena = sb("arena", [128, 21700])

        def view(at, *dims):
            n = int(np.prod(dims))
            assert at + n <= 21700
            v = arena[:, at:at + n]
            if len(dims) == 2:
                v = v.rearrange("p (a b) -> p a b", a=dims[0])
            if len(dims) == 3:
                v = v.rearrange("p (a b c) -> p a b c", a=dims[0], b=dims[1])
            return v

        squares_out = view(8704, TT, D)
        xnT = view(0, KD, T)
        xsT = view(2112, KD, 32)
        rT = view(2368, H * NV, T)
        xn = view(2368, TT, D)
        prow = view(15100, 1024)
        sg = view(6592, 2, 4, T)
        qT = view(8704, 4, T)
        kT = view(9760, 4, T)
        rot = view(10816, 4, T)
        v_sb = view(11872, 2, DV)
        vs_sb = view(12896, 128)
        ktok = view(13024, 2, DK)
        sc = view(13536, 384)
        st = view(14000, 2, DV)
        sq = view(15100, NV, T)
        rinv = view(16160, T)
        qsm = view(16424, 2, 2, NS * 32)
        ks = view(17448, 2, 2 * NS)
        S = [view(17480 + 1024 * n, 2, DV) for n in range(3)]
        vb = [view(20552 + 512 * n, DV) for n in range(2)]
        cc = view(8704, 4, T)
        U = view(9760, 4, T + 2)
        cv = view(10824, 4, T)
        aT = view(11880, KD, T)
        ctok = view(14000, D)
        merged = view(6592, KD, T)
        gas = merged
        gbs = view(8704, KD, T)
        xn2 = view(0, TT, D)
        xn2T = view(3072, KD, T)
        ws = view(5184, D)
        route = view(6592, 20, E)
        squares2 = [view(12824, D), view(13848, D), view(7232, D)]
        rest = squares2
        xp = view(9240, 3 * 2 * D // 2).bitcast(BF16).rearrange("p (n t d) -> p n t d", n=3, t=2)
        xps = view(12312, D // 2).bitcast(BF16)
        P = view(8336, TT * 2 * SLOTS // 2).bitcast(BF16).rearrange("p (t s) -> p t s", s=SLOTS)
        Pg = view(8528, TT * 2, SLOTS)
        pick = view(8912, SLOTS).bitcast(BF16).rearrange("p (e s) -> p e s", e=2)
        gT = view(8976, T)
        xgT = view(0, KD, 128)
        gcl = view(1024, 2, 512)
        ucl = view(2048, 2, 512)
        sig = view(3072, 2, 512)
        acts = view(4096, 2, 512)
        squares3 = view(1024, TT, D)
        actT = view(5120, 2, 512)
        ysb = view(6144, D)
        pgT = view(7168, T)
        n2b = view(15100, D)
        nfb = view(16124, D)
        b2 = view(17148, D)
        b1 = view(18172, 2 * D)
        bp = view(20220, D).bitcast(BF16)
        b1_rest = view(10816, 2 * D)
        b1_part = view(12864, D).bitcast(BF16)
        rs_t = sb("rs_t", [128, 128])
        sample_part = view(18172, 3 * D // 2).bitcast(BF16).rearrange("p (n d) -> p n d", n=3)

        psum = [ctx.enter_context(nc.psum_tensor(f"bank{n}", [128, 512], F32)) for n in range(8)]

        cos, sin = cst[:, C_COS:C_COS + T], cst[:, C_SIN:C_SIN + T]
        cosk, sink = cst[:, C_COSK:C_COSK + T], cst[:, C_SINK:C_SINK + T]
        ident = cst[:, C_ID:C_ID + 128]
        tri = cst[:, C_TRI:C_TRI + 128]
        slot_no = cst[:, C_SLOT:C_SLOT + SLOTS]

        def mask(h, n):
            return cst[:, C_MASK + h * LP:C_MASK + h * LP + n]

        v_dram = nc.dram_tensor("v_decode", (H, NS, DV), F32, kind="Internal").ap()

        chunk = [sem(f"chunk{n}") for n in range(RING)]
        chunk_used = sem("chunk_used")
        filled = [sem(f"filled{n}") for n in range(8)]
        emptied = [sem(f"emptied{n}") for n in range(8)]
        x_in, cst_in, prow_in, row0_out = sem("x_in"), sem("cst_in"), sem("prow_in"), sem("row0_out")
        const_set = sem("const_set")
        sumsq, mean1, root1, xn_ready = sem("sumsq"), sem("mean1"), sem("root1"), sem("xn_ready")
        xsT_ready = sem("xsT_ready")
        dve, act = sem("dve"), sem("act")
        qk_ready = sem("qk_ready")
        vs_out = [sem("vs_out0"), sem("vs_out1")]
        gate_sig, st_out = sem("gate_sig"), sem("st_out")
        qs_ready = sem("qs_ready")
        S_in = [sem(f"S_in{n}") for n in range(3)]
        S_out = [sem(f"S_out{n}") for n in range(3)]
        vb_in = [sem(f"vb_in{n}") for n in range(2)]
        S_scaled, S_new, S_read = sem("S_scaled"), sem("S_new"), sem("S_read")
        sq_ready = sem("sq_ready")
        rT_ready, ctok_out, merged_ready = sem("rT_ready"), sem("ctok_out"), sem("merged_ready")
        late_in = sem("late_in")
        b1_zero = sem("b1_zero")
        sumsq2, mean2, root2 = sem("sumsq2"), sem("mean2"), sem("root2")
        ws_ready, x2T_ready, part_ready, rest_ready, parts_zero = (sem("ws_ready"), sem("x2T_ready"), sem("part_ready"),
                                                                   sem("rest_ready"), sem("parts_zero"))
        h_decode, xps_ready = sem("h_decode"), sem("xps_ready")
        xn2_ready, below_max, gate_exp = sem("xn2_ready"), sem("below_max"), sem("gate_exp")
        selected, routed, rounds_ready, gT_ready = sem("selected"), sem("routed"), sem("rounds_ready"), sem("gT_ready")
        cols_ready, pick_ready, P_ready = sem("cols_ready"), sem("pick_ready"), sem("P_ready")
        gathered, xg_lo, xg_hi = sem("gathered"), sem("xg_lo"), sem("xg_hi")
        pg_turned, pgT_ready = sem("pg_turned"), sem("pgT_ready")
        up_done, g_clip, u_clip, sig_ready, ug_ready, act_ready = (sem("up_done"), sem("g_clip"), sem("u_clip"),
                                                                   sem("sig_ready"), sem("ug_ready"), sem("act_ready"))
        act_turned, actT_ready, down_done, y_ready = sem("act_turned"), sem("actT_ready"), sem("down_done"), sem("y_ready")
        combined, added, round_done = sem("combined"), sem("added"), sem("round_done")
        sumsq3, mean3, root3, y_scaled, y_out = sem("sumsq3"), sem("mean3"), sem("root3"), sem("y_scaled"), sem("y_out")

        block = ctx.enter_context(nc.Block())

        def fill(pe, name):
            bank, n = plan[name]
            if n > 1:
                pe.wait_ge(emptied[bank], n - 1)
            return psum[bank]

        def fills(ins, name):
            ins.then_inc(filled[plan[name][0]], 1)

        def read(eng, name):
            bank, n = plan[name]
            eng.wait_ge(filled[bank], n)
            return psum[bank]

        def empties(ins, name):
            ins.then_inc(emptied[plan[name][0]], 1)

        def was_read(eng, name):
            bank, n = plan[name]
            eng.wait_ge(emptied[bank], n)

        def was_filled(eng, name):
            bank, n = plan[name]
            eng.wait_ge(filled[bank], n)

        w_in = a["w_in"][0]

        def cols(w, c):
            return [w[512 * n:512 * (n + 1), c:c + 512].rearrange("(k p) n -> p k n", p=128) for n in range(2)]

        def mixer_chunks():
            def group(w, c, last):
                return [(x, last) for x in cols(w, c)]

            def tiles(name, w, c):
                return group(w, c, ("proj", name, 3))

            for g in range(2):
                yield from tiles(("q", g), w_in, W_Q + 512 * g)
                yield from tiles(("k", g), w_in, W_K + 512 * g)
                for h in (2 * g, 2 * g + 1):
                    yield from group(w_in, W_V + DV * h, ("v", h, 1))
                    yield from tiles(("g", h), w_in, W_G + DV * h)
            for g in range(2):
                for n, w in (("cc", W_CC), ("ch", W_CH), ("cb", W_CB)):
                    yield from tiles((n, g), w_in, w + 512 * g)
            for n, w, c in (("ga", w_in, W_GA), ("wa", a["w_a"][0], 0), ("gb", w_in, W_GB)):
                for g in range(2):
                    yield from tiles((n, g), w, c + 512 * g)
            for g in range(2):
                for half in range(2):
                    yield from tiles(("wb", g), a["w_b"][0][D * half:D * (half + 1), :], 512 * g)
            for g in range(2):
                yield from group(a["w_o"][0], 512 * g, ("wo", 2, 0))

        w1_rows = a["w_e1"].rearrange("l e (k p) n -> (l e) k p n", p=128)
        w2_rows = a["w_e2"].rearrange("l e (k two p) n -> (l e) k p two n", p=128, two=2)

        @block.sync
        def _(sp):
            sp.dma_start(hx[:, 0:2, :], a["x_prompt"][0].rearrange("(t p) d -> p t d", p=128)).then_inc(x_in, 16)
            sp.dma_start(hx[0:NS, 2, :], a["x_sample"][:, 0, :]).then_inc(x_in, 16)
            sp.dma_start(cst[:, :], a["tables"]).then_inc(cst_in, 16)
            mixer = list(mixer_chunks())
            assert len(mixer) == MIXER_CHUNKS

            def slot_free(n):
                was_filled(sp, mixer[n][1])

            for n, (src, _) in enumerate(mixer):
                if n >= RING:
                    slot_free(n - RING)
                sp.dma_start(ring[:, n % RING, :].rearrange("p (k n) -> p k n", k=4), src).then_inc(chunk[n % RING], 16)

            def pair_order():
                return [(True, e, k) for e in range(2) for k in range(8)] + [(False, e, k) for e in range(2) for k in range(4)]

            def used(it, n):
                w1, e, k = pair_order()[n]
                if k == (7 if w1 else 3):
                    sp.wait_ge(up_done if w1 else down_done, 2 * it + (e + 1 + (PRIMED if w1 else 0)))
                else:
                    before = 7 * e + k if w1 else 14 + 3 * e + k
                    sp.wait_ge(chunk_used, COUNTED * it + (before + 1))

            def load_pair(it, pair, first=False):
                for n, (w1, e, k) in enumerate(pair_order()):
                    dst = ring[:, n % RING, :]
                    if w1:
                        src = w1_rows[bass.ds(2 * pair + e, 1), k].rearrange("e p n -> p (e n)")
                    else:
                        src = w2_rows[bass.ds(2 * pair + e, 1), k].rearrange("e p two n -> p (e two) n")
                        dst = dst.rearrange("p (two n) -> p two n", two=2)
                    if n >= RING:
                        used(it, n - RING)
                    elif first:
                        slot_free(MIXER_CHUNKS - RING + n)
                    else:
                        used(it - 1, n + RING)
                    sp.dma_start(dst, src).then_inc(chunk[n % RING], 16)

            load_pair(0, 0, first=True)
            with sp.Fori(1, PAIRS) as pair:
                load_pair(pair, pair)
            sp.wait_ge(rounds_ready, 1)
            rounds = sp.value_load(rounds_i[0:1, 0:1], min_val=1, max_val=MAX_ROUNDS)
            with sp.If(rounds > 1):
                with sp.Fori(1, rounds) as r:
                    with sp.Fori(0, PAIRS) as pair:
                        load_pair(r * PAIRS + pair, pair)
            for t in range(TT):
                sp.wait_ge(y_scaled, t + 1)
                dst = o["y_prompt"][0, 128 * t:128 * (t + 1), :] if t < 2 else o["y_sample"][:, 0, :]
                sp.dma_start(dst, hx[0:ROWS[t], t, :]).then_inc(y_out, 16)
            sp.wait_ge(y_out, 16 * TT)

        @block.gpsimd
        def _(pool):
            pool.memset(ones[:, :], 1.0).then_inc(const_set, 1)
            pool.memset(rg[:, 0, :, :], -NOT_ROUTED).then_inc(const_set, 1)
            pool.memset(rg[:, 1, :, :], 0.0).then_inc(const_set, 1)
            pool.memset(qsm[:, :, :, :], 0.0).then_inc(const_set, 1)
            pool.memset(xsT[:, :, :], 0.0).then_inc(const_set, 1)
            pool.memset(stat[:, :], 1.0).then_inc(const_set, 1)
            src = a["state_ret"][0]
            total = H * NS

            def load(n):
                h, b = divmod(n, NS)
                if n >= 3:
                    pool.wait_ge(S_out[n % 3], 16 * (n // 3))
                    was_h, was_b = divmod(n - 3, NS)
                    if was_b == NS - 1:
                        was_filled(pool, ("rs", was_h))
                    else:
                        pool.wait_ge(S_read, (NS - 1) * was_h + was_b + 1)
                pool.dma_start(S[n % 3], src[b, h].rearrange("(k p) v -> p k v", p=128)).then_inc(S_in[n % 3], 16)

            def load_v(n):
                h, b = divmod(n, NS)
                if b == 0:
                    pool.wait_ge(vs_out[h % 2], 64 * (h // 2 + 1))
                if n >= 2:
                    pool.wait_ge(S_new, n - 1)
                pool.dma_start(vb[n % 2], v_dram[h, b:b + 1, :].to_broadcast([128, DV])).then_inc(vb_in[n % 2], 16)

            for n in range(3):
                load(n)
            for n in range(2):
                load_v(n)
            for n in range(total):
                h, b = divmod(n, NS)
                pool.wait_ge(S_new, n + 1)
                pool.dma_start(o["ret_sample"][0, b, h].rearrange("(k p) v -> p k v", p=128), S[n % 3])\
                    .then_inc(S_out[n % 3], 16)
                if n + 2 < total:
                    load_v(n + 2)
                if n + 3 < total:
                    load(n + 3)
            for n in range(3):
                pool.wait_ge(S_out[n], 16 * len(range(n, total, 3)))
            pool.wait_ge(rT_ready, H)
            was_filled(pool, ("ss", H - 1))
            pool.memset(bp[:, :], 0.0).then_inc(b1_zero, 1)
            pool.dma_start(b1[0:E, :], a["b_e1"][0]).then_inc(late_in, 16)
            pool.dma_start(b2[0:E, :], a["b_e2"][0]).then_inc(late_in, 16)
            pool.dma_start(n2b[:, :], a["norm2"][0:1, :].to_broadcast([128, D])).then_inc(late_in, 16)
            pool.dma_start(nfb[:, :], a["norm_f"].rearrange("(o n) -> o n", o=1).to_broadcast([128, D])).then_inc(late_in, 16)

            pool.wait_ge(merged_ready, KD)
            pool.memset(xps[:, :], 0.0).then_inc(parts_zero, 1)
            for part in range(2):
                for t, n in enumerate(ROWS):
                    pool.wait_ge(part_ready, 3 * part + t + 1)
                    src = xn2[0:n, t, :] if part == 0 else rest[t][0:n, :]
                    is_part = xp[:, part, t, :] if t < 2 else sample_part[0:n, part, :]
                    if part == 0:
                        dst = rest[t][0:n, :]
                    else:
                        dst = xp[:, 2, t, :] if t < 2 else sample_part[0:n, 2, :]
                        pool.wait_ge(rest_ready, t + 1)
                    pool.tensor_tensor(dst, src, is_part, ALU.subtract).then_inc(rest_ready, 1)

            pool.wait_ge(routed, 2)
            pool.wait_ge(rounds_ready, 1)
            rounds = pool.value_load(rounds_i[0:1, 0:1], min_val=1, max_val=MAX_ROUNDS)
            with pool.Fori(0, rounds) as r:
                with pool.Fori(0, PAIRS) as pair:
                    it = r * PAIRS + pair
                    e = 2 * pair
                    pool.wait_ge(P_ready, 2 * it + PRIMED)
                    pool.tensor_copy(rgc[:, :, :, :], rg[:, :, :, bass.ds(e, 2)]).then_inc(cols_ready, 1)
                    pool.wait_ge(up_done, 2 * it + PRIMED)
                    pool.tensor_copy(pick[:, :, :],
                                     cst[:, bass.ds(e + C_PICK, 2)].rearrange("p (e o) -> p e o", o=1)
                                     .to_broadcast([128, 2, SLOTS])).then_inc(pick_ready, 1)
                pool.wait_ge(cols_ready, PAIRS * (r + 1))
                pool.tensor_tensor(rg[:, 0, :, :], rg[:, 0, :, :],
                                   cst[:, C_THR + 1:C_THR + 2].rearrange("p (a o) -> p a o", a=1).to_broadcast([128, TT, E]),
                                   ALU.subtract).then_inc(round_done, 1)
                pool.wait_ge(round_done, r + 1)

        @block.scalar
        def _(ac):
            ac.sem_inc(actT_ready, PRIMED)
            ac.dma_start(prow[R_STATE:R_STATE + 2 * NS, :], a["state_conv"][0].rearrange("b w d -> (b w) d")).then_inc(prow_in, 16)
            ac.dma_start(prow[R_CONV:R_CONV + 3, :], a["conv_w"][0]).then_inc(prow_in, 16)
            ac.dma_start(prow[R_NORM:R_NORM + 1, :], a["norm1"]).then_inc(prow_in, 16)
            ac.dma_start(router[:, :, :], a["w_router"][0].rearrange("(k p) e -> p k e", p=128)).then_inc(prow_in, 16)
            ac.dma_start(router_b[:, :], a["b_router"].to_broadcast([128, E])).then_inc(prow_in, 16)
            ac.dma_start(o["conv_sample"][0, :, 0, :], a["state_conv"][0, :, 1, :]).then_inc(row0_out, 16)
            ac.wait_ge(x_in, 32)
            ac.wait_ge(const_set, 6)
            for t, n in enumerate(ROWS):
                ac.activation(squares_out[0:n, t, :], hx[0:n, t, :], ACT.Square, accum_out=stat[0:n, t:t + 1]).then_inc(sumsq, 1)
            ac.wait_ge(mean1, 1)
            ac.activation(stat[:, 6:9], stat[:, 3:6], ACT.Sqrt).then_inc(root1, 1)

            ac.wait_ge(emptied[4], plan["par"][1])
            for k in range(1, KD, 2):
                name = ("xT", k)
                ins = ac.activation(xnT[:, k, :], read(ac, name)[:, 0:T], ACT.Copy, scale=par[:, k, R_NORM:R_NORM + 1])
                empties(ins, name)

            for event in order:
                what, *which = event
                if what == "prep":
                    n = which[0]
                    ac.wait_ge(S_in[n % 3], 16 * (n // 3 + 1))
                    ac.activation(S[n % 3], S[n % 3], ACT.Copy, scale=gamma(n // NS)).then_inc(S_scaled, 1)
                    continue
                h = which[0]
                if what == "v":
                    t = which[1]
                    bank = read(ac, event)
                    if t < 2:
                        if t == 0 and h >= 1:
                            was_filled(ac, ("st", h - 1, 1))
                        empties(ac.activation(v_sb[:, t, :], bank[:, :], ACT.Copy), event)
                    else:
                        if h >= 1:
                            ac.wait_ge(vs_out[(h - 1) % 2], 64 * ((h - 1) // 2 + 1))
                        empties(ac.activation(vs_sb[:, :], bank[:, 0:128], ACT.Copy), event)
                elif what == "vs":
                    was_read(ac, ("v", h, 2))
                    for j in range(NV):
                        ac.dma_start(v_dram[h, :, 128 * j:128 * (j + 1)], vs_sb[32 * j:32 * j + NS, :]).then_inc(vs_out[h % 2], 16)
                elif what == "kt":
                    bank = read(ac, event)
                    for t in range(2):
                        ins = ac.activation(ktok[:, t, :], bank[:, DK * t:DK * (t + 1)], ACT.Copy,
                                            scale=cst[:, C_KDEC + 2 * h + t:C_KDEC + 2 * h + t + 1])
                    empties(ins, event)
                elif what == "out":
                    for g in range(2):
                        use = ("out", h, g)
                        bank = read(ac, use)
                        empties(ac.activation(rT[:, NV * h + 2 * g:NV * h + 2 * g + 2, 0:LP],
                                              bank[:, :].rearrange("p (a q) -> p a q", a=2), ACT.Copy), use)
                elif what == "st":
                    for g in range(2):
                        use = ("st", h, g)
                        bank = read(ac, use)
                        if g == 0 and h >= 1:
                            ac.wait_ge(st_out, 16 * h)
                        empties(ac.activation(st[:, g, :], bank[:, :], ACT.Copy), use)
                    for g in range(2):
                        was_read(ac, ("st", h, g))
                    ac.dma_start(o["ret_prompt"][0, 0, h].rearrange("(k p) v -> p k v", p=128), st[:, :, :]).then_inc(st_out, 16)
                elif what == "sqr":
                    was_read(ac, ("rsT", h))
                    for g in range(2):
                        was_read(ac, ("out", h, g))
                    if h >= 1:
                        was_filled(ac, ("ss", h - 1))
                    ac.activation(sq[:, :, :], rT[:, NV * h:NV * (h + 1), :], ACT.Square).then_inc(sq_ready, 1)
                elif what == "ss":
                    bank = read(ac, event)
                    if h >= 1:
                        ac.wait_ge(rT_ready, h)
                    empties(ac.activation(rinv[:, :], bank[:, 0:T], ACT.Sqrt, scale=1.0 / DV, bias=stat[:, 15:16]), event)
                elif what == "ct":
                    bank = read(ac, event)
                    if h == 0:
                        ac.wait_ge(st_out, 16 * H)
                    empties(ac.activation(ctok[0:NS + 2, 512 * h:512 * (h + 1)], bank[0:NS + 2, :], ACT.Copy), event)
                    if h == 1:
                        for g in range(2):
                            was_read(ac, ("ct", g))
                        ac.dma_start(o["conv_prompt"][0, 0], ctok[0:2, :]).then_inc(ctok_out, 16)
                        ac.dma_start(o["conv_sample"][0, :, 1, :], ctok[2:2 + NS, :]).then_inc(ctok_out, 16)
                elif what == "proj":
                    (name, g), j = which
                    if name == "g":
                        bank = read(ac, event)
                        if j == 0 and g >= 2:
                            ac.wait_ge(rT_ready, g - 1)
                        ac.activation(sg[:, g % 2, j, :], bank[:, 0:T], ACT.Sigmoid).then_inc(gate_sig, 1)
                    elif name == "cc":
                        bank = read(ac, event)
                        if g == 1:
                            was_read(ac, ("proj", ("ch", 0), j))
                        empties(ac.activation(cc[:, j, :], bank[:, 0:T], ACT.Copy), event)
                    elif name in ("ga", "gb"):
                        bank = read(ac, event)
                        if name == "ga" and j == 0:
                            ac.wait_ge(rT_ready, H - 1 + g)
                        if (name, g, j) == ("gb", 0, 0):
                            was_filled(ac, ("proj", ("wa", 1), 3))
                        dst = (gas if name == "ga" else gbs)[:, 4 * g + j, :]
                        empties(ac.activation(dst, bank[:, 0:T], ACT.Sigmoid), event)
            use = ("wo", 2, 0)
            for t, n in enumerate(ROWS):
                if t == 2:
                    bank = read(ac, use)
                    for j in range(4):
                        ins = ac.activation(ws[0:NS, 256 * j:256 * (j + 1)], bank[32 * j:32 * j + NS, 0:256], ACT.Copy)
                    empties(ins, use)
                    ac.wait_ge(h_decode, 1)
                else:
                    for c in range(2):
                        was_read(ac, ("wo", t, c))
                ac.activation(squares2[t][0:n, :], hx[0:n, t, :], ACT.Square, accum_out=stat[0:n, t:t + 1]).then_inc(sumsq2, 1)
                ac.wait_ge(mean2, t + 1)
                ac.activation(stat[:, 6 + t:7 + t], stat[:, 3 + t:4 + t], ACT.Sqrt).then_inc(root2, 1)
            ac.wait_ge(parts_zero, 1)
            for part in range(2):
                for t, n in enumerate(ROWS):
                    if part == 0:
                        ac.wait_ge(xn2_ready, t + 1)
                    else:
                        ac.wait_ge(rest_ready, t + 1)
                    dst = xp[:, part, t, :] if t < 2 else sample_part[0:n, part, :]
                    ac.activation(dst, xn2[0:n, t, :] if part == 0 else rest[t][0:n, :], ACT.Copy).then_inc(part_ready, 1)
                    if part == 0 and t < 2:
                        use = ("x2T", t, 1)
                        bank = read(ac, use)
                        empties(ac.activation(xn2T[:, 4:8, 128 * t:128 * (t + 1)],
                                              bank[:, :].rearrange("p (k q) -> p k q", k=4), ACT.Copy), use)
            ac.wait_ge(below_max, 1)
            ac.activation(route[:, 3:6, :], route[:, 3:6, :], ACT.Exp).then_inc(gate_exp, 1)
            for part in range(3):
                if part == 0:
                    ac.wait_ge(rest_ready, 6)
                    ac.wait_ge(part_ready, 6)
                ac.activation(xps[32 * part:32 * part + NS, :], sample_part[0:NS, part, :], ACT.Copy).then_inc(xps_ready, 1)

            ac.wait_ge(rounds_ready, 1)
            rounds = ac.value_load(rounds_i[0:1, 0:1], min_val=1, max_val=MAX_ROUNDS)
            with ac.Fori(0, rounds) as r:
                with ac.Fori(0, PAIRS) as pair:
                    it = r * PAIRS + pair
                    ac.wait_ge(gathered, 2 * it + 1)
                    ac.activation(xgT[:, 0:4, :], psum[6][:, :].rearrange("p (k s) -> p k s", k=4), ACT.Copy).then_inc(xg_lo, 1)
                    ac.wait_ge(pg_turned, it + (1 + PRIMED))
                    ac.activation(pgT[:, :], psum[5][:, 0:T], ACT.Copy).then_inc(pgT_ready, 1)
                    for e in range(2):
                        ac.wait_ge(g_clip, 2 * it + e + 1)
                        ac.activation(sig[:, e, :], gcl[:, e, :], ACT.Sigmoid, scale=ALPHA).then_inc(sig_ready, 1)
                    for e in range(2):
                        ac.wait_ge(act_turned, 2 * it + e + 1)
                        ac.activation(actT[:, e, :], psum[5][:, :], ACT.Copy).then_inc(actT_ready, 1)
            for t, n in enumerate(ROWS):
                if t == 0:
                    ac.wait_ge(added, 6 * PAIRS * rounds + PRIMED)
                ac.activation(squares3[0:n, t, :], hx[0:n, t, :], ACT.Square,
                              accum_out=stat[0:n, t:t + 1]).then_inc(sumsq3, 1)
                ac.wait_ge(mean3, t + 1)
                ac.activation(stat[:, 6 + t:7 + t], stat[:, 3 + t:4 + t], ACT.Sqrt).then_inc(root3, 1)
            ac.wait_ge(row0_out, 16)
            ac.wait_ge(st_out, 16 * H)

        @block.vector
        def _(v):
            steps = [0]
            for primed in (P_ready, added, y_ready):
                v.sem_inc(primed, PRIMED)

            def own(ins):
                steps[0] += 1
                ins.then_inc(dve, 1)

            def settle():
                v.wait_ge(dve, steps[0])

            def split_bias():
                v.wait_ge(late_in, 64)
                v.wait_ge(b1_zero, 1)
                was_filled(v, ("proj", ("wa", 1), 3))
                v.wait_ge(ctok_out, 32)
                src = b1[0:E, :]
                for part in range(3):
                    own(v.tensor_copy(b1_part[0:E, :], src))
                    settle()
                    if part < 2:
                        own(v.tensor_tensor(b1_rest[0:E, :], src, b1_part[0:E, :], ALU.subtract))
                    own(v.tensor_copy(bp[32 * part:32 * part + E, :], b1_part[0:E, :]))
                    settle()
                    src = b1_rest[0:E, :]

            def mean_to(src, dst, out_sem):
                v.tensor_scalar(dst, src, 1.0 / D, EPS, ALU.mult, ALU.add).then_inc(out_sem, 1)

            empties(v.tensor_copy(par[:, :, :], read(v, "par")[:, 0:KD * N_PAR].rearrange("p (k n) -> p k n", k=KD)), "par")
            v.wait_ge(const_set, 6)
            own(v.memset(stat[:, 15:16], EPS))
            v.wait_ge(sumsq, 3)
            mean_to(stat[:, 0:3], stat[:, 3:6], mean1)
            v.wait_ge(root1, 1)
            own(v.reciprocal(stat[:, 9:12], stat[:, 6:9]))
            settle()
            for t, n in enumerate(ROWS):
                v.tensor_scalar(xn[0:n, t, :], hx[0:n, t, :], stat[0:n, 9 + t:10 + t], None, ALU.mult).then_inc(xn_ready, 1)
            v.wait_ge(emptied[4], plan["par"][1])
            for k in range(0, KD, 2):
                name = ("xT", k)
                ins = v.tensor_scalar(xnT[:, k, :], read(v, name)[:, 0:T], par[:, k, R_NORM:R_NORM + 1], None, ALU.mult)
                empties(ins, name)
            for k in range(KD - PROJ_BANKS, KD):
                was_read(v, ("xT", k))
            v.tensor_copy(xsT[:, :, 0:NS], xnT[:, :, LP:T]).then_inc(xsT_ready, 1)

            def rotate(event):
                _, (name, g), j = event
                dst, cs, sn = (qT, cos, sin) if name == "q" else (kT, cosk, sink)
                lo, hi = ("proj", (name, g), j - 1), event
                x1, x2 = read(v, lo)[:, 0:T], read(v, hi)[:, 0:T]
                own(v.tensor_tensor(rot[:, 0, :], x1, cs, ALU.mult))
                own(v.tensor_tensor(rot[:, 1, :], x2, sn, ALU.mult))
                empties(v.tensor_tensor(rot[:, 2, :], x1, sn, ALU.mult), lo)
                empties(v.tensor_tensor(rot[:, 3, :], x2, cs, ALU.mult), hi)
                settle()
                was_read(v, lo)
                was_read(v, hi)
                v.tensor_tensor(dst[:, j - 1, :], rot[:, 0, :], rot[:, 1, :], ALU.subtract).then_inc(qk_ready, 1)
                v.tensor_tensor(dst[:, j, :], rot[:, 2, :], rot[:, 3, :], ALU.add).then_inc(qk_ready, 1)
                qk[0] += 2
                v.wait_ge(qk_ready, qk[0])

            qk = [0]

            for event in order:
                what, *which = event
                if what == "prep":
                    n = which[0]
                    h, b = divmod(n, NS)
                    v.wait_ge(S_scaled, n + 1)
                    v.wait_ge(vb_in[n % 2], 16 * (n // 2 + 1))
                    own(v.scalar_tensor_tensor(S[n % 3][:, 0, :], vb[n % 2], ks[:, h % 2, b:b + 1],
                                               S[n % 3][:, 0, :], ALU.mult, ALU.add))
                    v.scalar_tensor_tensor(S[n % 3][:, 1, :], vb[n % 2], ks[:, h % 2, NS + b:NS + b + 1],
                                           S[n % 3][:, 1, :], ALU.mult, ALU.add).then_inc(S_new, 1)
                elif what == "step" and which[0] % NS == NS - 1:
                    h = which[0] // NS
                    empties(v.tensor_copy(rs_t[:, :], read(v, ("rs", h))[:, 0:128]), ("rs", h))
                elif what == "rsT":
                    h = which[0]
                    bank = read(v, event)
                    empties(v.tensor_copy(rT[:, NV * h:NV * (h + 1), LP:T],
                                          bank[:, 0:128].rearrange("p (j s) -> p j s", j=NV)[:, :, 0:NS]), event)
                elif what == "ss":
                    h = which[0]
                    was_read(v, event)
                    own(v.reciprocal(rinv[:, :], rinv[:, :]))
                    settle()
                    for j in range(NV):
                        own(v.tensor_tensor(sg[:, h % 2, j, :], sg[:, h % 2, j, :], rinv[:, :], ALU.mult))
                    settle()
                    for j in range(NV):
                        ins = v.tensor_tensor(rT[:, NV * h + j, :], rT[:, NV * h + j, :], sg[:, h % 2, j, :], ALU.mult)
                    ins.then_inc(rT_ready, 1)
                elif what == "qs":
                    h = which[0]
                    if h >= 2:
                        was_filled(v, ("rs", h - 2))
                    for half in range(2):
                        own(v.tensor_copy(qsm[:, h % 2, half, 0:33 * (NS - 1) + 1:33], qT[:, 2 * (h % 2) + half, LP:T]))
                        v.tensor_copy(ks[:, h % 2, NS * half:NS * (half + 1)], kT[:, 2 * (h % 2) + half, LP:T])\
                            .then_inc(qs_ready, 1)
                    v.wait_ge(qs_ready, 2 * (h + 1))
                    settle()
                elif what == "sc":
                    h = which[0]
                    bank = read(v, event)
                    own(v.tensor_tensor(sc[:, 0:LP], bank[:, 0:LP], mask(h, LP), ALU.mult))
                    empties(v.tensor_tensor(sc[:, LP:384], bank[:, LP:384], mask(h, 128), ALU.mult), event)
                elif what == "taps":
                    g = which[0]

                    def tap(j, i):
                        return par[:, 4 * g + j, R_CONV + i:R_CONV + i + 1]

                    for j in range(4):
                        was_read(v, ("proj", ("ch", g), j))
                    settle()
                    old = par[:, 4 * g:4 * g + 4, R_STATE:R_STATE + 2 * NS].rearrange("p k (b w) -> p k w b", w=2)
                    for j in range(4):
                        own(v.tensor_scalar(cv[:, j, 0:LP], U[:, j, 0:LP], tap(j, 0), None, ALU.mult))
                        own(v.tensor_scalar(cv[:, j, LP:T], old[:, j, 0, :], tap(j, 0), None, ALU.mult))
                    settle()
                    for j in range(4):
                        own(v.scalar_tensor_tensor(cv[:, j, 0:LP], U[:, j, 1:LP + 1], tap(j, 1), cv[:, j, 0:LP], ALU.mult, ALU.add))
                        own(v.scalar_tensor_tensor(cv[:, j, LP:T], old[:, j, 1, :], tap(j, 1), cv[:, j, LP:T], ALU.mult, ALU.add))
                    settle()
                    for j in range(4):
                        own(v.scalar_tensor_tensor(cv[:, j, :], U[:, j, 2:T + 2], tap(j, 2), cv[:, j, :], ALU.mult, ALU.add))
                    settle()
                elif what == "proj":
                    (name, g), j = which
                    if name in ("q", "k"):
                        if (name, g, j) == ("q", 1, 0):
                            was_filled(v, ("sc", 1))
                            was_filled(v, ("kt", 1))
                        if j % 2 == 1:
                            rotate(event)
                    elif name == "g":
                        v.wait_ge(gate_sig, 4 * g + j + 1)
                        bank = psum[plan[event][0]]
                        empties(v.tensor_tensor(sg[:, g % 2, j, :], sg[:, g % 2, j, :], bank[:, 0:T], ALU.mult), event)
                        if j == 3:
                            for i in range(4):
                                was_read(v, ("proj", (name, g), i))
                    elif name == "ch":
                        bank = read(v, event)
                        was_read(v, ("proj", ("cc", g), j))
                        if (g, j) == (0, 0):
                            was_filled(v, ("st", H - 1, 1))
                            own(v.memset(U[:, :, 0:2], 0.0))
                        if (g, j) == (1, 0):
                            was_filled(v, ("ct", 0))
                        empties(v.tensor_tensor(U[:, j, 2:T + 2], bank[:, 0:T], cc[:, j, :], ALU.mult), event)
                    elif name == "cb":
                        bank = read(v, event)
                        empties(v.tensor_tensor(aT[:, 4 * g + j, :], bank[:, 0:T], cv[:, j, :], ALU.mult), event)
                    elif name == "wa":
                        bank = read(v, event)
                        was_read(v, ("proj", ("ga", g), j))
                        empties(v.tensor_tensor(merged[:, 4 * g + j, :], gas[:, 4 * g + j, :], bank[:, 0:T], ALU.mult), event)
                        if (g, j) == (1, 3):
                            split_bias()
                    elif name == "wb":
                        bank = read(v, event)
                        was_read(v, ("proj", ("gb", g), j))
                        empties(v.tensor_tensor(gbs[:, 4 * g + j, :], gbs[:, 4 * g + j, :], bank[:, 0:T], ALU.mult), event)
                        was_read(v, event)
                        was_read(v, ("proj", ("wa", g), j))
                        v.tensor_tensor(merged[:, 4 * g + j, :], merged[:, 4 * g + j, :], gbs[:, 4 * g + j, :], ALU.add)\
                            .then_inc(merged_ready, 1)
            for t, n in enumerate(ROWS):
                if t < 2:
                    for c in range(2):
                        bank = read(v, ("wo", t, c))
                        empties(v.tensor_tensor(hx[0:n, t, 512 * c:512 * (c + 1)], hx[0:n, t, 512 * c:512 * (c + 1)],
                                                bank[0:n, :], ALU.add), ("wo", t, c))
                else:
                    was_read(v, ("wo", 2, 0))
                    v.tensor_tensor(hx[0:n, t, :], hx[0:n, t, :], ws[0:n, :], ALU.add).then_inc(h_decode, 1)
                if t == 0:
                    v.wait_ge(late_in, 64)
                v.wait_ge(sumsq2, t + 1)
                mean_to(stat[:, t:t + 1], stat[:, 3 + t:4 + t], mean2)
                v.wait_ge(root2, t + 1)
                own(v.reciprocal(stat[:, 9 + t:10 + t], stat[:, 6 + t:7 + t]))
                settle()
                v.scalar_tensor_tensor(xn2[0:n, t, :], hx[0:n, t, :], stat[0:n, 9 + t:10 + t], n2b[0:n, :],
                                       ALU.mult, ALU.mult).then_inc(xn2_ready, 1)
            own(v.memset(route[:, :, :], 0.0))
            for t in range(2):
                use = ("x2T", t, 0)
                empties(v.tensor_copy(xn2T[:, 0:4, 128 * t:128 * (t + 1)],
                                      read(v, use)[:, :].rearrange("p (k q) -> p k q", k=4)), use)
            use = ("x2T", 2, 0)
            empties(v.tensor_copy(xn2T[:, :, LP:T], read(v, use)[:, 0:KD * NS].rearrange("p (k q) -> p k q", k=KD)), use)
            settle()
            L, ex, gt, eq, ceq, sel = (route[:, 3 * i:3 * i + 3, :] for i in range(6))
            top8 = route[:, 18, 0:8 * TT].rearrange("p (t i) -> p t i", t=TT)
            count, need, total, inv = (route[:, 19, 3 * i:3 * i + 3].rearrange("p (t o) -> p t o", o=1) for i in range(4))

            def wide(x):
                return x.to_broadcast([128, TT, E])

            bank = read(v, "logits")
            for t, n in enumerate(ROWS):
                ins = v.tensor_tensor(L[0:n, t, :], bank[0:n, E * t:E * (t + 1)], router_b[0:n, :], ALU.add)
                if t == 2:
                    empties(ins, "logits")
                else:
                    own(ins)
            was_read(v, "logits")
            settle()
            for t in range(TT):
                own(v.max(top8[:, t, :], L[:, t, :]))
            settle()
            v.tensor_tensor(ex, L, wide(top8[:, :, 0:1]), ALU.subtract).then_inc(below_max, 1)
            own(v.tensor_tensor(gt, L, wide(top8[:, :, TOP - 1:TOP]), ALU.is_gt))
            own(v.tensor_tensor(eq, L, wide(top8[:, :, TOP - 1:TOP]), ALU.is_equal))
            settle()
            own(v.reduce_sum(count, gt, AX.X))
            for t in range(TT):
                own(v.tensor_tensor_scan(ceq[:, t, :], ones[:, 0:E], eq[:, t, :], 0.0, ALU.mult, ALU.add))
            settle()
            own(v.tensor_scalar(need, count, -1.0, float(TOP), ALU.mult, ALU.add))
            settle()
            own(v.tensor_tensor(ceq, ceq, wide(need), ALU.is_le))
            settle()
            own(v.tensor_tensor(ceq, ceq, eq, ALU.mult))
            settle()
            v.tensor_tensor(sel, gt, ceq, ALU.add).then_inc(selected, 1)
            v.wait_ge(selected, 1)
            v.wait_ge(gate_exp, 1)
            own(v.tensor_tensor(ex, ex, sel, ALU.mult))
            settle()
            own(v.reduce_sum(total, ex, AX.X))
            settle()
            own(v.reciprocal(inv, total))
            settle()
            own(v.tensor_tensor(rg[:, 1, 0:2, :], ex[:, 0:2, :], inv[:, 0:2, :].to_broadcast([128, 2, E]), ALU.mult))
            own(v.tensor_scalar(rg[0:NS, 1, 2, :], ex[0:NS, 2, :], inv[0:NS, 2, :], None, ALU.mult))
            bank = read(v, "rank")
            for t, n in enumerate(ROWS):
                ins = v.scalar_tensor_tensor(rg[0:n, 0, t, :], bank[0:n, E * t:E * (t + 1)], NOT_ROUTED, sel[0:n, t, :],
                                             ALU.add, ALU.mult)
                if t == 2:
                    empties(ins, "rank")
                else:
                    own(ins)
            was_read(v, "rank")
            settle()
            for t, n in enumerate(ROWS):
                own(v.tensor_scalar(rg[0:n, 0, t, :], rg[0:n, 0, t, :], -NOT_ROUTED, None, ALU.add))
            settle()
            v.tensor_copy(rg[32:32 + NS, 0, 2, :], rg[0:NS, 0, 2, :]).then_inc(routed, 1)
            v.tensor_copy(rg[64:64 + NS, 0, 2, :], rg[0:NS, 0, 2, :]).then_inc(routed, 1)
            bank = read(v, "count")
            empties(v.reduce_max(route[:, 19, 12:13], bank[:, 0:E], AX.X), "count")
            was_read(v, "count")
            own(v.tensor_scalar(route[:, 19, 16:16 + MAX_ROUNDS], cst[:, C_THR:C_THR + MAX_ROUNDS], route[:, 19, 12:13], None, ALU.is_lt))
            settle()
            own(v.reduce_sum(route[:, 19, 13:14], route[:, 19, 16:16 + MAX_ROUNDS], AX.X))
            settle()
            v.tensor_copy(rounds_i[:, :], route[:, 19, 13:14]).then_inc(rounds_ready, 1)
            v.tensor_copy(gT[0:E, :], read(v, "gT")[0:E, 0:T]).then_inc(gT_ready, 1)
            for t, n in enumerate(ROWS):
                for c in range(2):
                    name = ("b2", t, c)
                    bank = read(v, name)
                    empties(v.tensor_tensor(hx[0:n, t, 512 * c:512 * (c + 1)], hx[0:n, t, 512 * c:512 * (c + 1)],
                                            bank[0:n, :], ALU.add), name)
            for b in range(4):
                v.wait_ge(emptied[b], uses[b])

            v.wait_ge(rounds_ready, 1)
            rounds = v.value_load(rounds_i[0:1, 0:1], min_val=1, max_val=MAX_ROUNDS)
            slots = slot_no.rearrange("p (o s) -> p o s", o=1).to_broadcast([128, 2 * TT, SLOTS])

            def per_slot(n):
                return rgc[:, n, :, :].rearrange("p t (e o) -> p (t e) o", o=1).to_broadcast([128, 2 * TT, SLOTS])

            with v.Fori(0, rounds) as r:
                with v.Fori(0, PAIRS) as pair:
                    it = r * PAIRS + pair
                    v.wait_ge(cols_ready, it + 1)
                    v.wait_ge(pg_turned, it + PRIMED)
                    v.tensor_tensor(P, slots, per_slot(0), ALU.is_equal).then_inc(P_ready, 1)
                    v.wait_ge(P_ready, 2 * it + (1 + PRIMED))
                    v.tensor_tensor(Pg, P, per_slot(1), ALU.mult).then_inc(P_ready, 1)
                    v.wait_ge(gathered, 2 * it + 2)
                    v.tensor_copy(xgT[:, 4:8, :], psum[7][:, :].rearrange("p (k s) -> p k s", k=4)).then_inc(xg_hi, 1)
                    for e in range(2):
                        v.wait_ge(up_done, 2 * it + (e + 1 + PRIMED))
                        v.tensor_scalar(gcl[:, e, :], psum[2 * e][:, :], LIMIT, None, ALU.min).then_inc(g_clip, 1)
                        v.tensor_scalar(ucl[:, e, :], psum[2 * e + 1][:, :], LIMIT, -LIMIT, ALU.min, ALU.max).then_inc(u_clip, 1)
                        v.wait_ge(g_clip, 2 * it + e + 1)
                        v.wait_ge(u_clip, 2 * it + e + 1)
                        v.scalar_tensor_tensor(ucl[:, e, :], ucl[:, e, :], 1.0, gcl[:, e, :], ALU.add, ALU.mult)\
                            .then_inc(ug_ready, 1)
                        v.wait_ge(ug_ready, 2 * it + e + 1)
                        v.wait_ge(sig_ready, 2 * it + e + 1)
                        v.tensor_tensor(acts[:, e, :], ucl[:, e, :], sig[:, e, :], ALU.mult).then_inc(act_ready, 1)
                    for e in range(2):
                        v.wait_ge(down_done, 2 * it + e + 1)
                        v.tensor_copy(ysb[SLOTS * e:SLOTS * (e + 1), 0:512], psum[4][0:64, :]).then_inc(y_ready, 1)
                        v.tensor_copy(ysb[SLOTS * e:SLOTS * (e + 1), 512:1024], psum[4][64:128, :]).then_inc(y_ready, 1)
                    for t, n in enumerate(ROWS):
                        for c in range(2):
                            v.wait_ge(combined, 6 * it + 2 * t + c + 1)
                            v.tensor_tensor(hx[0:n, t, 512 * c:512 * (c + 1)], hx[0:n, t, 512 * c:512 * (c + 1)],
                                            psum[6 + c][0:n, :], ALU.add).then_inc(added, 1)
                    v.wait_ge(added, 6 * it + (6 + PRIMED))
            for t, n in enumerate(ROWS):
                v.wait_ge(sumsq3, t + 1)
                mean_to(stat[:, t:t + 1], stat[:, 3 + t:4 + t], mean3)
                v.wait_ge(root3, t + 1)
                own(v.reciprocal(stat[:, 9 + t:10 + t], stat[:, 6 + t:7 + t]))
                settle()
                v.scalar_tensor_tensor(hx[0:n, t, :], hx[0:n, t, :], stat[0:n, 9 + t:10 + t], nfb[0:n, :],
                                       ALU.mult, ALU.mult).then_inc(y_scaled, 1)

        @block.tensor
        def _(pe):
            at = [0]
            for primed in (pg_turned, up_done):
                pe.sem_inc(primed, PRIMED)

            def chunk_ready(n):
                pe.wait_ge(chunk[n % RING], 16 * (n // RING + 1))

            def weight(n, k):
                return ring[:, n % RING, 512 * k:512 * (k + 1)]

            first = {}

            def chunks_of(name, groups=1):
                if name not in first:
                    first[name] = at[0]
                    at[0] += 2 * groups
                    for n in range(2 * groups):
                        chunk_ready(first[name] + n)
                return first[name]

            def project(event):
                _, name, j = event
                rhs, groups = {"wa": (aT, 1), "wb": (rT, 2)}.get(name[0], (xnT, 1))
                n = chunks_of(name, groups)
                bank = fill(pe, event)
                for k in range(KD * groups):
                    ins = pe.matmul(bank[:, 0:T], weight(n + k // 4, k % 4)[:, 128 * j:128 * (j + 1)], rhs[:, k, :],
                                    start=k == 0, stop=k == KD * groups - 1)
                fills(ins, event)

            pe.wait_ge(cst_in, 16)
            pe.wait_ge(prow_in, 80)
            bank = fill(pe, "par")
            for k in range(KD):
                ins = pe.transpose(bank[:, N_PAR * k:N_PAR * (k + 1)], prow[0:N_PAR, 128 * k:128 * (k + 1)],
                                   ident[0:N_PAR, 0:N_PAR])
            fills(ins, "par")
            pe.wait_ge(xn_ready, 3)
            for k in range(KD):
                name = ("xT", k)
                bank = fill(pe, name)
                for t, n in enumerate(ROWS):
                    ins = pe.transpose(bank[:, 128 * t:128 * t + n], xn[0:n, t, 128 * k:128 * (k + 1)], ident[0:n, 0:n])
                fills(ins, name)
            pe.wait_ge(xsT_ready, 1)
            for event in order:
                what, *which = event
                if what == "proj":
                    name, j = which
                    if (name, j) == (("wa", 0), 0):
                        for i in range(1, 4):
                            was_read(pe, ("proj", ("cb", 1), i))
                    if (name, j) == (("wb", 0), 0):
                        pe.wait_ge(rT_ready, H)
                    project(event)
                elif what == "v":
                    h, t = which
                    n = chunks_of(("v", h))
                    bank = fill(pe, event)
                    for k in range(KD):
                        w = weight(n + k // 4, k % 4)
                        if t < 2:
                            ins = pe.matmul(bank[:, :], xnT[:, k, 128 * t:128 * (t + 1)], w, start=k == 0, stop=k == KD - 1)
                        else:
                            for j in range(4):
                                ins = pe.matmul(bank[32 * j:32 * (j + 1), 0:128], xsT[:, k, :], w[:, 128 * j:128 * (j + 1)],
                                                start=k == 0, stop=k == KD - 1)
                    fills(ins, event)
                elif what == "kt":
                    h = which[0]
                    hh = 2 * (h % 2)
                    pe.wait_ge(qk_ready, 8 * (h // 2 + 1))
                    bank = fill(pe, event)
                    for t in range(2):
                        for half in range(2):
                            ins = pe.transpose(bank[:, DK * t + 128 * half:DK * t + 128 * (half + 1)],
                                               kT[:, hh + half, 128 * t:128 * (t + 1)], ident)
                    fills(ins, event)
                elif what == "sc":
                    hh = 2 * (which[0] % 2)
                    bank = fill(pe, event)
                    for half in range(2):
                        pe.matmul(bank[:, 0:LP], kT[:, hh + half, 0:128], qT[:, hh + half, 0:LP], start=half == 0, stop=half == 1)
                    for half in range(2):
                        ins = pe.matmul(bank[:, LP:384], kT[:, hh + half, 128:256], qT[:, hh + half, 128:256],
                                        start=half == 0, stop=half == 1)
                    fills(ins, event)
                elif what == "out":
                    h = which[0]
                    was_read(pe, ("sc", h))
                    for t in range(2):
                        was_read(pe, ("v", h, t))
                    for g in range(2):
                        bank = fill(pe, ("out", h, g))
                        for j in range(2):
                            dv = 128 * (2 * g + j)
                            pe.matmul(bank[:, LP * j:LP * (j + 1)], v_sb[:, 0, dv:dv + 128], sc[:, 0:LP], start=True, stop=False)
                            ins = pe.matmul(bank[:, LP * j + 128:LP * (j + 1)], v_sb[:, 1, dv:dv + 128], sc[:, LP:384],
                                            start=False, stop=True)
                        fills(ins, ("out", h, g))
                elif what == "st":
                    h = which[0]
                    was_read(pe, ("kt", h))
                    for g in range(2):
                        bank = fill(pe, ("st", h, g))
                        for t in range(2):
                            ins = pe.matmul(bank[:, :], ktok[:, t, 128 * g:128 * (g + 1)], v_sb[:, t, :], start=t == 0, stop=t == 1)
                        fills(ins, ("st", h, g))
                elif what == "step":
                    n = which[0]
                    h, b = divmod(n, NS)
                    use = ("rs", h)
                    bank = fill(pe, use) if b == 0 else psum[RS_BANK]
                    pe.wait_ge(S_new, n + 1)
                    for half in range(2):
                        for j in range(NV):
                            ins = pe.matmul(bank[32 * j:32 * (j + 1), 0:128], qsm[:, h % 2, half, 32 * b:32 * (b + 1)],
                                            S[n % 3][:, half, 128 * j:128 * (j + 1)],
                                            start=b == 0 and half == 0, stop=b == NS - 1 and half == 1)
                    if b < NS - 1:
                        ins.then_inc(S_read, 1)
                    else:
                        fills(ins, use)
                elif what == "rsT":
                    h = which[0]
                    bank = fill(pe, event)
                    was_read(pe, ("rs", h))
                    fills(pe.transpose(bank[:, 0:128], rs_t[:, :], ident), event)
                elif what == "ss":
                    h = which[0]
                    bank = fill(pe, event)
                    pe.wait_ge(sq_ready, h + 1)
                    for j in range(NV):
                        ins = pe.matmul(bank[:, 0:T], ones[:, :], sq[:, j, :], start=j == 0, stop=j == NV - 1)
                    fills(ins, event)
                elif what == "ct":
                    g = which[0]
                    bank = fill(pe, event)
                    for j in range(4):
                        was_read(pe, ("proj", ("ch", g), j))
                    for j in range(4):
                        ins = pe.transpose(bank[0:NS + 2, 128 * j:128 * (j + 1)], U[:, j, LP:T + 2], ident)
                    fills(ins, event)
            pe.wait_ge(merged_ready, KD)
            n = chunks_of("wo", 2)
            assert at[0] == MIXER_CHUNKS
            for t in range(2):
                for c in range(2):
                    bank = fill(pe, ("wo", t, c))
                    for k in range(KD):
                        ins = pe.matmul(bank[:, :], merged[:, k, 128 * t:128 * (t + 1)], weight(n + 2 * c + k // 4, k % 4),
                                        start=k == 0, stop=k == KD - 1)
                    fills(ins, ("wo", t, c))
            bank = fill(pe, ("wo", 2, 0))
            for k in range(KD):
                for j in range(4):
                    w = weight(n + 2 * (j // 2) + k // 4, k % 4)[:, 256 * (j % 2):256 * (j % 2 + 1)]
                    ins = pe.matmul(bank[32 * j:32 * j + NS, 0:256], merged[:, k, LP:T], w, start=k == 0, stop=k == KD - 1)
            fills(ins, ("wo", 2, 0))
            for t, n in enumerate(ROWS):
                pe.wait_ge(xn2_ready, t + 1)
                for g in range(2 if t < 2 else 1):
                    use = ("x2T", t, g)
                    bank = fill(pe, use)
                    for i in range(4 if t < 2 else KD):
                        k = 4 * g + i
                        ins = pe.transpose(bank[:, n * i:n * (i + 1)], xn2[0:n, t, 128 * k:128 * (k + 1)], ident[0:n, 0:n])
                    fills(ins, use)
            bank = fill(pe, "logits")
            for t, n in enumerate(ROWS):
                for g in range(2 if t < 2 else 1):
                    was_read(pe, ("x2T", t, g))
                for k in range(KD):
                    ins = pe.matmul(bank[0:n, E * t:E * (t + 1)], xn2T[:, k, 128 * t:128 * t + n], router[:, k, :],
                                    start=k == 0, stop=k == KD - 1)
            fills(ins, "logits")
            pe.wait_ge(selected, 1)
            bank = fill(pe, "rank")
            for t, n in enumerate(ROWS):
                for s in range(t + 1):
                    ins = pe.matmul(bank[0:n, E * t:E * (t + 1)], (tri if s == t else ones)[0:ROWS[s], 0:n],
                                    route[0:ROWS[s], 15 + s, :], start=s == 0, stop=s == t)
            fills(ins, "rank")
            bank = fill(pe, "count")
            for s in range(TT):
                ins = pe.matmul(bank[:, 0:E], ones[0:ROWS[s], :], route[0:ROWS[s], 15 + s, :], start=s == 0, stop=s == TT - 1)
            fills(ins, "count")
            pe.wait_ge(routed, 2)
            bank = fill(pe, "gT")
            for t, n in enumerate(ROWS):
                ins = pe.transpose(bank[0:E, 128 * t:128 * t + n], rg[0:n, 1, t, :], ident[0:n, 0:n])
            fills(ins, "gT")
            pe.wait_ge(gT_ready, 1)
            pe.wait_ge(late_in, 64)
            for t, n in enumerate(ROWS):
                for c in range(2):
                    bank = fill(pe, ("b2", t, c))
                    fills(pe.matmul(bank[0:n, :], gT[0:E, 128 * t:128 * t + n], b2[0:E, 512 * c:512 * (c + 1)],
                                    start=True, stop=True), ("b2", t, c))
            for b in range(4):
                pe.wait_ge(emptied[b], uses[b])

            rounds_at = rounds_i[0:1, 0:1]
            pe.wait_ge(rounds_ready, 1)
            rounds = pe.value_load(rounds_at, min_val=1, max_val=MAX_ROUNDS)
            uses_before = MIXER_CHUNKS // RING
            pe.wait_ge(xps_ready, 3)
            pe.wait_ge(rest_ready, 6)
            with pe.Fori(0, rounds) as r:
                with pe.Fori(0, PAIRS) as pair:
                    it = r * PAIRS + pair

                    def slot_ready(n):
                        pe.wait_ge(chunk[n % RING], 32 * it + 16 * (uses_before + n // RING + 1))

                    pe.wait_ge(P_ready, 2 * it + (2 + PRIMED))
                    pe.wait_ge(added, 6 * it + PRIMED)
                    for half in range(2):
                        for k in range(4 * half, 4 * half + 4):
                            out = psum[6 + half][:, 128 * (k % 4):128 * (k % 4 + 1)]
                            for t in range(2):
                                for part in range(3):
                                    pe.matmul(out, xp[:, part, t, 128 * k:128 * (k + 1)], P[:, 2 * t:2 * t + 2, :],
                                              start=t == 0 and part == 0, stop=False)
                            ins = pe.matmul(out, xps[:, 128 * k:128 * (k + 1)], P[:, 4:6, :], start=False, stop=True)
                        ins.then_inc(gathered, 1)
                    pe.wait_ge(actT_ready, 2 * it + PRIMED)
                    for t, n in enumerate(ROWS):
                        ins = pe.transpose(psum[5][:, 128 * t:128 * t + n],
                                           Pg[0:n, 2 * t:2 * t + 2, :].rearrange("p e s -> p (e s)"), ident[0:n, 0:n])
                    ins.then_inc(pg_turned, 1)
                    pe.wait_ge(pick_ready, it + 1)
                    for e in range(2):
                        if e == 0:
                            pe.wait_ge(xg_lo, it + 1)
                            pe.wait_ge(xg_hi, it + 1)
                        for k in range(-1, KD):
                            if k >= 0:
                                slot_ready(KD * e + k)
                            for q in range(2):
                                for half in range(2):
                                    out = psum[2 * e + q][64 * half:64 * (half + 1), :]
                                    c = D * q + 512 * half
                                    if k < 0:
                                        pe.matmul(out, pick[:, e, :], bp[:, c:c + 512], start=True, stop=False)
                                    else:
                                        ins = pe.matmul(out, xgT[:, k, 64 * e:64 * (e + 1)],
                                                        ring[:, (KD * e + k) % RING, c:c + 512], start=False, stop=k == KD - 1)
                            if k >= 0:
                                ins.then_inc(up_done if k == KD - 1 else chunk_used, 1)
                    for e in range(2):
                        pe.wait_ge(act_ready, 2 * it + e + 1)
                        if e == 0:
                            pe.wait_ge(pgT_ready, it + 1)
                        else:
                            pe.wait_ge(actT_ready, 2 * it + (e + PRIMED))
                        for k in range(4):
                            ins = pe.transpose(psum[5][:, 128 * k:128 * (k + 1)], acts[:, e, 128 * k:128 * (k + 1)], ident)
                        ins.then_inc(act_turned, 1)
                        pe.wait_ge(actT_ready, 2 * it + (e + 1 + PRIMED))
                        pe.wait_ge(y_ready, 4 * it + (2 * e + PRIMED))
                        for f in range(KD):
                            n = 2 * KD + 4 * e + f // 2
                            if f % 2 == 0:
                                slot_ready(n)
                            lhs = actT[:, e, 128 * (f % 4) + 64 * (f // 4):128 * (f % 4) + 64 * (f // 4) + 64]
                            for half in range(2):
                                c = D * (f % 2) + 512 * half
                                ins = pe.matmul(psum[4][64 * half:64 * (half + 1), :], lhs, ring[:, n % RING, c:c + 512],
                                                start=f == 0, stop=f == KD - 1)
                            if f % 2 == 1:
                                ins.then_inc(down_done if f == KD - 1 else chunk_used, 1)
                    pe.wait_ge(y_ready, 4 * it + (4 + PRIMED))
                    for t, n in enumerate(ROWS):
                        for c in range(2):
                            if t:
                                pe.wait_ge(added, 6 * it + (2 * t + c - 1 + PRIMED))
                            pe.matmul(psum[6 + c][0:n, :], pgT[:, 128 * t:128 * t + n], ysb[:, 512 * c:512 * (c + 1)],
                                      start=True, stop=True).then_inc(combined, 1)


INPUTS = ["x_prompt", "x_sample", "state_conv", "state_ret", "norm1", "w_in", "conv_w", "w_a", "w_b", "w_o", "norm2",
          "w_router", "b_router", "w_e1", "b_e1", "w_e2", "b_e2", "norm_f"]
OUTPUTS = [("y_prompt", (1, LP, D)), ("y_sample", (NS, 1, D)), ("conv_prompt", (1, 1, 2, D)),
           ("ret_prompt", (1, 1, H, DK, DV)), ("conv_sample", (1, NS, 2, D)), ("ret_sample", (1, NS, H, DK, DV))]


def kernel(**inputs):
    import concourse.bacc as bacc
    from concourse.bass_utils import run_bass_kernel_spmd

    nc = bacc.Bacc("TRN2", target_bir_lowering=False, num_devices=1)
    arrays = {name: np.ascontiguousarray(inputs[name]) for name in INPUTS}
    arrays["tables"] = shape_constants()
    a = {n: nc.dram_tensor(f"in_{n}", x.shape, F32, kind="ExternalInput").ap() for n, x in arrays.items()}
    o = {n: nc.dram_tensor(f"out_{n}", s, F32, kind="ExternalOutput").ap() for n, s in OUTPUTS}
    build(nc, a, o)
    r = run_bass_kernel_spmd(nc, [{f"in_{n}": x for n, x in arrays.items()}], core_ids=[0])
    return tuple(r.results[0][f"out_{n}"] for n, _ in OUTPUTS)
```

```python
import concourse.bass as bass
from concourse import mybir
from contextlib import ExitStack
import numpy as np

F32 = mybir.dt.float32
BF16 = mybir.dt.bfloat16
I32 = mybir.dt.int32
ALU = mybir.AluOpType
ACT = mybir.ActivationFunctionType
AX = mybir.AxisListType

D = 1024
LP = 256
NS = 8
T = LP + NS
TT = 3
ROWS = (128, 128, NS)
KD = D // 128
H = 4
DK = D // H
DV = 2 * DK
NV = DV // 128
PAST = 2048
E = 32
TOP = 4
SLOTS = 64
PAIRS = E // 2
MAX_ROUNDS = -(-T // SLOTS)
ALPHA = 1.702
LIMIT = 7.0
EPS = 1e-5
PRIMED = 1
ADDED = 5
TILE_ORDER = (2, 0, 1)
SPLITS = ((0, 2, 0, D), (0, 0, 0, D), (1, 2, 0, D), (1, 0, 0, D),
          (0, 1, 0, D // 2), (0, 1, D // 2, D), (1, 1, 0, D // 2), (1, 1, D // 2, D))
RANKED = 4096.0

RING = 12
CH = 2048
MIXER_CHUNKS = 5 * RING
PAIR_CHUNKS = 2 * RING
COUNTED = PAIR_CHUNKS - 4

C_ID = 0
C_TRI = C_ID + 128
C_KDEC = C_TRI + 128
C_SLOT = C_KDEC + 2 * H
C_THR = C_SLOT + SLOTS
C_PICK = C_THR + MAX_ROUNDS
C_COS = C_PICK + E
C_SIN, C_COSK, C_SINK = C_COS + T, C_COS + 2 * T, C_COS + 3 * T
C_MASK = C_COS + 4 * T
N_CONST = C_MASK + H * LP
TABLE_PARTS = (0, C_COS, C_MASK, N_CONST)

W_CB, W_CC, W_CH, W_Q, W_K, W_V, W_G, W_GA, W_GB = (0, 1024, 2048, 3072, 4096, 5120, 7168, 9216, 10240)

R_STATE, R_CONV, R_NORM, R_NORM2, N_PAR = 0, 2 * NS, 2 * NS + 3, 2 * NS + 4, 2 * NS + 5


def gamma(h):
    return 1.0 - 2.0 ** (-5 - h)


def shape_constants():
    f = np.float32
    c = np.zeros((128, N_CONST), f)
    pos = np.concatenate([np.arange(LP), np.full(NS, PAST)]).astype(f)
    inv = f(10000.0) ** (-np.linspace(0.0, 1.0, 128, dtype=f))
    ang = (pos[None, :] * inv[:, None]).astype(f)
    c[:, C_COS:C_COS + T] = np.cos(ang)
    c[:, C_SIN:C_SIN + T] = np.sin(ang)
    c[:, C_COSK:C_COSK + T] = c[:, C_COS:C_COS + T] * f(DK ** -0.5)
    c[:, C_SINK:C_SINK + T] = c[:, C_SIN:C_SIN + T] * f(DK ** -0.5)
    p = np.arange(128)
    q = np.arange(LP)
    for h in range(H):
        d = q[None, :] - p[:, None]
        c[:, C_MASK + h * LP:C_MASK + (h + 1) * LP] = np.where(d >= 0, gamma(h) ** np.maximum(d, 0), 0.0)
        for t in range(2):
            c[:, C_KDEC + 2 * h + t] = gamma(h) ** (LP - 1 - (t * 128 + p)).astype(np.float64)
    c[:, C_ID:C_ID + 128] = np.eye(128)
    c[:, C_TRI:C_TRI + 128] = p[:, None] < p[None, :]
    c[:, C_SLOT:C_SLOT + SLOTS] = RANKED + np.arange(SLOTS)
    c[:, C_THR:C_THR + MAX_ROUNDS] = np.arange(MAX_ROUNDS) * SLOTS
    for part in range(3):
        c[32 * part:32 * part + E, C_PICK:C_PICK + E] = np.eye(E)
    return c


PROJ_BANKS = 3
RS_BANK, TURN_BANK, SUM_BANK = 3, 4, 5
DEFERRED = (2, 3)
STEP_EVERY = 6.5
VALUES_TO_STEP = 18.0


CONV_ORDER = (("cc", 0), ("ch", 0), ("cc", 1), ("cb", 0), ("ch", 1))


def mixer_order():
    main = []

    def proj(name, work=3.6):
        main.extend([(("proj", name, j), work) for j in range(4)])

    for h in range(H):
        if h % 2 == 0:
            proj(("q", h // 2))
            proj(("k", h // 2))
        main.extend([(("v", h, 2), 2.2), (("vs", h), 0.0), (("v", h, 0), 7.0), (("qs", h), 0.0), (("kt", h), 0.5),
                     (("sc", h), 1.4), (("v", h, 1), 7.0)])
        proj(("g", h))
        main.append((("out", h), 2.7))
        main.append((("save", h), 0.0) if h in DEFERRED else (("st", h), 3.6))
    for n, g in CONV_ORDER:
        proj((n, g))
        if n == "ch":
            main += [(("taps", g), 0.0), (("ct", g), 0.5)]
    proj(("ga", 0))
    proj(("cb", 1))
    order, ends = [], []
    now, last, n = 0.0, 0.0, 0
    values_at = {}
    for event, work in main:
        order.append(event)
        now += work
        if event[0] == "vs":
            values_at[event[1]] = now
        if work < 2.0:
            continue
        if ends:
            order.append(ends.pop(0))
        if n < H * NS and n // NS in values_at and now - values_at[n // NS] > VALUES_TO_STEP \
                and now - last >= STEP_EVERY:
            order.append(("prep", n))
            if n:
                order.append(("step", n - 1))
            n += 1
            last = now
            now += 1.0
            if n % NS == 1 and n > 1:
                ends += [(what, n // NS - 1) for what in ("rsT", "sqr", "ss")]
        elif n == H * NS and now - last >= STEP_EVERY:
            order.append(("step", n - 1))
            ends += [(what, H - 1) for what in ("rsT", "sqr", "ss")]
            n += 1
    assert n > H * NS and not ends
    order += [("proj", ("ga", 1), j) for j in range(4)]
    for name in ("wa", "gb", "wb"):
        for g in range(2):
            order += [("proj", (name, g), j) for j in range(4)]
    at = {e: i for i, e in enumerate(order)}
    assert len(at) == len(order)
    assert at["ss", H - 2] < at["proj", ("ga", 0), 0]
    for h in range(H - 2):
        assert at["ss", h] < at["proj", ("g", h + 2), 0] and at["rsT", h] < at["qs", h + 2]
    return order


def bank_plan(order):
    count, plan = [0] * 8, {}

    def use(name, bank):
        count[bank] += 1
        plan[name] = (bank, count[bank])

    use("par", TURN_BANK)
    for k in range(KD):
        use(("xT", k), k)
    n = 0
    for event in order:
        what, *which = event
        if what in ("proj", "v"):
            use(event, n % PROJ_BANKS)
            n += 1
        elif what == "step" and which[0] % NS == 0:
            use(("rs", which[0] // NS), RS_BANK)
        elif what in ("rsT", "kt"):
            use(event, TURN_BANK)
        elif what in ("sc", "ss"):
            use(event, SUM_BANK)
        elif what in ("out", "st"):
            use((what, which[0], 0), 6)
            use((what, which[0], 1), 7)
        elif what == "ct":
            use(event, TURN_BANK)
    use(("wo", 2, 0), 4)
    for t in range(2):
        for c in range(2):
            use(("wo", t, c), 2 * t + c)
    use(("hT", 2, 0), 0)
    for n, (t, g) in enumerate([(0, 0), (0, 1), (1, 0), (1, 1)]):
        use(("hT", t, g), 5 + n % 3)
    use("logits", 1)
    use("rank", 2)
    use("count", 3)
    for i, h in enumerate(DEFERRED):
        use(("st", h, 0), (0, 1)[i])
        use(("st", h, 1), (4, 5)[i])
    return plan, count


def build(nc, a, o):
    order = mixer_order()
    plan, uses = bank_plan(order)
    ctx = ExitStack()
    with ctx:
        def sb(name, shape, dt=F32):
            return ctx.enter_context(nc.sbuf_tensor(name, shape, dt))

        def sem(name):
            return ctx.enter_context(nc.semaphore(name))

        ring = sb("ring", [128, RING, CH])
        hx = sb("hx", [128, TT, D])
        cst = sb("cst", [128, N_CONST])
        par = sb("par", [128, KD, N_PAR])
        ones = sb("ones", [128, 128])
        stat = sb("stat", [128, 16])
        router = sb("router", [128, KD, E])
        router_b = sb("router_b", [128, E])
        rg = sb("rg", [128, 2, TT, E])
        rgc = sb("rgc", [128, 2, TT, 2])
        rounds_i = sb("rounds_i", [128, 1], I32)
        arena = sb("arena", [128, 21700])

        def view(at, *dims):
            n = int(np.prod(dims))
            assert at + n <= 21700
            v = arena[:, at:at + n]
            if len(dims) == 2:
                v = v.rearrange("p (a b) -> p a b", a=dims[0])
            if len(dims) == 3:
                v = v.rearrange("p (a b c) -> p a b c", a=dims[0], b=dims[1])
            return v

        squares_out = view(8704, TT, D)
        xnT = view(0, KD, T)
        xsT = view(2112, KD, 32)
        rT = view(2368, H * NV, T)
        xn = view(2368, TT, D)
        prow = view(15100, 1024)
        sg = view(6592, 2, 4, T)
        qT = view(8704, 4, T)
        kT = view(9760, 4, T)
        rot = view(10816, 4, T)
        v_sb = view(11872, 2, DV)
        vs_sb = view(12896, 128)
        ktok = view(13024, 2, DK)
        sc = view(13536, 384)
        st = view(14000, 2, DV)
        sq = view(15100, NV, T)
        rinv = view(16160, T)
        qsm = view(16424, 2, 2, NS * 32)
        ks = view(17448, 2, 2 * NS)
        S = [view(17480 + 1024 * n, 2, DV) for n in range(3)]
        vb = [view(20552 + 512 * n, DV) for n in range(2)]
        cc = view(8704, 4, T)
        U = view(9760, 4, T + 2)
        cv = view(10824, 4, T)
        aT = view(11880, KD, T)
        ctok = view(14000, D)
        merged = view(6592, KD, T)
        gas = merged
        gbs = view(8704, KD, T)
        xn2 = view(0, TT, D)
        hT = view(3072, KD, T)
        ws = view(5184, D)
        route = view(5184, 20, E)
        squares2 = [view(9240, D), view(9240 + 3 * D // 2, D), view(18172, D)]
        xp = view(9240, 3 * 2 * D // 2).bitcast(BF16).rearrange("p (t n d) -> p t n d", n=3, t=2)
        v_kept = [view(12824, 2, DV), view(17148, 2, DV)]
        k_kept = [view(13848, 2, DK), view(14360, 2, DK)]
        st_kept = [view(3072, 2, DV), view(4096, 2, DV)]
        xps = view(12312, D // 2).bitcast(BF16)
        P = view(8336, TT * 2 * SLOTS // 2).bitcast(BF16).rearrange("p (t s) -> p t s", s=SLOTS)
        Pg = view(8528, TT * 2, SLOTS)
        pick = view(8912, SLOTS).bitcast(BF16).rearrange("p (e s) -> p e s", e=2)
        xgT = view(0, KD, 128)
        gcl = view(1024, 2, 512)
        ucl = view(2048, 2, 512)
        sig = view(3072, 2, 512)
        acts = view(4096, 2, 512)
        squares3 = view(1024, TT, D)
        actT = view(5120, 2, 512)
        ysb = view(6144, D)
        pgT = view(7168, T)
        n2b = view(15100, D)
        nfb = view(16124, D)
        b2 = view(17148, D)
        b1 = view(18172, 2 * D)
        bp = view(20220, D).bitcast(BF16)
        bp2 = view(19708, D // 2).bitcast(BF16)
        bias_rest = view(10816, 2 * D)
        bias_part = view(12864, D).bitcast(BF16)
        y_last = view(18172, D)
        tri_b = sb("tri_b", [128, 128], BF16)
        ones_b = sb("ones_b", [128, 128], BF16)
        sel_b = sb("sel_b", [128, TT, E], BF16)
        rs_t = sb("rs_t", [128, 128])
        sample_part = view(18172, 3 * D // 2).bitcast(BF16).rearrange("p (n d) -> p n d", n=3)

        psum = [ctx.enter_context(nc.psum_tensor(f"bank{n}", [128, 512], F32)) for n in range(8)]

        cos, sin = cst[:, C_COS:C_COS + T], cst[:, C_SIN:C_SIN + T]
        cosk, sink = cst[:, C_COSK:C_COSK + T], cst[:, C_SINK:C_SINK + T]
        ident = cst[:, C_ID:C_ID + 128]
        tri = cst[:, C_TRI:C_TRI + 128]
        slot_no = cst[:, C_SLOT:C_SLOT + SLOTS]

        def mask(h, n):
            return cst[:, C_MASK + h * LP:C_MASK + h * LP + n]

        v_kept_dram = nc.dram_tensor("v_kept", (len(DEFERRED), 128, 2, DV), F32, kind="Internal").ap()
        k_kept_dram = nc.dram_tensor("k_kept", (len(DEFERRED), 128, 2, DK), F32, kind="Internal").ap()
        v_dram = nc.dram_tensor("v_decode", (H, NS, DV), F32, kind="Internal").ap()

        chunk = [sem(f"chunk{n}") for n in range(RING)]
        chunk_used = sem("chunk_used")
        filled = [sem(f"filled{n}") for n in range(8)]
        emptied = [sem(f"emptied{n}") for n in range(8)]
        x_in = [sem(f"x_in{t}") for t in range(TT)]
        cst_in = [sem(f"cst_in{n}") for n in range(3)]
        prow_in, router_in, router_ready, row0_out = sem("prow_in"), sem("router_in"), sem("router_ready"), sem("row0_out")
        const_set = sem("const_set")
        sumsq, mean1, root1, xn_ready = sem("sumsq"), sem("mean1"), sem("root1"), sem("xn_ready")
        xsT_ready = sem("xsT_ready")
        dve = sem("dve")
        qk_ready = sem("qk_ready")
        vs_out = [sem("vs_out0"), sem("vs_out1")]
        gate_sig, st_out = sem("gate_sig"), sem("st_out")
        qs_ready = sem("qs_ready")
        S_in = [sem(f"S_in{n}") for n in range(3)]
        S_out = [sem(f"S_out{n}") for n in range(3)]
        vb_in = [sem(f"vb_in{n}") for n in range(2)]
        S_scaled, S_new, S_read = sem("S_scaled"), sem("S_new"), sem("S_read")
        sq_ready, sq_half, sq_sum = sem("sq_ready"), sem("sq_half"), sem("sq_sum")
        rT_ready, ctok_out, merged_ready = sem("rT_ready"), sem("ctok_out"), sem("merged_ready")
        saved, kept_in, kept_read = sem("saved"), sem("kept_in"), sem("kept_read")
        prepared = sem("prepared")
        late_in = sem("late_in")
        sumsq2, mean2, root2 = sem("sumsq2"), sem("mean2"), sem("root2")
        part_ready, rest_ready, parts_zero = sem("part_ready"), sem("rest_ready"), sem("parts_zero")
        h_decode, xps_ready = sem("h_decode"), sem("xps_ready")
        xn2_ready, below_max, gate_exp = sem("xn2_ready"), sem("below_max"), sem("gate_exp")
        selected, routed, rounds_ready = sem("selected"), sem("routed"), sem("rounds_ready")
        cols_ready, pick_ready, P_ready = sem("cols_ready"), sem("pick_ready"), sem("P_ready")
        gathered, xg_lo, xg_hi = sem("gathered"), sem("xg_lo"), sem("xg_hi")
        pg_turned, pgT_ready = sem("pg_turned"), sem("pgT_ready")
        up_done, g_clip, u_clip, sig_ready, ug_ready, act_ready = (sem("up_done"), sem("g_clip"), sem("u_clip"),
                                                                   sem("sig_ready"), sem("ug_ready"), sem("act_ready"))
        act_turned, actT_ready, down_done = sem("act_turned"), sem("actT_ready"), sem("down_done")
        y_ready, y_hi_ready = sem("y_ready"), sem("y_hi_ready")
        combined, added, round_done = sem("combined"), sem("added"), sem("round_done")
        inv3, gained, y_last_ready = sem("inv3"), sem("gained"), sem("y_last_ready")
        sumsq3, mean3, root3, y_scaled, y_out = sem("sumsq3"), sem("mean3"), sem("root3"), sem("y_scaled"), sem("y_out")

        block = ctx.enter_context(nc.Block())

        def fill(pe, name):
            bank, n = plan[name]
            if n > 1:
                pe.wait_ge(emptied[bank], n - 1)
            return psum[bank]

        def fills(ins, name):
            ins.then_inc(filled[plan[name][0]], 1)

        def read(eng, name):
            bank, n = plan[name]
            eng.wait_ge(filled[bank], n)
            return psum[bank]

        def empties(ins, name):
            ins.then_inc(emptied[plan[name][0]], 1)

        def was_read(eng, name):
            bank, n = plan[name]
            eng.wait_ge(emptied[bank], n)

        def was_filled(eng, name):
            bank, n = plan[name]
            eng.wait_ge(filled[bank], n)

        w_in = a["w_in"][0]

        def cols(w, c):
            return [w[512 * n:512 * (n + 1), c:c + 512].rearrange("(k p) n -> p k n", p=128) for n in range(2)]

        def mixer_chunks():
            def group(w, c, last):
                return [(x, last) for x in cols(w, c)]

            def tiles(name, w, c):
                return group(w, c, ("proj", name, 3))

            for g in range(2):
                yield from tiles(("q", g), w_in, W_Q + 512 * g)
                yield from tiles(("k", g), w_in, W_K + 512 * g)
                for h in (2 * g, 2 * g + 1):
                    yield from group(w_in, W_V + DV * h, ("v", h, 1))
                    yield from tiles(("g", h), w_in, W_G + DV * h)
            w_conv = dict(cc=W_CC, ch=W_CH, cb=W_CB)
            for n, g in CONV_ORDER:
                yield from tiles((n, g), w_in, w_conv[n] + 512 * g)
            yield from tiles(("ga", 0), w_in, W_GA)
            yield from tiles(("cb", 1), w_in, W_CB + 512)
            yield from tiles(("ga", 1), w_in, W_GA + 512)
            for n, w, c in (("wa", a["w_a"][0], 0), ("gb", w_in, W_GB)):
                for g in range(2):
                    yield from tiles((n, g), w, c + 512 * g)
            for g in range(2):
                for half in range(2):
                    yield from tiles(("wb", g), a["w_b"][0][D * half:D * (half + 1), :], 512 * g)
            for g in range(2):
                yield from group(a["w_o"][0], 512 * g, ("wo", 1, g))

        w1_rows = a["w_e1"].rearrange("l e (k p) n -> (l e) k p n", p=128)
        w2_rows = a["w_e2"].rearrange("l e (k two p) n -> (l e) k p two n", p=128, two=2)

        @block.sync
        def _(sp):
            sp.dma_start(hx[0:NS, 2, :], a["x_sample"][:, 0, :]).then_inc(x_in[2], 16)
            for t in range(2):
                sp.dma_start(hx[:, t, :], a["x_prompt"][0, 128 * t:128 * (t + 1), :]).then_inc(x_in[t], 16)

            def load_tables(n):
                c = slice(TABLE_PARTS[n], TABLE_PARTS[n + 1])
                sp.dma_start(cst[:, c], a["tables"][:, c]).then_inc(cst_in[n], 16)

            load_tables(0)
            sp.dma_start(prow[R_STATE:R_STATE + 2 * NS, :], a["state_conv"][0].rearrange("b w d -> (b w) d")).then_inc(prow_in, 16)
            sp.dma_start(prow[R_CONV:R_CONV + 3, :], a["conv_w"][0]).then_inc(prow_in, 16)
            sp.dma_start(prow[R_NORM:R_NORM + 1, :], a["norm1"]).then_inc(prow_in, 16)
            sp.dma_start(prow[R_NORM2:R_NORM2 + 1, :], a["norm2"]).then_inc(prow_in, 16)
            mixer = list(mixer_chunks())
            assert len(mixer) == MIXER_CHUNKS

            def slot_free(n):
                was_filled(sp, mixer[n][1])

            for n, (src, _) in enumerate(mixer):
                if n >= RING:
                    slot_free(n - RING)
                sp.dma_start(ring[:, n % RING, :].rearrange("p (k n) -> p k n", k=4), src).then_inc(chunk[n % RING], 16)
                if n in (1, 3):
                    load_tables(1 + n // 2)

            def pair_order():
                return [(True, e, k) for e in range(2) for k in range(8)] + [(False, e, k) for e in range(2) for k in range(4)]

            def used(it, n):
                w1, e, k = pair_order()[n]
                if k == (7 if w1 else 3):
                    sp.wait_ge(up_done if w1 else down_done, 2 * it + (e + 1 + (PRIMED if w1 else 0)))
                else:
                    before = 7 * e + k if w1 else 14 + 3 * e + k
                    sp.wait_ge(chunk_used, COUNTED * it + (before + 1))

            def load_pair(it, pair, first=False):
                for n, (w1, e, k) in enumerate(pair_order()):
                    dst = ring[:, n % RING, :]
                    if w1:
                        src = w1_rows[bass.ds(2 * pair + e, 1), k].rearrange("e p n -> p (e n)")
                    else:
                        src = w2_rows[bass.ds(2 * pair + e, 1), k].rearrange("e p two n -> p (e two) n")
                        dst = dst.rearrange("p (two n) -> p two n", two=2)
                    if n >= RING:
                        used(it, n - RING)
                    elif first:
                        slot_free(MIXER_CHUNKS - RING + n)
                    else:
                        used(it - 1, n + RING)
                    sp.dma_start(dst, src).then_inc(chunk[n % RING], 16)

            load_pair(0, 0, first=True)
            with sp.Fori(1, PAIRS) as pair:
                load_pair(pair, pair)
            sp.wait_ge(rounds_ready, 1)
            rounds = sp.value_load(rounds_i[0:1, 0:1], min_val=1, max_val=MAX_ROUNDS)
            with sp.If(rounds > 1):
                with sp.Fori(1, rounds) as r:
                    with sp.Fori(0, PAIRS) as pair:
                        load_pair(r * PAIRS + pair, pair)
            for t in range(2):
                sp.wait_ge(y_scaled, t + 1)
                sp.dma_start(o["y_prompt"][0, 128 * t:128 * (t + 1), :], hx[:, t, :]).then_inc(y_out, 16)
                if t == 0:
                    sp.wait_ge(y_last_ready, 1)
                    sp.dma_start(o["y_sample"][:, 0, :], y_last[0:NS, :]).then_inc(y_out, 16)
            sp.wait_ge(y_out, 16 * TT)

        @block.gpsimd
        def _(pool):
            pool.memset(stat[:, :], 1.0).then_inc(const_set, 1)
            pool.memset(ones[:, :], 1.0).then_inc(const_set, 1)
            pool.memset(rg[:, :, :, :], 0.0).then_inc(const_set, 1)
            pool.memset(qsm[:, :, :, :], 0.0).then_inc(const_set, 1)
            pool.memset(xsT[:, :, :], 0.0).then_inc(const_set, 1)
            pool.memset(ones_b[:, :], 1.0).then_inc(const_set, 1)
            src = a["state_ret"][0]
            total = H * NS

            def load(n):
                h, b = divmod(n, NS)
                if n >= 3:
                    pool.wait_ge(S_out[n % 3], 16 * (n // 3))
                    was_h, was_b = divmod(n - 3, NS)
                    if was_b == NS - 1:
                        was_filled(pool, ("rs", was_h))
                    else:
                        pool.wait_ge(S_read, (NS - 1) * was_h + was_b + 1)
                pool.dma_start(S[n % 3], src[b, h].rearrange("(k p) v -> p k v", p=128)).then_inc(S_in[n % 3], 16)

            def load_v(n):
                h, b = divmod(n, NS)
                if b == 0:
                    pool.wait_ge(vs_out[h % 2], 64 * (h // 2 + 1))
                if n >= 2:
                    pool.wait_ge(S_new, n - 1)
                pool.dma_start(vb[n % 2], v_dram[h, b:b + 1, :].to_broadcast([128, DV])).then_inc(vb_in[n % 2], 16)

            pool.wait_ge(xn_ready, TT)
            pool.dma_start(router[:, :, :], a["w_router"][0].rearrange("(k p) e -> p k e", p=128)).then_inc(router_in, 16)
            pool.dma_start(router_b[:, :], a["b_router"].to_broadcast([128, E])).then_inc(router_in, 16)
            pool.dma_start(o["conv_sample"][0, :, 0, :], a["state_conv"][0, :, 1, :]).then_inc(row0_out, 16)
            for n in range(3):
                load(n)
            for n in range(2):
                load_v(n)
            for n in range(total):
                h, b = divmod(n, NS)
                pool.wait_ge(S_new, n + 1)
                pool.dma_start(o["ret_sample"][0, b, h].rearrange("(k p) v -> p k v", p=128), S[n % 3])\
                    .then_inc(S_out[n % 3], 16)
                if n + 2 < total:
                    load_v(n + 2)
                if n + 3 < total:
                    load(n + 3)
            for n in range(3):
                pool.wait_ge(S_out[n], 16 * len(range(n, total, 3)))
            pool.wait_ge(rT_ready, H)
            was_filled(pool, ("ss", H - 1))
            pool.dma_start(b1[0:E, :], a["b_e1"][0]).then_inc(late_in, 16)
            pool.dma_start(b2[0:E, :], a["b_e2"][0]).then_inc(late_in, 16)
            pool.dma_start(n2b[:, :], a["norm2"][0:1, :].to_broadcast([128, D])).then_inc(late_in, 16)
            pool.dma_start(nfb[:, :], a["norm_f"].rearrange("(o n) -> o n", o=1).to_broadcast([128, D])).then_inc(late_in, 16)

            pool.wait_ge(prepared, 1)
            pool.wait_ge(saved, 32 * len(DEFERRED))
            for i in range(len(DEFERRED)):
                pool.dma_start(v_kept[i], v_kept_dram[i]).then_inc(kept_in, 16)
                pool.dma_start(k_kept[i], k_kept_dram[i]).then_inc(kept_in, 16)

            pool.wait_ge(merged_ready, KD)
            pool.memset(xps[:, :], 0.0).then_inc(parts_zero, 1)
            for i, (part, t, lo, hi) in enumerate(SPLITS):
                n = ROWS[t]
                pool.wait_ge(part_ready, i + 1)
                is_part = xp[:, t, part, lo:hi] if t < 2 else sample_part[0:n, part, :]
                if part == 0:
                    src, dst = xn2[0:n, t, lo:hi], xn2[0:n, t, lo:hi]
                else:
                    src, dst = xn2[0:n, t, lo:hi], xp[:, t, 2, lo:hi] if t < 2 else sample_part[0:n, 2, :]
                    pool.wait_ge(rest_ready, SPLITS.index((0, t, lo, hi)) + 1)
                pool.tensor_tensor(dst, src, is_part, ALU.subtract).then_inc(rest_ready, 1)

            pool.wait_ge(rounds_ready, 1)
            rounds = pool.value_load(rounds_i[0:1, 0:1], min_val=1, max_val=MAX_ROUNDS)
            pool.wait_ge(routed, 2)
            with pool.Fori(0, rounds) as r:
                with pool.Fori(0, PAIRS) as pair:
                    it = r * PAIRS + pair
                    e = 2 * pair
                    pool.wait_ge(P_ready, 2 * it + PRIMED)
                    pool.tensor_copy(rgc[:, :, :, :], rg[:, :, :, bass.ds(e, 2)]).then_inc(cols_ready, 1)
                    pool.wait_ge(y_ready, 2 * it + PRIMED)
                    pool.tensor_copy(pick[:, :, :],
                                     cst[:, bass.ds(e + C_PICK, 2)].rearrange("p (e o) -> p e o", o=1)
                                     .to_broadcast([128, 2, SLOTS])).then_inc(pick_ready, 1)
                pool.wait_ge(cols_ready, PAIRS * (r + 1))
                pool.tensor_tensor(rg[:, 0, :, :], rg[:, 0, :, :],
                                   cst[:, C_THR + 1:C_THR + 2].rearrange("p (a o) -> p a o", a=1).to_broadcast([128, TT, E]),
                                   ALU.subtract).then_inc(round_done, 1)
                pool.wait_ge(round_done, r + 1)
            pool.wait_ge(added, 6 * PAIRS * rounds + ADDED)
            pool.tensor_tensor(y_last[0:NS, :], hx[0:NS, 2, :], nfb[0:NS, :], ALU.mult).then_inc(gained, 1)

        @block.scalar
        def _(ac):
            for primed in (actT_ready, y_hi_ready):
                ac.sem_inc(primed, PRIMED)
            ac.wait_ge(const_set, 1)
            ac.activation(stat[:, 13:14], stat[:, 12:13], ACT.Sqrt)
            for t in TILE_ORDER:
                n = ROWS[t]
                ac.wait_ge(x_in[t], 16)
                ac.activation(squares_out[0:n, t, :], hx[0:n, t, :], ACT.Square, accum_out=stat[0:n, t:t + 1]).then_inc(sumsq, 1)
                ac.wait_ge(mean1, TILE_ORDER.index(t) + 1)
                ac.activation(stat[:, 6 + t:7 + t], stat[:, 3 + t:4 + t], ACT.Sqrt).then_inc(root1, 1)

            ac.wait_ge(emptied[4], plan["par"][1])
            for k in range(1, KD, 2):
                name = ("xT", k)
                ins = ac.activation(xnT[:, k, :], read(ac, name)[:, 0:T], ACT.Copy, scale=par[:, k, R_NORM:R_NORM + 1])
                empties(ins, name)

            for event in order:
                what, *which = event
                if what == "prep":
                    n = which[0]
                    ac.wait_ge(S_in[n % 3], 16 * (n // 3 + 1))
                    ac.activation(S[n % 3], S[n % 3], ACT.Copy, scale=gamma(n // NS)).then_inc(S_scaled, 1)
                    continue
                h = which[0]
                if what == "v":
                    t = which[1]
                    bank = read(ac, event)
                    if t < 2:
                        if t == 0 and h >= 1:
                            if h - 1 in DEFERRED:
                                was_filled(ac, ("out", h - 1, 1))
                                ac.wait_ge(saved, 32 * (DEFERRED.index(h - 1) + 1))
                            else:
                                was_filled(ac, ("st", h - 1, 1))
                        empties(ac.activation(v_sb[:, t, :], bank[:, :], ACT.Copy), event)
                    else:
                        if h >= 1:
                            ac.wait_ge(vs_out[(h - 1) % 2], 64 * ((h - 1) // 2 + 1))
                        empties(ac.activation(vs_sb[:, :], bank[:, 0:128], ACT.Copy), event)
                elif what == "vs":
                    was_read(ac, ("v", h, 2))
                    for j in range(NV):
                        ac.dma_start(v_dram[h, :, 128 * j:128 * (j + 1)], vs_sb[32 * j:32 * j + NS, :]).then_inc(vs_out[h % 2], 16)
                elif what == "kt":
                    bank = read(ac, event)
                    for t in range(2):
                        ins = ac.activation(ktok[:, t, :], bank[:, DK * t:DK * (t + 1)], ACT.Copy,
                                            scale=cst[:, C_KDEC + 2 * h + t:C_KDEC + 2 * h + t + 1])
                    empties(ins, event)
                elif what == "out":
                    for g in range(2):
                        use = ("out", h, g)
                        bank = read(ac, use)
                        empties(ac.activation(rT[:, NV * h + 2 * g:NV * h + 2 * g + 2, 0:LP],
                                              bank[:, :].rearrange("p (a q) -> p a q", a=2), ACT.Copy), use)
                elif what == "save":
                    for t in range(2):
                        was_read(ac, ("v", h, t))
                    was_read(ac, ("kt", h))
                    i = DEFERRED.index(h)
                    ac.dma_start(v_kept_dram[i], v_sb[:, :, :]).then_inc(saved, 16)
                    ac.dma_start(k_kept_dram[i], ktok[:, :, :]).then_inc(saved, 16)
                elif what == "st":
                    for g in range(2):
                        use = ("st", h, g)
                        bank = read(ac, use)
                        if g == 0 and h >= 1:
                            ac.wait_ge(st_out, 16 * h)
                        empties(ac.activation(st[:, g, :], bank[:, :], ACT.Copy), use)
                    for g in range(2):
                        was_read(ac, ("st", h, g))
                    ac.dma_start(o["ret_prompt"][0, 0, h].rearrange("(k p) v -> p k v", p=128), st[:, :, :]).then_inc(st_out, 16)
                elif what == "sqr":
                    was_read(ac, ("rsT", h))
                    for g in range(2):
                        was_read(ac, ("out", h, g))
                    if h >= 1:
                        was_filled(ac, ("ss", h - 1))
                    ac.activation(sq[:, :, :], rT[:, NV * h:NV * (h + 1), :], ACT.Square).then_inc(sq_ready, 1)
                elif what == "ss":
                    bank = read(ac, event)
                    if h >= 1:
                        ac.wait_ge(rT_ready, h)
                    empties(ac.activation(rinv[:, :], bank[:, 0:T], ACT.Sqrt, scale=1.0 / DV, bias=stat[:, 15:16]), event)
                elif what == "ct":
                    bank = read(ac, event)
                    if h == 0:
                        ac.wait_ge(st_out, 16 * (H - len(DEFERRED)))
                    empties(ac.activation(ctok[0:NS + 2, 512 * h:512 * (h + 1)], bank[0:NS + 2, :], ACT.Copy), event)
                    if h == 1:
                        for g in range(2):
                            was_read(ac, ("ct", g))
                        ac.dma_start(o["conv_prompt"][0, 0], ctok[0:2, :]).then_inc(ctok_out, 16)
                        ac.dma_start(o["conv_sample"][0, :, 1, :], ctok[2:2 + NS, :]).then_inc(ctok_out, 16)
                elif what == "proj":
                    (name, g), j = which
                    if name == "g":
                        bank = read(ac, event)
                        if j == 0 and g >= 2:
                            ac.wait_ge(rT_ready, g - 1)
                        ac.activation(sg[:, g % 2, j, :], bank[:, 0:T], ACT.Sigmoid).then_inc(gate_sig, 1)
                    elif name == "cc":
                        bank = read(ac, event)
                        if g == 1:
                            was_read(ac, ("proj", ("ch", 0), j))
                        empties(ac.activation(cc[:, j, :], bank[:, 0:T], ACT.Copy), event)
                    elif name in ("ga", "gb"):
                        bank = read(ac, event)
                        if name == "ga" and j == 0:
                            ac.wait_ge(rT_ready, H - 1 + g)
                        if (name, g, j) == ("gb", 0, 0):
                            was_filled(ac, ("proj", ("wa", 1), 3))
                        dst = (gas if name == "ga" else gbs)[:, 4 * g + j, :]
                        empties(ac.activation(dst, bank[:, 0:T], ACT.Sigmoid), event)
            def norm2(t):
                n = ROWS[t]
                ac.activation(squares2[t][0:n, :], hx[0:n, t, :], ACT.Square, accum_out=stat[0:n, t:t + 1]).then_inc(sumsq2, 1)
                ac.wait_ge(mean2, TILE_ORDER.index(t) + 1)
                ac.activation(stat[:, 6 + t:7 + t], stat[:, 3 + t:4 + t], ACT.Sqrt).then_inc(root2, 1)

            def split(part, t, lo=0, hi=D):
                n = ROWS[t]
                if part == 0:
                    ac.wait_ge(xn2_ready, TILE_ORDER.index(t) + 1 + (1 if lo else 0))
                else:
                    ac.wait_ge(rest_ready, SPLITS.index((0, t, lo, hi)) + 1)
                dst = xp[:, t, part, lo:hi] if t < 2 else sample_part[0:n, part, :]
                ac.activation(dst, xn2[0:n, t, lo:hi], ACT.Copy).then_inc(part_ready, 1)

            use = ("wo", 2, 0)
            bank = read(ac, use)
            for j in range(4):
                ins = ac.activation(ws[0:NS, 256 * j:256 * (j + 1)], bank[32 * j:32 * j + NS, 0:256], ACT.Copy)
            empties(ins, use)
            ac.wait_ge(h_decode, 1)
            norm2(2)
            for c in range(2):
                was_read(ac, ("wo", 0, c))
            norm2(0)
            ac.wait_ge(parts_zero, 1)
            split(0, 2)
            split(0, 0)
            bank = read(ac, ("hT", 0, 1))
            empties(ac.activation(hT[:, 4:8, 0:128], bank[:, :].rearrange("p (k q) -> p k q", k=4), ACT.Copy), ("hT", 0, 1))
            split(1, 2)
            split(1, 0)
            ac.wait_ge(rest_ready, SPLITS.index((1, 2, 0, D)) + 1)
            ac.wait_ge(part_ready, SPLITS.index((1, 2, 0, D)) + 1)
            for part in range(3):
                ac.activation(xps[32 * part:32 * part + NS, :], sample_part[0:NS, part, :], ACT.Copy).then_inc(xps_ready, 1)
            for c in range(2):
                was_read(ac, ("wo", 1, c))
            norm2(1)
            split(0, 1, 0, D // 2)
            split(0, 1, D // 2, D)
            ac.wait_ge(below_max, 1)
            ac.activation(route[:, 3:6, :], route[:, 3:6, :], ACT.Exp).then_inc(gate_exp, 1)
            split(1, 1, 0, D // 2)
            split(1, 1, D // 2, D)

            for i, h in enumerate(DEFERRED):
                for g in range(2):
                    ac.activation(st_kept[i][:, g, :], read(ac, ("st", h, g))[:, :], ACT.Copy).then_inc(kept_read, 1)
                ac.wait_ge(kept_read, 2 * (i + 1))
                ac.dma_start(o["ret_prompt"][0, 0, h].rearrange("(k p) v -> p k v", p=128), st_kept[i]).then_inc(st_out, 16)

            ac.wait_ge(rounds_ready, 1)
            rounds = ac.value_load(rounds_i[0:1, 0:1], min_val=1, max_val=MAX_ROUNDS)
            with ac.Fori(0, rounds) as r:
                with ac.Fori(0, PAIRS) as pair:
                    it = r * PAIRS + pair
                    ac.wait_ge(gathered, 2 * it + 1)
                    ac.activation(xgT[:, 0:4, :], psum[6][:, :].rearrange("p (k s) -> p k s", k=4), ACT.Copy).then_inc(xg_lo, 1)
                    ac.wait_ge(pg_turned, it + (1 + PRIMED))
                    ac.activation(pgT[:, :], psum[5][:, 0:T], ACT.Copy).then_inc(pgT_ready, 1)
                    for e in range(2):
                        ac.wait_ge(g_clip, 2 * it + e + 1)
                        ac.wait_ge(st_out, 16 * H)
                        ac.activation(sig[:, e, :], gcl[:, e, :], ACT.Sigmoid, scale=ALPHA).then_inc(sig_ready, 1)
                    for e in range(2):
                        ac.wait_ge(act_turned, 2 * it + e + 1)
                        ac.activation(actT[:, e, :], psum[5][:, :], ACT.Copy).then_inc(actT_ready, 1)
                        ac.wait_ge(down_done, 2 * it + e + 1)
                        ac.activation(ysb[SLOTS * e:SLOTS * (e + 1), 512:1024], psum[4][64:128, :], ACT.Copy).then_inc(y_hi_ready, 1)
            ac.activation(stat[:, 13:14], stat[:, 12:13], ACT.Sqrt)
            for t, n in enumerate(ROWS):
                ac.wait_ge(added, 6 * PAIRS * rounds + (2 * t - 4 + ADDED))
                ac.activation(squares3[0:n, t, :], hx[0:n, t, :], ACT.Square,
                              accum_out=stat[0:n, t:t + 1]).then_inc(sumsq3, 1)
            ac.wait_ge(mean3, 1)
            ac.activation(stat[:, 6:9], stat[:, 3:6], ACT.Sqrt).then_inc(root3, 1)
            ac.wait_ge(inv3, 1)
            ac.wait_ge(gained, 1)
            ac.activation(y_last[0:NS, :], y_last[0:NS, :], ACT.Copy, scale=stat[0:NS, 11:12]).then_inc(y_last_ready, 1)
            ac.wait_ge(row0_out, 16)
            ac.wait_ge(st_out, 16 * H)

        @block.vector
        def _(v):
            steps = [0]
            for primed in (P_ready, y_ready):
                v.sem_inc(primed, PRIMED)
            v.sem_inc(added, ADDED)

            def own(ins):
                steps[0] += 1
                ins.then_inc(dve, 1)

            def settle():
                v.wait_ge(dve, steps[0])

            def prepare_experts():
                v.wait_ge(router_in, 32)
                v.tensor_tensor(router[:, :, :], router[:, :, :], par[:, :, R_NORM2:R_NORM2 + 1].to_broadcast([128, KD, E]),
                                ALU.mult).then_inc(router_ready, 1)
                v.wait_ge(late_in, 64)
                was_filled(v, ("proj", ("wa", 1), 3))
                v.wait_ge(ctok_out, 32)
                for bias, parts, n in ((b1, bp, 2 * D), (b2, bp2, D)):
                    own(v.memset(parts[3 * E:128, :], 0.0))
                    src = bias[0:E, :]
                    for part in range(3):
                        own(v.tensor_copy(bias_part[0:E, 0:n], src))
                        settle()
                        if part < 2:
                            own(v.tensor_tensor(bias_rest[0:E, 0:n], src, bias_part[0:E, 0:n], ALU.subtract))
                        own(v.tensor_copy(parts[E * part:E * (part + 1), :], bias_part[0:E, 0:n]))
                        settle()
                        src = bias_rest[0:E, 0:n]
                v.sem_inc(prepared, 1)

            def mean_to(src, dst, out_sem):
                v.tensor_scalar(dst, src, 1.0 / D, EPS, ALU.mult, ALU.add).then_inc(out_sem, 1)

            v.wait_ge(const_set, 6)
            own(v.memset(stat[:, 15:16], EPS))
            for t in TILE_ORDER:
                n = ROWS[t]
                if t == TILE_ORDER[-1]:
                    empties(v.tensor_copy(par[:, :, :], read(v, "par")[:, 0:KD * N_PAR].rearrange("p (k n) -> p k n", k=KD)), "par")
                v.wait_ge(sumsq, TILE_ORDER.index(t) + 1)
                mean_to(stat[:, t:t + 1], stat[:, 3 + t:4 + t], mean1)
                v.wait_ge(root1, TILE_ORDER.index(t) + 1)
                own(v.reciprocal(stat[:, 9 + t:10 + t], stat[:, 6 + t:7 + t]))
                settle()
                v.tensor_scalar(xn[0:n, t, :], hx[0:n, t, :], stat[0:n, 9 + t:10 + t], None, ALU.mult).then_inc(xn_ready, 1)
            v.wait_ge(emptied[4], plan["par"][1])
            for k in range(0, KD, 2):
                name = ("xT", k)
                ins = v.tensor_scalar(xnT[:, k, :], read(v, name)[:, 0:T], par[:, k, R_NORM:R_NORM + 1], None, ALU.mult)
                empties(ins, name)
            for k in range(KD):
                was_read(v, ("xT", k))
            v.tensor_copy(xsT[:, :, 0:NS], xnT[:, :, LP:T]).then_inc(xsT_ready, 1)
            v.wait_ge(cst_in[0], 16)
            own(v.tensor_copy(tri_b[:, :], tri))
            v.wait_ge(cst_in[1], 16)

            def rotate(event):
                _, (name, g), j = event
                dst, cs, sn = (qT, cos, sin) if name == "q" else (kT, cosk, sink)
                lo, hi = ("proj", (name, g), j - 1), event
                x1, x2 = read(v, lo)[:, 0:T], read(v, hi)[:, 0:T]
                own(v.tensor_tensor(rot[:, 0, :], x1, cs, ALU.mult))
                own(v.tensor_tensor(rot[:, 1, :], x2, sn, ALU.mult))
                empties(v.tensor_tensor(rot[:, 2, :], x1, sn, ALU.mult), lo)
                empties(v.tensor_tensor(rot[:, 3, :], x2, cs, ALU.mult), hi)
                settle()
                was_read(v, lo)
                was_read(v, hi)
                v.tensor_tensor(dst[:, j - 1, :], rot[:, 0, :], rot[:, 1, :], ALU.subtract).then_inc(qk_ready, 1)
                v.tensor_tensor(dst[:, j, :], rot[:, 2, :], rot[:, 3, :], ALU.add).then_inc(qk_ready, 1)
                qk[0] += 2
                v.wait_ge(qk_ready, qk[0])

            qk = [0]

            for event in order:
                what, *which = event
                if what == "prep":
                    n = which[0]
                    h, b = divmod(n, NS)
                    v.wait_ge(S_scaled, n + 1)
                    v.wait_ge(vb_in[n % 2], 16 * (n // 2 + 1))
                    own(v.scalar_tensor_tensor(S[n % 3][:, 0, :], vb[n % 2], ks[:, h % 2, b:b + 1],
                                               S[n % 3][:, 0, :], ALU.mult, ALU.add))
                    v.scalar_tensor_tensor(S[n % 3][:, 1, :], vb[n % 2], ks[:, h % 2, NS + b:NS + b + 1],
                                           S[n % 3][:, 1, :], ALU.mult, ALU.add).then_inc(S_new, 1)
                elif what == "step" and which[0] % NS == NS - 1:
                    h = which[0] // NS
                    empties(v.tensor_copy(rs_t[:, :], read(v, ("rs", h))[:, 0:128]), ("rs", h))
                elif what == "rsT":
                    h = which[0]
                    bank = read(v, event)
                    empties(v.tensor_copy(rT[:, NV * h:NV * (h + 1), LP:T],
                                          bank[:, 0:128].rearrange("p (j s) -> p j s", j=NV)[:, :, 0:NS]), event)
                elif what == "sqr":
                    h = which[0]
                    v.wait_ge(sq_ready, h + 1)
                    v.tensor_tensor(sq[:, 0:2, :], sq[:, 0:2, :], sq[:, 2:4, :], ALU.add).then_inc(sq_half, 1)
                    v.wait_ge(sq_half, h + 1)
                    v.tensor_tensor(sq[:, 0, :], sq[:, 0, :], sq[:, 1, :], ALU.add).then_inc(sq_sum, 1)
                elif what == "ss":
                    h = which[0]
                    was_read(v, event)
                    own(v.reciprocal(rinv[:, :], rinv[:, :]))
                    settle()
                    for j in range(NV):
                        own(v.tensor_tensor(sg[:, h % 2, j, :], sg[:, h % 2, j, :], rinv[:, :], ALU.mult))
                    settle()
                    for j in range(NV):
                        ins = v.tensor_tensor(rT[:, NV * h + j, :], rT[:, NV * h + j, :], sg[:, h % 2, j, :], ALU.mult)
                    ins.then_inc(rT_ready, 1)
                elif what == "qs":
                    h = which[0]
                    if h >= 2:
                        was_filled(v, ("rs", h - 2))
                    for half in range(2):
                        own(v.tensor_copy(qsm[:, h % 2, half, 0:33 * (NS - 1) + 1:33], qT[:, 2 * (h % 2) + half, LP:T]))
                        v.tensor_copy(ks[:, h % 2, NS * half:NS * (half + 1)], kT[:, 2 * (h % 2) + half, LP:T])\
                            .then_inc(qs_ready, 1)
                    v.wait_ge(qs_ready, 2 * (h + 1))
                    settle()
                elif what == "sc":
                    h = which[0]
                    bank = read(v, event)
                    if h == 0:
                        v.wait_ge(cst_in[2], 16)
                    own(v.tensor_tensor(sc[:, 0:LP], bank[:, 0:LP], mask(h, LP), ALU.mult))
                    empties(v.tensor_tensor(sc[:, LP:384], bank[:, LP:384], mask(h, 128), ALU.mult), event)
                elif what == "taps":
                    g = which[0]
                    v.wait_ge(saved, 32 * len(DEFERRED))

                    def tap(j, i):
                        return par[:, 4 * g + j, R_CONV + i:R_CONV + i + 1]

                    for j in range(4):
                        was_read(v, ("proj", ("ch", g), j))
                    settle()
                    old = par[:, 4 * g:4 * g + 4, R_STATE:R_STATE + 2 * NS].rearrange("p k (b w) -> p k w b", w=2)
                    for j in range(4):
                        own(v.tensor_scalar(cv[:, j, 0:LP], U[:, j, 0:LP], tap(j, 0), None, ALU.mult))
                        own(v.tensor_scalar(cv[:, j, LP:T], old[:, j, 0, :], tap(j, 0), None, ALU.mult))
                    settle()
                    for j in range(4):
                        own(v.scalar_tensor_tensor(cv[:, j, 0:LP], U[:, j, 1:LP + 1], tap(j, 1), cv[:, j, 0:LP], ALU.mult, ALU.add))
                        own(v.scalar_tensor_tensor(cv[:, j, LP:T], old[:, j, 1, :], tap(j, 1), cv[:, j, LP:T], ALU.mult, ALU.add))
                    settle()
                    for j in range(4):
                        own(v.scalar_tensor_tensor(cv[:, j, :], U[:, j, 2:T + 2], tap(j, 2), cv[:, j, :], ALU.mult, ALU.add))
                    settle()
                elif what == "proj":
                    (name, g), j = which
                    if name in ("q", "k"):
                        if (name, g, j) == ("q", 1, 0):
                            was_filled(v, ("sc", 1))
                            was_filled(v, ("kt", 1))
                        if j % 2 == 1:
                            rotate(event)
                    elif name == "g":
                        v.wait_ge(gate_sig, 4 * g + j + 1)
                        bank = psum[plan[event][0]]
                        empties(v.tensor_tensor(sg[:, g % 2, j, :], sg[:, g % 2, j, :], bank[:, 0:T], ALU.mult), event)
                        if j == 3:
                            for i in range(4):
                                was_read(v, ("proj", (name, g), i))
                    elif name == "ch":
                        bank = read(v, event)
                        was_read(v, ("proj", ("cc", g), j))
                        if (g, j) == (0, 0):
                            was_filled(v, ("out", H - 1, 1))
                            own(v.memset(U[:, :, 0:2], 0.0))
                        if (g, j) == (1, 0):
                            was_filled(v, ("ct", 0))
                        empties(v.tensor_tensor(U[:, j, 2:T + 2], bank[:, 0:T], cc[:, j, :], ALU.mult), event)
                    elif name == "cb":
                        bank = read(v, event)
                        empties(v.tensor_tensor(aT[:, 4 * g + j, :], bank[:, 0:T], cv[:, j, :], ALU.mult), event)
                    elif name == "wa":
                        bank = read(v, event)
                        was_read(v, ("proj", ("ga", g), j))
                        empties(v.tensor_tensor(merged[:, 4 * g + j, :], gas[:, 4 * g + j, :], bank[:, 0:T], ALU.mult), event)
                        if (g, j) == (1, 3):
                            prepare_experts()
                    elif name == "wb":
                        bank = read(v, event)
                        was_read(v, ("proj", ("gb", g), j))
                        empties(v.tensor_tensor(gbs[:, 4 * g + j, :], gbs[:, 4 * g + j, :], bank[:, 0:T], ALU.mult), event)
                        was_read(v, event)
                        was_read(v, ("proj", ("wa", g), j))
                        v.tensor_tensor(merged[:, 4 * g + j, :], merged[:, 4 * g + j, :], gbs[:, 4 * g + j, :], ALU.add)\
                            .then_inc(merged_ready, 1)
            def turned(t, g):
                n = ROWS[t]
                use = ("hT", t, g)
                k = 4 if t < 2 else KD
                empties(v.tensor_copy(hT[:, 4 * g:4 * g + k, 128 * t:128 * t + n],
                                      read(v, use)[:, 0:k * n].rearrange("p (k q) -> p k q", k=k)), use)

            for t in TILE_ORDER:
                n = ROWS[t]
                if t < 2:
                    for c in range(2):
                        bank = read(v, ("wo", t, c))
                        empties(v.tensor_tensor(hx[0:n, t, 512 * c:512 * (c + 1)], hx[0:n, t, 512 * c:512 * (c + 1)],
                                                bank[0:n, :], ALU.add), ("wo", t, c))
                        if (t, c) == (1, 0):
                            turned(2, 0)
                            turned(0, 0)
                            turned(1, 0)
                else:
                    was_read(v, ("wo", 2, 0))
                    v.tensor_tensor(hx[0:n, t, :], hx[0:n, t, :], ws[0:n, :], ALU.add).then_inc(h_decode, 1)
                    v.wait_ge(h_decode, 1)
                    v.wait_ge(late_in, 64)
                    own(v.memset(route[:, :, :], 0.0))
                if t == 1:
                    turned(1, 1)
                v.wait_ge(sumsq2, TILE_ORDER.index(t) + 1)
                mean_to(stat[:, t:t + 1], stat[:, 3 + t:4 + t], mean2)
                v.wait_ge(root2, TILE_ORDER.index(t) + 1)
                own(v.reciprocal(stat[:, 9 + t:10 + t], stat[:, 6 + t:7 + t]))
                settle()
                for lo, hi in ((0, D // 2), (D // 2, D)) if t == 1 else ((0, D),):
                    v.scalar_tensor_tensor(xn2[0:n, t, lo:hi], hx[0:n, t, lo:hi], stat[0:n, 9 + t:10 + t], n2b[0:n, lo:hi],
                                           ALU.mult, ALU.mult).then_inc(xn2_ready, 1)
            L, ex, gt, eq, ceq = (route[:, 3 * i:3 * i + 3, :] for i in range(5))
            top8 = route[:, 18, 0:8 * TT].rearrange("p (t i) -> p t i", t=TT)
            count, total, inv = (route[:, 19, 3 * i:3 * i + 3].rearrange("p (t o) -> p t o", o=1) for i in range(3))
            fullest, n_rounds, below = route[:, 19, 12:13], route[:, 19, 13:14], route[:, 19, 16:16 + MAX_ROUNDS]

            def wide(x):
                return x.to_broadcast([128, TT, E])

            bank = read(v, "logits")
            for t, n in enumerate(ROWS):
                ins = v.scalar_tensor_tensor(L[0:n, t, :], bank[0:n, E * t:E * (t + 1)], stat[0:n, 9 + t:10 + t],
                                             router_b[0:n, :], ALU.mult, ALU.add)
                if t == 2:
                    empties(ins, "logits")
                else:
                    own(ins)
            was_read(v, "logits")
            settle()
            for t in range(TT):
                own(v.max(top8[:, t, :], L[:, t, :]))
            settle()
            own(v.tensor_tensor(gt, L, wide(top8[:, :, TOP - 1:TOP]), ALU.is_gt))
            own(v.tensor_tensor(eq, L, wide(top8[:, :, TOP - 1:TOP]), ALU.is_equal))
            settle()
            own(v.reduce_sum(count, gt, AX.X))
            v.tensor_tensor(ex, L, wide(top8[:, :, 0:1]), ALU.subtract).then_inc(below_max, 1)
            settle()
            for t in range(TT):
                own(v.tensor_tensor_scan(ceq[:, t, :], ones[:, 0:E], eq[:, t, :], count[:, t, :], ALU.mult, ALU.add))
            settle()
            own(v.scalar_tensor_tensor(ceq, ceq, float(TOP), eq, ALU.is_le, ALU.mult))
            settle()
            v.tensor_tensor(sel_b[:, :, :], gt, ceq, ALU.add).then_inc(selected, 1)
            v.wait_ge(selected, 1)
            v.wait_ge(gate_exp, 1)
            own(v.tensor_tensor(ex, ex, sel_b[:, :, :], ALU.mult))
            settle()
            own(v.reduce_sum(total, ex, AX.X))
            bank = read(v, "count")
            empties(v.reduce_max(fullest, bank[:, 0:E], AX.X), "count")
            was_read(v, "count")
            settle()
            own(v.tensor_scalar(below, cst[:, C_THR:C_THR + MAX_ROUNDS], fullest, None, ALU.is_lt))
            own(v.reciprocal(inv, total))
            settle()
            own(v.reduce_sum(n_rounds, below, AX.X))
            own(v.tensor_tensor(rg[:, 1, 0:2, :], ex[:, 0:2, :], inv[:, 0:2, :].to_broadcast([128, 2, E]), ALU.mult))
            settle()
            v.tensor_copy(rounds_i[:, :], n_rounds).then_inc(rounds_ready, 1)
            own(v.tensor_scalar(rg[0:NS, 1, 2, :], ex[0:NS, 2, :], inv[0:NS, 2, :], None, ALU.mult))
            bank = read(v, "rank")
            own(v.scalar_tensor_tensor(rg[:, 0, 0:2, :], bank[:, 0:2 * E].rearrange("p (t e) -> p t e", e=E), RANKED,
                                       sel_b[:, 0:2, :], ALU.add, ALU.mult))
            empties(v.scalar_tensor_tensor(rg[0:NS, 0, 2, :], bank[0:NS, 2 * E:3 * E], RANKED, sel_b[0:NS, 2, :],
                                           ALU.add, ALU.mult), "rank")
            was_read(v, "rank")
            settle()
            v.tensor_copy(rg[32:32 + NS, 0, 2, :], rg[0:NS, 0, 2, :]).then_inc(routed, 1)
            v.tensor_copy(rg[64:64 + NS, 0, 2, :], rg[0:NS, 0, 2, :]).then_inc(routed, 1)

            v.wait_ge(rounds_ready, 1)
            rounds = v.value_load(rounds_i[0:1, 0:1], min_val=1, max_val=MAX_ROUNDS)
            slots = slot_no.rearrange("p (o s) -> p o s", o=1).to_broadcast([128, 2 * TT, SLOTS])

            def per_slot(n):
                return rgc[:, n, :, :].rearrange("p t (e o) -> p (t e) o", o=1).to_broadcast([128, 2 * TT, SLOTS])

            with v.Fori(0, rounds) as r:
                with v.Fori(0, PAIRS) as pair:
                    it = r * PAIRS + pair
                    v.wait_ge(cols_ready, it + 1)
                    v.wait_ge(pg_turned, it + PRIMED)
                    v.tensor_tensor(P, slots, per_slot(0), ALU.is_equal).then_inc(P_ready, 1)
                    v.wait_ge(P_ready, 2 * it + (1 + PRIMED))
                    v.tensor_tensor(Pg, P, per_slot(1), ALU.mult).then_inc(P_ready, 1)
                    v.wait_ge(gathered, 2 * it + 2)
                    v.tensor_copy(xgT[:, 4:8, :], psum[7][:, :].rearrange("p (k s) -> p k s", k=4)).then_inc(xg_hi, 1)
                    for e in range(2):
                        v.wait_ge(up_done, 2 * it + (e + 1 + PRIMED))
                        v.tensor_scalar(gcl[:, e, :], psum[2 * e][:, :], LIMIT, None, ALU.min).then_inc(g_clip, 1)
                        v.tensor_scalar(ucl[:, e, :], psum[2 * e + 1][:, :], LIMIT, -LIMIT, ALU.min, ALU.max).then_inc(u_clip, 1)
                        v.wait_ge(g_clip, 2 * it + e + 1)
                        v.wait_ge(u_clip, 2 * it + e + 1)
                        v.scalar_tensor_tensor(ucl[:, e, :], ucl[:, e, :], 1.0, gcl[:, e, :], ALU.add, ALU.mult)\
                            .then_inc(ug_ready, 1)
                        v.wait_ge(ug_ready, 2 * it + e + 1)
                        v.wait_ge(sig_ready, 2 * it + e + 1)
                        v.tensor_tensor(acts[:, e, :], ucl[:, e, :], sig[:, e, :], ALU.mult).then_inc(act_ready, 1)
                    for e in range(2):
                        v.wait_ge(down_done, 2 * it + e + 1)
                        v.tensor_copy(ysb[SLOTS * e:SLOTS * (e + 1), 0:512], psum[4][0:64, :]).then_inc(y_ready, 1)
                    for t, n in enumerate(ROWS):
                        for c in range(2):
                            v.wait_ge(combined, 6 * it + 2 * t + c + 1)
                            v.tensor_tensor(hx[0:n, t, 512 * c:512 * (c + 1)], hx[0:n, t, 512 * c:512 * (c + 1)],
                                            psum[6 + c][0:n, :], ALU.add).then_inc(added, 1)
                    v.wait_ge(added, 6 * it + (6 + ADDED))
            v.wait_ge(sumsq3, TT)
            mean_to(stat[:, 0:3], stat[:, 3:6], mean3)
            v.wait_ge(root3, 1)
            v.reciprocal(stat[:, 9:12], stat[:, 6:9]).then_inc(inv3, 1)
            v.wait_ge(inv3, 1)
            for t in range(2):
                v.scalar_tensor_tensor(hx[:, t, :], hx[:, t, :], stat[:, 9 + t:10 + t], nfb[:, :],
                                       ALU.mult, ALU.mult).then_inc(y_scaled, 1)

        @block.tensor
        def _(pe):
            at = [0]
            for primed in (pg_turned, up_done):
                pe.sem_inc(primed, PRIMED)

            def chunk_ready(n):
                pe.wait_ge(chunk[n % RING], 16 * (n // RING + 1))

            def weight(n, k):
                return ring[:, n % RING, 512 * k:512 * (k + 1)]

            first = {}

            def chunks_of(name, groups=1):
                if name not in first:
                    first[name] = at[0]
                    at[0] += 2 * groups
                return first[name]

            def project(event):
                _, name, j = event
                rhs, groups = {"wa": (aT, 1), "wb": (rT, 2)}.get(name[0], (xnT, 1))
                n = chunks_of(name, groups)
                bank = fill(pe, event)
                for k in range(KD * groups):
                    if j == 0 and k % 4 == 0:
                        chunk_ready(n + k // 4)
                    if event == order[0]:
                        was_read(pe, ("xT", k))
                    ins = pe.matmul(bank[:, 0:T], weight(n + k // 4, k % 4)[:, 128 * j:128 * (j + 1)], rhs[:, k, :],
                                    start=k == 0, stop=k == KD * groups - 1)
                fills(ins, event)

            pe.wait_ge(cst_in[0], 16)
            pe.wait_ge(prow_in, 64)
            bank = fill(pe, "par")
            for k in range(KD):
                ins = pe.transpose(bank[:, N_PAR * k:N_PAR * (k + 1)], prow[0:N_PAR, 128 * k:128 * (k + 1)],
                                   ident[0:N_PAR, 0:N_PAR])
            fills(ins, "par")
            for t in TILE_ORDER:
                pe.wait_ge(xn_ready, TILE_ORDER.index(t) + 1)
                n = ROWS[t]
                for k in [k for k in range(KD) if k != TURN_BANK] + [TURN_BANK] if t == TILE_ORDER[0] else range(KD):
                    name = ("xT", k)
                    bank = fill(pe, name) if t == TILE_ORDER[0] else psum[plan[name][0]]
                    ins = pe.transpose(bank[:, 128 * t:128 * t + n], xn[0:n, t, 128 * k:128 * (k + 1)], ident[0:n, 0:n])
                    if t == TILE_ORDER[-1]:
                        fills(ins, name)
            for event in order:
                what, *which = event
                if what == "proj":
                    name, j = which
                    if (name, j) == (("wa", 0), 0):
                        for i in range(1, 4):
                            was_read(pe, ("proj", ("cb", 1), i))
                    if (name, j) == (("wb", 0), 0):
                        pe.wait_ge(rT_ready, H)
                    project(event)
                elif what == "v":
                    h, t = which
                    n = chunks_of(("v", h))
                    bank = fill(pe, event)
                    if (h, t) == (0, 2):
                        pe.wait_ge(xsT_ready, 1)
                    for k in range(KD):
                        if t == 2 and k % 4 == 0:
                            chunk_ready(n + k // 4)
                        w = weight(n + k // 4, k % 4)
                        if t < 2:
                            ins = pe.matmul(bank[:, :], xnT[:, k, 128 * t:128 * (t + 1)], w, start=k == 0, stop=k == KD - 1)
                        else:
                            for j in range(4):
                                ins = pe.matmul(bank[32 * j:32 * (j + 1), 0:128], xsT[:, k, :], w[:, 128 * j:128 * (j + 1)],
                                                start=k == 0, stop=k == KD - 1)
                    fills(ins, event)
                elif what == "kt":
                    h = which[0]
                    hh = 2 * (h % 2)
                    pe.wait_ge(qk_ready, 8 * (h // 2 + 1))
                    bank = fill(pe, event)
                    for t in range(2):
                        for half in range(2):
                            ins = pe.transpose(bank[:, DK * t + 128 * half:DK * t + 128 * (half + 1)],
                                               kT[:, hh + half, 128 * t:128 * (t + 1)], ident)
                    fills(ins, event)
                elif what == "sc":
                    hh = 2 * (which[0] % 2)
                    bank = fill(pe, event)
                    for half in range(2):
                        pe.matmul(bank[:, 0:LP], kT[:, hh + half, 0:128], qT[:, hh + half, 0:LP], start=half == 0, stop=half == 1)
                    for half in range(2):
                        ins = pe.matmul(bank[:, LP:384], kT[:, hh + half, 128:256], qT[:, hh + half, 128:256],
                                        start=half == 0, stop=half == 1)
                    fills(ins, event)
                elif what == "out":
                    h = which[0]
                    was_read(pe, ("sc", h))
                    for t in range(2):
                        was_read(pe, ("v", h, t))
                    for g in range(2):
                        bank = fill(pe, ("out", h, g))
                        for j in range(2):
                            dv = 128 * (2 * g + j)
                            pe.matmul(bank[:, LP * j:LP * (j + 1)], v_sb[:, 0, dv:dv + 128], sc[:, 0:LP], start=True, stop=False)
                            ins = pe.matmul(bank[:, LP * j + 128:LP * (j + 1)], v_sb[:, 1, dv:dv + 128], sc[:, LP:384],
                                            start=False, stop=True)
                        fills(ins, ("out", h, g))
                elif what == "st":
                    h = which[0]
                    was_read(pe, ("kt", h))
                    for g in range(2):
                        bank = fill(pe, ("st", h, g))
                        for t in range(2):
                            ins = pe.matmul(bank[:, :], ktok[:, t, 128 * g:128 * (g + 1)], v_sb[:, t, :], start=t == 0, stop=t == 1)
                        fills(ins, ("st", h, g))
                elif what == "step":
                    n = which[0]
                    h, b = divmod(n, NS)
                    use = ("rs", h)
                    bank = fill(pe, use) if b == 0 else psum[RS_BANK]
                    pe.wait_ge(S_new, n + 1)
                    for half in range(2):
                        for j in range(NV):
                            ins = pe.matmul(bank[32 * j:32 * (j + 1), 0:128], qsm[:, h % 2, half, 32 * b:32 * (b + 1)],
                                            S[n % 3][:, half, 128 * j:128 * (j + 1)],
                                            start=b == 0 and half == 0, stop=b == NS - 1 and half == 1)
                    if b < NS - 1:
                        ins.then_inc(S_read, 1)
                    else:
                        fills(ins, use)
                elif what == "rsT":
                    h = which[0]
                    bank = fill(pe, event)
                    was_read(pe, ("rs", h))
                    fills(pe.transpose(bank[:, 0:128], rs_t[:, :], ident), event)
                elif what == "ss":
                    h = which[0]
                    bank = fill(pe, event)
                    pe.wait_ge(sq_sum, h + 1)
                    fills(pe.matmul(bank[:, 0:T], ones[:, :], sq[:, 0, :], start=True, stop=True), event)
                elif what == "ct":
                    g = which[0]
                    bank = fill(pe, event)
                    for j in range(4):
                        was_read(pe, ("proj", ("ch", g), j))
                    for j in range(4):
                        ins = pe.transpose(bank[0:NS + 2, 128 * j:128 * (j + 1)], U[:, j, LP:T + 2], ident)
                    fills(ins, event)
            n = chunks_of("wo", 2)
            for i in range(4):
                chunk_ready(n + i)
            assert at[0] == MIXER_CHUNKS

            def out_product(t, c, ks=range(KD)):
                bank = fill(pe, ("wo", t, c)) if ks[0] == 0 else psum[plan["wo", t, c][0]]
                for k in ks:
                    ins = pe.matmul(bank[:, :], merged[:, k, 128 * t:128 * (t + 1)], weight(n + 2 * c + k // 4, k % 4),
                                    start=k == 0, stop=k == KD - 1)
                if ks[-1] == KD - 1:
                    fills(ins, ("wo", t, c))

            def turn(t, g):
                rows = ROWS[t]
                if t == 2:
                    pe.wait_ge(h_decode, 1)
                else:
                    was_read(pe, ("wo", t, g))
                bank = fill(pe, ("hT", t, g))
                for i in range(4 if t < 2 else KD):
                    k = 4 * g + i
                    ins = pe.transpose(bank[:, rows * i:rows * (i + 1)], hx[0:rows, t, 128 * k:128 * (k + 1)],
                                       ident[0:rows, 0:rows])
                fills(ins, ("hT", t, g))

            def route_logits(t, ks=range(KD)):
                rows = ROWS[t]
                for g in range(2 if t < 2 else 1):
                    if 4 * g in ks:
                        was_read(pe, ("hT", t, g))
                for k in ks:
                    ins = pe.matmul(psum[plan["logits"][0]][0:rows, E * t:E * (t + 1)], hT[:, k, 128 * t:128 * t + rows],
                                    router[:, k, :], start=k == 0, stop=k == KD - 1)
                return ins

            def final_states(first, last):
                pe.wait_ge(kept_in, 32 * len(DEFERRED))
                for step in range(first, last):
                    i, g, t = step // 4, step // 2 % 2, step % 2
                    use = ("st", DEFERRED[i], g)
                    bank = fill(pe, use) if t == 0 else psum[plan[use][0]]
                    ins = pe.matmul(bank[:, :], k_kept[i][:, t, 128 * g:128 * (g + 1)], v_kept[i][:, t, :],
                                    start=t == 0, stop=t == 1)
                    if t == 1:
                        fills(ins, use)

            bank = fill(pe, ("wo", 2, 0))
            for k in range(KD):
                pe.wait_ge(merged_ready, k + 1)
                for j in range(4):
                    w = weight(n + 2 * (j // 2) + k // 4, k % 4)[:, 256 * (j % 2):256 * (j % 2 + 1)]
                    ins = pe.matmul(bank[32 * j:32 * j + NS, 0:256], merged[:, k, LP:T], w, start=k == 0, stop=k == KD - 1)
            fills(ins, ("wo", 2, 0))
            out_product(0, 0)
            out_product(0, 1)
            out_product(1, 0)
            for t, g in ((2, 0), (0, 0), (0, 1), (1, 0)):
                turn(t, g)
            out_product(1, 1, range(0, 4))
            fill(pe, "logits")
            pe.wait_ge(router_ready, 1)
            route_logits(2)
            route_logits(0)
            route_logits(1, range(0, 4))
            out_product(1, 1, range(4, 8))
            final_states(0, 1)
            turn(1, 1)
            final_states(1, 2)
            fills(route_logits(1, range(4, 8)), "logits")
            final_states(2, 5)
            pe.wait_ge(selected, 1)
            bank = fill(pe, "count")
            for s in range(TT):
                ins = pe.matmul(bank[:, 0:E], ones_b[0:ROWS[s], :], sel_b[0:ROWS[s], s, :], start=s == 0, stop=s == TT - 1)
            fills(ins, "count")
            bank = fill(pe, "rank")
            for t, rows in enumerate(ROWS):
                for s in range(t + 1):
                    ins = pe.matmul(bank[0:rows, E * t:E * (t + 1)], (tri_b if s == t else ones_b)[0:ROWS[s], 0:rows],
                                    sel_b[0:ROWS[s], s, :], start=s == 0, stop=s == t)
            fills(ins, "rank")
            final_states(5, 8)
            for b in (2, 3, 6, 7):
                pe.wait_ge(emptied[b], uses[b])

            rounds_at = rounds_i[0:1, 0:1]
            pe.wait_ge(rounds_ready, 1)
            rounds = pe.value_load(rounds_at, min_val=1, max_val=MAX_ROUNDS)
            uses_before = MIXER_CHUNKS // RING
            pe.wait_ge(xps_ready, 3)
            pe.wait_ge(rest_ready, len(SPLITS))
            with pe.Fori(0, rounds) as r:
                with pe.Fori(0, PAIRS) as pair:
                    it = r * PAIRS + pair

                    def slot_ready(n):
                        pe.wait_ge(chunk[n % RING], 32 * it + 16 * (uses_before + n // RING + 1))

                    pe.wait_ge(P_ready, 2 * it + (1 + PRIMED))
                    pe.wait_ge(added, 6 * it + ADDED)
                    for half in range(2):
                        for k in range(4 * half, 4 * half + 4):
                            out = psum[6 + half][:, 128 * (k % 4):128 * (k % 4 + 1)]
                            for t in range(2):
                                for part in range(3):
                                    pe.matmul(out, xp[:, t, part, 128 * k:128 * (k + 1)], P[:, 2 * t:2 * t + 2, :],
                                              start=t == 0 and part == 0, stop=False)
                            ins = pe.matmul(out, xps[:, 128 * k:128 * (k + 1)], P[:, 4:6, :], start=False, stop=True)
                        ins.then_inc(gathered, 1)
                    pe.wait_ge(pick_ready, it + 1)
                    pe.wait_ge(kept_read, 2 * len(DEFERRED))
                    for e in range(2):
                        for k in range(-1, KD):
                            if e == 0 and k in (0, 4):
                                pe.wait_ge(xg_hi if k else xg_lo, it + 1)
                            if k >= 0:
                                slot_ready(KD * e + k)
                            for q in range(2):
                                for half in range(2):
                                    out = psum[2 * e + q][64 * half:64 * (half + 1), :]
                                    c = D * q + 512 * half
                                    if k < 0:
                                        pe.matmul(out, pick[:, e, :], bp[:, c:c + 512], start=True, stop=False)
                                    else:
                                        ins = pe.matmul(out, xgT[:, k, 64 * e:64 * (e + 1)],
                                                        ring[:, (KD * e + k) % RING, c:c + 512], start=False, stop=k == KD - 1)
                            if k >= 0:
                                ins.then_inc(up_done if k == KD - 1 else chunk_used, 1)
                        if e == 0:
                            pe.wait_ge(P_ready, 2 * it + (2 + PRIMED))
                            pe.wait_ge(actT_ready, 2 * it + PRIMED)
                            for t, n in enumerate(ROWS):
                                ins = pe.transpose(psum[5][:, 128 * t:128 * t + n],
                                                   Pg[0:n, 2 * t:2 * t + 2, :].rearrange("p e s -> p (e s)"), ident[0:n, 0:n])
                            ins.then_inc(pg_turned, 1)
                    for e in range(2):
                        pe.wait_ge(act_ready, 2 * it + e + 1)
                        if e == 0:
                            pe.wait_ge(pgT_ready, it + 1)
                        else:
                            pe.wait_ge(actT_ready, 2 * it + (e + PRIMED))
                        for k in range(4):
                            ins = pe.transpose(psum[5][:, 128 * k:128 * (k + 1)], acts[:, e, 128 * k:128 * (k + 1)], ident)
                        ins.then_inc(act_turned, 1)
                        pe.wait_ge(actT_ready, 2 * it + (e + 1 + PRIMED))
                        pe.wait_ge(y_ready, 2 * it + (e + PRIMED))
                        pe.wait_ge(y_hi_ready, 2 * it + (e + PRIMED))
                        for half in range(2):
                            pe.matmul(psum[4][64 * half:64 * (half + 1), :], pick[:, e, :], bp2[:, 512 * half:512 * (half + 1)],
                                      start=True, stop=False)
                        for f in range(KD):
                            n = 2 * KD + 4 * e + f // 2
                            if f % 2 == 0:
                                slot_ready(n)
                            lhs = actT[:, e, 128 * (f % 4) + 64 * (f // 4):128 * (f % 4) + 64 * (f // 4) + 64]
                            for half in range(2):
                                c = D * (f % 2) + 512 * half
                                ins = pe.matmul(psum[4][64 * half:64 * (half + 1), :], lhs, ring[:, n % RING, c:c + 512],
                                                start=False, stop=f == KD - 1)
                            if f % 2 == 1:
                                ins.then_inc(down_done if f == KD - 1 else chunk_used, 1)
                    pe.wait_ge(y_ready, 2 * it + (2 + PRIMED))
                    pe.wait_ge(y_hi_ready, 2 * it + (2 + PRIMED))
                    for t, n in enumerate(ROWS):
                        for c in range(2):
                            if t:
                                pe.wait_ge(added, 6 * it + (2 * t + c - 1 + ADDED))
                            pe.matmul(psum[6 + c][0:n, :], pgT[:, 128 * t:128 * t + n], ysb[:, 512 * c:512 * (c + 1)],
                                      start=True, stop=True).then_inc(combined, 1)


INPUTS = ["x_prompt", "x_sample", "state_conv", "state_ret", "norm1", "w_in", "conv_w", "w_a", "w_b", "w_o", "norm2",
          "w_router", "b_router", "w_e1", "b_e1", "w_e2", "b_e2", "norm_f"]
OUTPUTS = [("y_prompt", (1, LP, D)), ("y_sample", (NS, 1, D)), ("conv_prompt", (1, 1, 2, D)),
           ("ret_prompt", (1, 1, H, DK, DV)), ("conv_sample", (1, NS, 2, D)), ("ret_sample", (1, NS, H, DK, DV))]


def kernel(**inputs):
    import concourse.bacc as bacc
    from concourse.bass_utils import run_bass_kernel_spmd

    nc = bacc.Bacc("TRN2", target_bir_lowering=False, num_devices=1)
    arrays = {name: np.ascontiguousarray(inputs[name]) for name in INPUTS}
    arrays["tables"] = shape_constants()
    a = {n: nc.dram_tensor(f"in_{n}", x.shape, F32, kind="ExternalInput").ap() for n, x in arrays.items()}
    o = {n: nc.dram_tensor(f"out_{n}", s, F32, kind="ExternalOutput").ap() for n, s in OUTPUTS}
    build(nc, a, o)
    r = run_bass_kernel_spmd(nc, [{f"in_{n}": x for n, x in arrays.items()}], core_ids=[0])
    return tuple(r.results[0][f"out_{n}"] for n, _ in OUTPUTS)
```
